# Optimizing a Trainium2 kernel written in Bass

```python
import jax, jax.numpy as jnp
from jax import lax
import numpy as np
import math

D_MODEL = 2048
BATCH = 1
SEQ = 256
DEPTH = 1

D_RNN = 2048
N_RNN_BLOCKS = 8
RNN_BLOCK = D_RNN // N_RNN_BLOCKS
CONV_WIDTH = 4
LRU_C = 8.0
N_Q_HEADS = 32
N_KV_HEADS = 4
HEAD_DIM = 64
Q_GROUP = N_Q_HEADS // N_KV_HEADS
WINDOW = 128
ATTN_BLOCK = 128
ROPE_THETA = 10000.0
D_FF = 4 * D_MODEL
RMS_EPS = 1e-6
NEG_INF = -1e30

IN_SPLITS = (D_RNN, D_RNN, N_Q_HEADS * HEAD_DIM, N_KV_HEADS * HEAD_DIM, N_KV_HEADS * HEAD_DIM, D_MODEL, D_MODEL)
IN_OFFSETS = tuple(int(o) for o in np.cumsum(IN_SPLITS)[:-1])
D_IN = int(sum(IN_SPLITS))


def rmsnorm(x, g):
    xf = x.astype(jnp.float32)
    y = xf * lax.rsqrt(jnp.mean(xf * xf, axis=-1, keepdims=True) + RMS_EPS)
    return (y * g.astype(jnp.float32)).astype(x.dtype)

def rope(x, positions):
    half = HEAD_DIM // 2
    inv_freq = ROPE_THETA ** (-jnp.arange(0, HEAD_DIM, 2, dtype=jnp.float32) / HEAD_DIM)
    ang = positions.astype(jnp.float32)[..., None] * inv_freq
    cos = jnp.cos(ang)[:, :, None, :]
    sin = jnp.sin(ang)[:, :, None, :]
    xf = x.astype(jnp.float32)
    x1, x2 = xf[..., :half], xf[..., half:]
    out = jnp.concatenate([x1 * cos - x2 * sin, x2 * cos + x1 * sin], axis=-1)
    return out.astype(x.dtype)

def causal_depthwise_conv(x, w, b):
    S = x.shape[1]
    xp = jnp.pad(x, ((0, 0), (CONV_WIDTH - 1, 0), (0, 0)))
    y = b
    for k in range(CONV_WIDTH):
        y = y + xp[:, k:k + S] * w[k]
    return y

def rg_lru(x, positions, w_a, b_a, w_x, b_x, lam):
    B, S, _ = x.shape
    xf = x.astype(jnp.float32)
    xb = xf.reshape(B, S, N_RNN_BLOCKS, RNN_BLOCK)
    r = jax.nn.sigmoid(jnp.einsum('bsni,nij->bsnj', xb, w_a.astype(jnp.float32)).reshape(B, S, D_RNN) + b_a)
    i = jax.nn.sigmoid(jnp.einsum('bsni,nij->bsnj', xb, w_x.astype(jnp.float32)).reshape(B, S, D_RNN) + b_x)
    log_a = -LRU_C * r * jax.nn.softplus(-lam.astype(jnp.float32))
    a = jnp.exp(log_a)
    mult = jnp.sqrt(-jnp.expm1(2.0 * log_a))
    reset = (positions == 0)[..., None]
    a = jnp.where(reset, 0.0, a)
    mult = jnp.where(reset, 1.0, mult)
    b = mult * (i * xf)

    def combine(left, right):
        a_l, b_l = left
        a_r, b_r = right
        return a_l * a_r, a_r * b_l + b_r

    _, h = lax.associative_scan(combine, (a, b), axis=1)
    return h.astype(x.dtype)

def sliding_window_sink_attention(q, k, v, sinks):
    B, S = q.shape[0], q.shape[1]
    T = ATTN_BLOCK
    NB = S // T
    scale = HEAD_DIM ** -0.5
    qb = q.reshape(B, NB, T, N_KV_HEADS, Q_GROUP, HEAD_DIM) * scale
    kb = k.reshape(B, NB, T, N_KV_HEADS, HEAD_DIM)
    vb = v.reshape(B, NB, T, N_KV_HEADS, HEAD_DIM)
    pad = ((0, 0), (1, 0), (0, 0), (0, 0), (0, 0))
    kk = jnp.concatenate([jnp.pad(kb, pad)[:, :-1], kb], axis=2)
    vv = jnp.concatenate([jnp.pad(vb, pad)[:, :-1], vb], axis=2)
    scores = jnp.einsum('bnqhgd,bnkhd->bnhgqk', qb, kk).astype(jnp.float32)
    qi = jnp.arange(T)[:, None]
    ki = jnp.arange(2 * T)[None, :]
    dist = qi + T - ki
    band = (dist >= 0) & (dist < WINDOW)
    not_pad = (jnp.arange(NB)[:, None, None] > 0) | (ki >= T)[None]
    valid = (band[None] & not_pad)[None, :, None, None]
    scores = jnp.where(valid, scores, NEG_INF)
    sink = sinks.astype(jnp.float32).reshape(N_KV_HEADS, Q_GROUP)[None, None, :, :, None, None]
    m = jnp.maximum(jnp.max(scores, axis=-1, keepdims=True), sink)
    p = jnp.exp(scores - m)
    denom = jnp.sum(p, axis=-1, keepdims=True) + jnp.exp(sink - m)
    probs = (p / denom).astype(v.dtype)
    out = jnp.einsum('bnhgqk,bnkhd->bnqhgd', probs, vv)
    return out.reshape(B, S, N_Q_HEADS * HEAD_DIM)

def first_inputs(seed: int = 0) -> dict:
    key = jax.random.key(seed)
    ks = jax.random.split(key, 20)
    f32 = jnp.float32
    L = DEPTH

    def nrm(k, shape, scale):
        return jax.random.normal(k, shape, f32) * scale

    def gain(k):
        return 1.0 + 0.05 * jax.random.normal(k, (L, D_MODEL), f32)

    x = jax.random.normal(ks[0], (BATCH, SEQ, D_MODEL), f32)
    positions = jnp.broadcast_to(jnp.arange(SEQ, dtype=jnp.int32)[None, :], (BATCH, SEQ))
    u = jax.random.uniform(ks[9], (L, D_RNN), f32, 0.9, 0.999)
    a0 = u ** (1.0 / LRU_C)
    lru_lambda = jnp.log(a0) - jnp.log1p(-a0)
    return {
        "x": x,
        "positions": positions,
        "norm_mix_pre": gain(ks[1]),
        "w_in": nrm(ks[2], (L, D_MODEL, D_IN), D_MODEL ** -0.5),
        "conv_w": nrm(ks[3], (L, CONV_WIDTH, D_RNN), CONV_WIDTH ** -0.5),
        "conv_b": nrm(ks[4], (L, D_RNN), 0.01),
        "w_rg_a": nrm(ks[5], (L, N_RNN_BLOCKS, RNN_BLOCK, RNN_BLOCK), RNN_BLOCK ** -0.5),
        "b_rg_a": nrm(ks[6], (L, D_RNN), 0.01),
        "w_rg_x": nrm(ks[7], (L, N_RNN_BLOCKS, RNN_BLOCK, RNN_BLOCK), RNN_BLOCK ** -0.5),
        "b_rg_x": nrm(ks[8], (L, D_RNN), 0.01),
        "lru_lambda": lru_lambda,
        "attn_sinks": nrm(ks[10], (L, N_Q_HEADS), 0.5),
        "w_rnn_proj": nrm(ks[11], (L, D_RNN, D_MODEL), D_RNN ** -0.5),
        "w_attn_proj": nrm(ks[12], (L, N_Q_HEADS * HEAD_DIM, D_MODEL), (N_Q_HEADS * HEAD_DIM) ** -0.5),
        "w_out": nrm(ks[13], (L, D_MODEL, D_MODEL), D_MODEL ** -0.5),
        "norm_mix_post": gain(ks[14]),
        "norm_mlp_pre": gain(ks[15]),
        "w_mlp_up": nrm(ks[16], (L, D_MODEL, D_FF), D_MODEL ** -0.5),
        "w_mlp_down": nrm(ks[17], (L, D_FF, D_MODEL), D_FF ** -0.5),
        "norm_mlp_post": gain(ks[18]),
    }

def first_block(x, positions, norm_mix_pre, w_in, conv_w, conv_b, w_rg_a, b_rg_a, w_rg_x, b_rg_x, lru_lambda, attn_sinks, w_rnn_proj, w_attn_proj, w_out, norm_mix_post, norm_mlp_pre, w_mlp_up, w_mlp_down, norm_mlp_post):
    B, S, _ = x.shape
    for l in range(DEPTH):
        h = rmsnorm(x, norm_mix_pre[l])
        proj = h @ w_in[l]
        xr, yr, q, k, v, g_rnn, g_attn = jnp.split(proj, IN_OFFSETS, axis=-1)
        xr = causal_depthwise_conv(xr, conv_w[l], conv_b[l])
        xr = rg_lru(xr, positions, w_rg_a[l], b_rg_a[l], w_rg_x[l], b_rg_x[l], lru_lambda[l])
        y_rnn = xr * jax.nn.gelu(yr)
        q = rope(q.reshape(B, S, N_Q_HEADS, HEAD_DIM), positions)
        k = rope(k.reshape(B, S, N_KV_HEADS, HEAD_DIM), positions)
        v = v.reshape(B, S, N_KV_HEADS, HEAD_DIM)
        y_att = sliding_window_sink_attention(q, k, v, attn_sinks[l])
        mix = jax.nn.sigmoid(g_rnn) * (y_rnn @ w_rnn_proj[l]) + jax.nn.sigmoid(g_attn) * (y_att @ w_attn_proj[l])
        x = x + rmsnorm(mix @ w_out[l], norm_mix_post[l])
        h = rmsnorm(x, norm_mlp_pre[l])
        u = jnp.square(jax.nn.relu(h @ w_mlp_up[l]))
        x = x + rmsnorm(u @ w_mlp_down[l], norm_mlp_post[l])
    return x


Q_CHUNK = 128
A_CONFIGS = ((128, 1), (512, 4), (2048, 16))
N_A_GROUPS = len(A_CONFIGS)
A_HEADS_PER_GROUP = 4
A_HEADS = N_A_GROUPS * A_HEADS_PER_GROUP
A_BLOCK = 128
B_HEADS = 8
MOBA_BLOCK = 256
MOBA_TOPK = 3
C_KV_HEADS = 3
C_GROUP = 4
C_HEADS = C_KV_HEADS * C_GROUP
CMP_STRIDE = 16
CMP_LEN = 2 * CMP_STRIDE
CMP_HIDDEN = 128
SLC_BLOCK = 64
SLC_TOPN = 16
WIN = 512
FORCE_SCORE = 1e9
N_HEADS = A_HEADS + B_HEADS + C_HEADS
MIX_WIDTH = N_HEADS * HEAD_DIM
A_WIDTH = 3 * A_HEADS * HEAD_DIM
B_WIDTH = 3 * B_HEADS * HEAD_DIM
C_Q_WIDTH = C_HEADS * HEAD_DIM
C_KV_WIDTH = 6 * C_KV_HEADS * HEAD_DIM
C_GATE_WIDTH = 3 * C_HEADS
IN_WIDTH = A_WIDTH + B_WIDTH + C_Q_WIDTH + C_KV_WIDTH + C_GATE_WIDTH
D_FF_2 = 5632
CONV_WIDTH_2 = 3
N_BUCKETS = 32
T5_MAX_DIST = 2048
EPS = 1e-6
NEG = -1e30
Q_SCALE = HEAD_DIM ** -0.5


def rmsnorm_2(x, g):
    x32 = x.astype(jnp.float32)
    y = x32 * lax.rsqrt(jnp.mean(x32 * x32, axis=-1, keepdims=True) + EPS)
    return (y * g.astype(jnp.float32)).astype(x.dtype)

def t5_bucket(dist):
    n = jnp.maximum(dist, 0)
    max_exact = N_BUCKETS // 2
    nf = jnp.maximum(n, 1).astype(jnp.float32)
    large = max_exact + (jnp.log(nf / max_exact) / math.log(T5_MAX_DIST / max_exact)
                         * (N_BUCKETS - max_exact)).astype(jnp.int32)
    large = jnp.minimum(large, N_BUCKETS - 1)
    return jnp.where(n < max_exact, n, large)

def masked_softmax(s, mask):
    s32 = jnp.where(mask, s.astype(jnp.float32), NEG)
    m = jnp.max(s32, axis=-1, keepdims=True)
    e = jnp.where(mask, jnp.exp(s32 - m), 0.0)
    den = jnp.sum(e, axis=-1, keepdims=True)
    p = e / jnp.maximum(den, 1e-30)
    lse = m[..., 0] + jnp.log(jnp.maximum(den[..., 0], 1e-30))
    return p, lse

def dilated_group(q, k, v, window, dilation, tbl):
    B, S, H, dh = q.shape
    L = S // dilation
    nq = -(-L // A_BLOCK)
    Lp = nq * A_BLOCK
    nback = window // dilation

    def to_class(t):
        t = t.reshape(B, L, dilation, H, dh).transpose(0, 2, 3, 1, 4)
        return jnp.pad(t, ((0, 0), (0, 0), (0, 0), (0, Lp - L), (0, 0)))

    def band(t):
        tp = jnp.pad(t, ((0, 0), (0, 0), (0, 0), (A_BLOCK, 0), (0, 0)))
        prev = tp[:, :, :, :Lp].reshape(B, dilation, H, nq, A_BLOCK, dh)
        cur = t.reshape(B, dilation, H, nq, A_BLOCK, dh)
        return jnp.concatenate([prev, cur], axis=4)

    qb = to_class(q).reshape(B, dilation, H, nq, A_BLOCK, dh)
    kb = band(to_class(k))
    vb = band(to_class(v))
    a = jnp.arange(A_BLOCK)[:, None]
    bk = jnp.arange(2 * A_BLOCK)[None, :]
    rel = a + A_BLOCK - bk
    key_idx = jnp.arange(nq)[:, None, None] * A_BLOCK - A_BLOCK + bk[None]
    mask = (rel >= 0)[None] & (rel <= nback)[None] & (key_idx >= 0)
    bias = tbl[:, t5_bucket(rel * dilation)]
    s = jnp.einsum('bdhnqe,bdhnke->bdhnqk', qb, kb) + bias[:, None]
    p, lse = masked_softmax(s, mask)
    o = jnp.einsum('bdhnqk,bdhnke->bdhnqe', p.astype(v.dtype), vb)
    o = o.reshape(B, dilation, H, Lp, dh)[:, :, :, :L].transpose(0, 3, 1, 2, 4).reshape(B, S, H, dh)
    lse = lse.reshape(B, dilation, H, Lp)[:, :, :, :L].transpose(0, 3, 1, 2).reshape(B, S, H)
    return o, lse

def dilated_mixer(pA, tbl_a):
    B, S = pA.shape[:2]
    outs, lses = [], []
    for g, (w, d) in enumerate(A_CONFIGS):
        o, lse = dilated_group(pA[:, :, g, 0] * Q_SCALE, pA[:, :, g, 1], pA[:, :, g, 2], w, d,
                               tbl_a[g * A_HEADS_PER_GROUP:(g + 1) * A_HEADS_PER_GROUP])
        outs.append(o)
        lses.append(lse)
    alpha = jax.nn.softmax(jnp.stack(lses, axis=2), axis=2)
    o = jnp.stack(outs, axis=2) * alpha[..., None].astype(outs[0].dtype)
    return o.reshape(B, S, A_HEADS * HEAD_DIM)

def moba_mixer(q, k, v, tbl):
    B, S, H, dh = q.shape
    q, k, v = (t.transpose(0, 2, 1, 3) for t in (q, k, v))
    nb = -(-S // MOBA_BLOCK)
    Sp = nb * MOBA_BLOCK
    kp = jnp.pad(k, ((0, 0), (0, 0), (0, Sp - S), (0, 0)))
    vp = jnp.pad(v, ((0, 0), (0, 0), (0, Sp - S), (0, 0)))
    kb = kp.reshape(B, H, nb, MOBA_BLOCK, dh)
    vb = vp.reshape(B, H, nb, MOBA_BLOCK, dh)
    kmean = jnp.mean(kb.astype(jnp.float32), axis=3).astype(k.dtype)
    topk = min(MOBA_TOPK, nb)
    ar_b = jnp.arange(B)[:, None, None, None]
    ar_h = jnp.arange(H)[None, :, None, None]
    blk_off = jnp.arange(MOBA_BLOCK)

    def chunk(c):
        start = c * Q_CHUNK
        t = start + jnp.arange(Q_CHUNK)
        ob = start // MOBA_BLOCK
        qc = lax.dynamic_slice_in_dim(q, start, Q_CHUNK, axis=2)
        gate = jnp.einsum('bhqe,bhne->bhqn', qc, kmean).astype(jnp.float32)
        past = jnp.arange(nb) < ob
        gate = jnp.where(past, gate, NEG)
        _, idx = lax.top_k(gate, topk)
        sel_ok = idx < ob
        ks = kb[ar_b, ar_h, idx].reshape(B, H, Q_CHUNK, topk * MOBA_BLOCK, dh)
        vs = vb[ar_b, ar_h, idx].reshape(B, H, Q_CHUNK, topk * MOBA_BLOCK, dh)
        pos_s = (idx[..., None] * MOBA_BLOCK + blk_off).reshape(B, H, Q_CHUNK, topk * MOBA_BLOCK)
        mask_s = jnp.repeat(sel_ok, MOBA_BLOCK, axis=-1)
        ko = lax.dynamic_slice_in_dim(kp, ob * MOBA_BLOCK, MOBA_BLOCK, axis=2)
        vo = lax.dynamic_slice_in_dim(vp, ob * MOBA_BLOCK, MOBA_BLOCK, axis=2)
        pos_o = ob * MOBA_BLOCK + blk_off
        mask_o = jnp.broadcast_to(pos_o[None, :] <= t[:, None], (B, H, Q_CHUNK, MOBA_BLOCK))
        s_s = (jnp.einsum('bhqe,bhqke->bhqk', qc, ks)
               + tbl[ar_h, t5_bucket(t[None, None, :, None] - pos_s)])
        s_o = (jnp.einsum('bhqe,bhke->bhqk', qc, ko)
               + tbl[:, t5_bucket(t[:, None] - pos_o[None, :])][None])
        p, _ = masked_softmax(jnp.concatenate([s_s, s_o], -1), jnp.concatenate([mask_s, mask_o], -1))
        p = p.astype(v.dtype)
        n_sel = topk * MOBA_BLOCK
        return (jnp.einsum('bhqk,bhqke->bhqe', p[..., :n_sel], vs)
                + jnp.einsum('bhqk,bhke->bhqe', p[..., n_sel:], vo))

    outs = lax.map(chunk, jnp.arange(S // Q_CHUNK))
    return outs.transpose(1, 0, 3, 2, 4).reshape(B, S, H * dh)

def nsa_mixer(q, kvC, gates, cmp_w1, cmp_w2, cmp_pe, tbl):
    B, S, _, dh = q.shape
    KV, G = C_KV_HEADS, C_GROUP
    q = q.reshape(B, S, KV, G, dh).transpose(0, 2, 3, 1, 4)
    k_cmp, v_cmp, k_slc, v_slc, k_win, v_win = (kvC[:, :, i].transpose(0, 2, 1, 3) for i in range(6))
    gates = gates.reshape(B, S, KV, G, 3).transpose(0, 2, 3, 1, 4)
    n_cmp = S // CMP_STRIDE - 1
    n_slc = S // SLC_BLOCK
    n_sel = min(SLC_TOPN, n_slc)

    def compress(t, w1, w2, pe):
        sub = t.reshape(B, KV, S // CMP_STRIDE, CMP_STRIDE, dh)
        blocks = jnp.concatenate([sub[:, :, :-1], sub[:, :, 1:]], axis=3) + pe
        return jax.nn.gelu(blocks.reshape(B, KV, n_cmp, CMP_LEN * dh) @ w1) @ w2

    kc = compress(k_cmp, cmp_w1[0], cmp_w2[0], cmp_pe[0])
    vc = compress(v_cmp, cmp_w1[1], cmp_w2[1], cmp_pe[1])
    cmp_end = jnp.arange(n_cmp) * CMP_STRIDE + CMP_LEN - 1
    ci = jnp.arange(n_cmp)[:, None] * CMP_STRIDE
    sj = jnp.arange(n_slc)[None, :] * SLC_BLOCK
    overlap = ((ci < sj + SLC_BLOCK) & (ci + CMP_LEN > sj)).astype(jnp.float32)
    ksb = k_slc.reshape(B, KV, n_slc, SLC_BLOCK, dh)
    vsb = v_slc.reshape(B, KV, n_slc, SLC_BLOCK, dh)
    kwp = jnp.pad(k_win, ((0, 0), (0, 0), (WIN, 0), (0, 0)))
    vwp = jnp.pad(v_win, ((0, 0), (0, 0), (WIN, 0), (0, 0)))
    tbl_kgn = tbl.reshape(KV, G, N_BUCKETS)
    tbl_kng = tbl_kgn.transpose(0, 2, 1)
    ar_b = jnp.arange(B)[:, None, None, None]
    ar_kv = jnp.arange(KV)[None, :, None, None]
    slc_off = jnp.arange(SLC_BLOCK)
    jj = jnp.arange(n_slc)[None, :]

    def chunk(c):
        start = c * Q_CHUNK
        t = start + jnp.arange(Q_CHUNK)
        qc = lax.dynamic_slice_in_dim(q, start, Q_CHUNK, axis=3)
        s_c = jnp.einsum('bkgqe,bkne->bkgqn', qc, kc)
        p_c, _ = masked_softmax(s_c, cmp_end[None, :] <= t[:, None])
        o_c = jnp.einsum('bkgqn,bkne->bkgqe', p_c.astype(v_cmp.dtype), vc)
        imp = jnp.einsum('bkgqn,nj->bkqj', p_c, overlap)
        own = (t // SLC_BLOCK)[:, None]
        valid = jj <= own
        forced = (jj == 0) | (jj == own) | (jj == own - 1)
        score = jnp.where(valid, jnp.where(forced, FORCE_SCORE, imp), -1.0)
        _, idx = lax.top_k(score, n_sel)
        ks = ksb[ar_b, ar_kv, idx].reshape(B, KV, Q_CHUNK, n_sel * SLC_BLOCK, dh)
        vs = vsb[ar_b, ar_kv, idx].reshape(B, KV, Q_CHUNK, n_sel * SLC_BLOCK, dh)
        pos = (idx[..., None] * SLC_BLOCK + slc_off).reshape(B, KV, Q_CHUNK, n_sel * SLC_BLOCK)
        dist = t[None, None, :, None] - pos
        bias_s = tbl_kng[ar_kv, t5_bucket(dist)].transpose(0, 1, 4, 2, 3)
        s_s = jnp.einsum('bkgqe,bkqse->bkgqs', qc, ks) + bias_s
        p_s, _ = masked_softmax(s_s, (dist >= 0)[:, :, None])
        o_s = jnp.einsum('bkgqs,bkqse->bkgqe', p_s.astype(v_slc.dtype), vs)
        kw = lax.dynamic_slice_in_dim(kwp, start, Q_CHUNK + WIN, axis=2)
        vw = lax.dynamic_slice_in_dim(vwp, start, Q_CHUNK + WIN, axis=2)
        pos_w = start - WIN + jnp.arange(Q_CHUNK + WIN)
        dist_w = t[:, None] - pos_w[None, :]
        mask_w = (dist_w >= 0) & (dist_w < WIN) & (pos_w[None, :] >= 0)
        s_w = jnp.einsum('bkgqe,bkse->bkgqs', qc, kw) + tbl_kgn[:, :, t5_bucket(dist_w)]
        p_w, _ = masked_softmax(s_w, mask_w)
        o_w = jnp.einsum('bkgqs,bkse->bkgqe', p_w.astype(v_win.dtype), vw)
        g = lax.dynamic_slice_in_dim(gates, start, Q_CHUNK, axis=3).astype(o_c.dtype)
        return g[..., 0:1] * o_c + g[..., 1:2] * o_s + g[..., 2:3] * o_w

    outs = lax.map(chunk, jnp.arange(S // Q_CHUNK))
    return outs.transpose(1, 0, 4, 2, 3, 5).reshape(B, S, C_HEADS * dh)

def conv_ffn(h, w_up, conv_w, conv_b, w_down):
    S = h.shape[1]
    u = h @ w_up
    up = jnp.pad(u, ((0, 0), (CONV_WIDTH_2 - 1, 0), (0, 0)))
    acc = conv_b
    for j in range(CONV_WIDTH_2):
        acc = acc + conv_w[j] * up[:, CONV_WIDTH_2 - 1 - j:CONV_WIDTH_2 - 1 - j + S]
    a, g = jnp.split(acc, 2, axis=-1)
    return (jax.nn.silu(g) * a) @ w_down

def second_inputs(seed: int = 0) -> dict:
    key = jax.random.key(seed)
    ks = jax.random.split(key, 14)
    nrm = jax.random.normal
    f32 = jnp.float32
    return {
        "x": nrm(ks[0], (BATCH, SEQ, D_MODEL), f32),
        "rel_table": 0.5 * nrm(ks[1], (N_HEADS, N_BUCKETS), f32),
        "w_in": nrm(ks[2], (DEPTH, D_MODEL, IN_WIDTH), f32) * D_MODEL ** -0.5,
        "w_out": nrm(ks[3], (DEPTH, MIX_WIDTH, D_MODEL), f32) * MIX_WIDTH ** -0.5,
        "cmp_w1": nrm(ks[4], (DEPTH, 2, CMP_LEN * HEAD_DIM, CMP_HIDDEN), f32) * (CMP_LEN * HEAD_DIM) ** -0.5,
        "cmp_w2": nrm(ks[5], (DEPTH, 2, CMP_HIDDEN, HEAD_DIM), f32) * CMP_HIDDEN ** -0.5,
        "cmp_pe": 0.5 * nrm(ks[6], (DEPTH, 2, CMP_LEN, HEAD_DIM), f32),
        "norm_attn": 1.0 + 0.05 * nrm(ks[7], (DEPTH, D_MODEL), f32),
        "norm_mlp": 1.0 + 0.05 * nrm(ks[8], (DEPTH, D_MODEL), f32),
        "w_up": nrm(ks[9], (DEPTH, D_MODEL, 2 * D_FF_2), f32) * D_MODEL ** -0.5,
        "conv_w": nrm(ks[10], (DEPTH, CONV_WIDTH_2, 2 * D_FF_2), f32) * CONV_WIDTH_2 ** -0.5,
        "conv_b": 0.02 * nrm(ks[11], (DEPTH, 2 * D_FF_2), f32),
        "w_down": nrm(ks[12], (DEPTH, D_FF_2, D_MODEL), f32) * D_FF_2 ** -0.5,
        "norm_final": 1.0 + 0.05 * nrm(ks[13], (D_MODEL,), f32),
    }

def second_block(x, rel_table, w_in, w_out, cmp_w1, cmp_w2, cmp_pe, norm_attn, norm_mlp,
              w_up, conv_w, conv_b, w_down, norm_final):
    B, S, _ = x.shape
    tbl_a = rel_table[:A_HEADS]
    tbl_b = rel_table[A_HEADS:A_HEADS + B_HEADS]
    tbl_c = rel_table[A_HEADS + B_HEADS:]
    for l in range(DEPTH):
        h = rmsnorm_2(x, norm_attn[l])
        proj = h @ w_in[l]
        pA = proj[..., :A_WIDTH].reshape(B, S, N_A_GROUPS, 3, A_HEADS_PER_GROUP, HEAD_DIM)
        pB = proj[..., A_WIDTH:A_WIDTH + B_WIDTH].reshape(B, S, 3, B_HEADS, HEAD_DIM)
        pC = proj[..., A_WIDTH + B_WIDTH:]
        o_a = dilated_mixer(pA, tbl_a)
        o_b = moba_mixer(pB[:, :, 0] * Q_SCALE, pB[:, :, 1], pB[:, :, 2], tbl_b)
        q_c = pC[..., :C_Q_WIDTH].reshape(B, S, C_HEADS, HEAD_DIM) * Q_SCALE
        kv_c = pC[..., C_Q_WIDTH:C_Q_WIDTH + C_KV_WIDTH].reshape(B, S, 6, C_KV_HEADS, HEAD_DIM)
        g_c = jax.nn.sigmoid(pC[..., C_Q_WIDTH + C_KV_WIDTH:].reshape(B, S, C_HEADS, 3))
        o_c = nsa_mixer(q_c, kv_c, g_c, cmp_w1[l], cmp_w2[l], cmp_pe[l], tbl_c)
        x = x + jnp.concatenate([o_a, o_b, o_c], axis=-1) @ w_out[l]
        h = rmsnorm_2(x, norm_mlp[l])
        x = x + conv_ffn(h, w_up[l], conv_w[l], conv_b[l], w_down[l])
    return rmsnorm_2(x, norm_final)


def setup_inputs(seed=0):
    out = dict(first_inputs(seed))
    for name, value in second_inputs(seed + 1).items():
        if name != "x":
            out[name + "_2"] = value
    return out


def reference(
    x, positions, norm_mix_pre, w_in, conv_w, conv_b, w_rg_a, b_rg_a, w_rg_x, b_rg_x,
    lru_lambda, attn_sinks, w_rnn_proj, w_attn_proj, w_out, norm_mix_post, norm_mlp_pre,
    w_mlp_up, w_mlp_down, norm_mlp_post, rel_table_2, w_in_2, w_out_2, cmp_w1_2, cmp_w2_2,
    cmp_pe_2, norm_attn_2, norm_mlp_2, w_up_2, conv_w_2, conv_b_2, w_down_2, norm_final_2,
):
    x = first_block(
        x, positions, norm_mix_pre, w_in, conv_w, conv_b, w_rg_a, b_rg_a, w_rg_x, b_rg_x,
        lru_lambda, attn_sinks, w_rnn_proj, w_attn_proj, w_out, norm_mix_post, norm_mlp_pre,
        w_mlp_up, w_mlp_down, norm_mlp_post,
    )
    return second_block(
        x, rel_table_2, w_in_2, w_out_2, cmp_w1_2, cmp_w2_2, cmp_pe_2, norm_attn_2, norm_mlp_2,
        w_up_2, conv_w_2, conv_b_2, w_down_2, norm_final_2,
    )


_drawn_inputs = setup_inputs


def setup_inputs(seed=0):
    import zlib

    import numpy as np

    out = dict(_drawn_inputs(seed))
    spreads = {}
    factors = {'b_rg_a': 8.0,
     'b_rg_x': 8.0,
     'attn_sinks': 3.353,
     'norm_attn_2': 4.933,
     'conv_b_2': 6.184,
     'norm_mlp_2': 5.65}
    for name, (base, spread) in spreads.items():
        noise = np.random.default_rng([zlib.crc32(name.encode()), seed]).standard_normal(out[name].shape)
        drawn = base * np.exp(spread * noise) if base else spread * noise
        out[name] = __import__('jax').numpy.asarray(drawn.astype(out[name].dtype))
    for name, factor in factors.items():
        out[name] = (out[name] * factor).astype(out[name].dtype)
    return out
```

```python
from contextlib import ExitStack

import concourse.bass as bass
import numpy as np
from concourse import mybir

F32 = mybir.dt.float32
F32R = mybir.dt.float32r
I32 = mybir.dt.int32
ALU = mybir.AluOpType
ACT = mybir.ActivationFunctionType
AX = mybir.AxisListType

P = 128
S = 256
D = 2048
NC_D = D // P
EPS = 1e-6
HD = 64
QS = HD ** -0.5
NEG = -1e30
SUB = 16
HALF = SUB // 2
FF1, FF2 = 8192, 5632
FF1_H = FF1 // P // 2
FF2_H = FF2 // P // 2
DN2_SUB = FF2_H // 2
SC = 384
N_CMP = S // 16 - 1
CMP_LEN = 32
KV_C = 3

STREAM = [("X", 16, 16), ("RG", 4, 16), ("Q", 18, 16), ("Y", 16, 16), ("V", 2, 16), ("G", 32, 16),
          ("MR", 16, 16), ("MA", 16, 16), ("O", 16, 16),
          ("UP0", 32, 16), ("DN0", 32, 16), ("UP1", 32, 16), ("DN1", 32, 16),
          ("P2", 32, 16), ("V2", 14, 16), ("O2", 16, 16),
          ("FU0", 44, 16), ("FD0", 32, DN2_SUB), ("FU1", 44, 16), ("FD1", 32, DN2_SUB)]
U0, N_UNITS, T0 = {}, 0, {}
_t = 0
for _name, _n, _ in STREAM:
    U0[_name], T0[_name] = N_UNITS, _t
    N_UNITS += _n
    _t += {"RG": 0}.get(_name, _n // 2 if _name[:2] in ("DN", "FD") else _n)

PARAM_COLS = {}
N_PARAM = 0
for _name, _n in [("norm_mix_pre", 16), ("conv_w", 64), ("conv_b", 16), ("b_rg_a", 16), ("b_rg_x", 16),
                  ("lru_lambda", 16), ("norm_mix_post", 16), ("norm_mlp_pre", 16), ("norm_mlp_post", 16),
                  ("norm_attn_2", 16), ("norm_mlp_2", 16), ("norm_final_2", 16), ("conv_w_2", 264),
                  ("conv_b_2", 88)]:
    PARAM_COLS[_name] = N_PARAM
    N_PARAM += _n

C_ID, C_ROT, C_FREQ, N_CONST = 0, 128, 256, 257


class Link:

    def __init__(self, eng, sem):
        self.eng, self.sem, self.base, self.i, self.per, self.k = eng, sem, 0, 0, 0, 0

    def begin(self, i, per):
        self.i, self.per, self.k = i, per, 0

    def end(self, trips):
        assert self.k == self.per, f"{self.k} links in the loop"
        self.base, self.i, self.per, self.k = self.base + trips * self.per, 0, 0, 0

    def flush(self):
        self.base, self.k = self.base + self.k, 0

    def __call__(self, ins):
        self.k += 1
        ins.then_inc(self.sem, 1)
        self.eng.wait_ge(self.sem, self.base + self.i * self.per + self.k)


def split_sizes(n):
    return (n // 2 + n % 2, n // 2)


def windows(t, part, n_part, col, dims):
    a = t[part:part + n_part, col:col + 1]
    return bass.AP(a.tensor, a.offset, [list(a.ap[0])] + [list(d) for d in dims])


def program(nc, dram):
    with ExitStack() as ctx:
        top = [(nc.sbuf_base + 31) // 32 * 32]

        def place(name, shape, dtype=F32, at=None):
            size = int(np.prod(shape[1:])) * 4
            off = top[0] if at is None else at
            if at is None:
                top[0] += (size + 31) // 32 * 32
            return nc.alloc_sbuf_tensor_at(name, shape, dtype, offset=off)

        def region(size):
            off = top[0]
            top[0] += size
            assert top[0] <= nc.sbuf_usable_end, top[0]
            return off

        KB = 1024
        w_raw = place("w_raw", [P, 2, SUB * P])
        w_hi = place("w_hi", [P, 4, HALF * P], F32R)
        w_lo = place("w_lo", [P, 4, HALF * P], F32R)
        x = place("x", [P, NC_D, S])
        h_hi = place("h_hi", [P, NC_D, S], F32R)
        h_lo = place("h_lo", [P, NC_D, S], F32R)
        reg_c = region(16 * KB)
        qy = place("qy", [P, NC_D, S], at=reg_c)
        cw1 = place("cw1", [P, CMP_LEN, P], at=reg_c)
        reg_d = region(64 * KB)
        d_hi = place("d_hi", [P, NC_D, S], F32R, at=reg_d)
        d_lo = place("d_lo", [P, NC_D, S], F32R, at=reg_d + 16 * KB)
        a_lru = place("a_lru", [P, NC_D, S], at=reg_d + 16 * KB)
        gates = place("gates", [P, 2 * NC_D, S], at=reg_d + 32 * KB)
        u_hi = place("u_hi", [P, FF1_H, S], F32R, at=reg_d)
        u_lo = place("u_lo", [P, FF1_H, S], F32R, at=reg_d + 32 * KB)
        qk2 = place("qk2", [P, 29, S], at=reg_d)
        ks2 = place("ks2", [P, 2, KV_C, S], at=reg_d + 29 * KB)
        v2 = place("v2", [P, 2, 14 * P], at=reg_d + 35 * KB)
        spare = [reg_d + 49 * KB]

        def in_spare(name, shape, dtype=F32):
            t = place(name, shape, dtype, at=spare[0])
            spare[0] += (int(np.prod(shape[1:])) * 4 + 31) // 32 * 32
            assert spare[0] <= reg_d + 64 * KB
            return t

        q2s = in_spare("q2s", [P, 3, S])
        v2s = in_spare("v2s", [P, 2, 3, 2, HD])
        pt2 = in_spare("pt2", [P, 3, SC])
        hid = in_spare("hid", [P, 2, KV_C * N_CMP])
        kc = in_spare("kc", [P, KV_C * N_CMP])
        vc = in_spare("vc", [N_CMP, KV_C, HD])
        vcs = in_spare("vcs", [N_CMP, HD])
        cw2 = in_spare("cw2", [P, 2, HD])
        gate2 = in_spare("gate2", [P, 2, 36])
        ptc = in_spare("ptc", [N_CMP, S])
        cpe = in_spare("cpe", [P, CMP_LEN])
        reg_e = region(16 * KB)
        xr = place("xr", [P, NC_D, S], at=reg_e)
        vv = place("vv", [P, 2, S], at=reg_e)
        mask1 = place("mask1", [P, SC], at=reg_e + 2 * KB)
        sb1 = place("sb1", [P, 2, SC], at=reg_e + 4 * KB)
        pt1 = place("pt1", [P, 2, SC], at=reg_e + 7 * KB)
        q1s = place("q1s", [P, S], at=reg_e + 10 * KB)
        kpe = place("kpe", [P, KV_C, N_CMP, CMP_LEN], at=reg_e)
        sb2 = place("sb2", [P, 2, 3, SC], at=reg_e)
        bias_a = place("bias_a", [P, 3, SC], at=reg_e + 9 * KB + 256)
        sbc = place("sbc", [P, 2, N_CMP], at=reg_e + 14 * KB)
        cmask = place("cmask", [P, 2, 2, N_CMP], at=reg_e + 14 * KB + 256)
        reg_k = region(5 * KB)
        kt = place("kt", [P, 2, S], at=reg_k)
        cos = place("cos", [P, S], at=reg_k + 2 * KB)
        sin = place("sin", [P, S], at=reg_k + 3 * KB)
        is_reset = place("is_reset", [P, S], at=reg_k + 4 * KB)
        bias_b = place("bias_b", [P, 3, SC], at=reg_k)
        par = place("par", [P, N_PARAM])
        const = place("const", [P, N_CONST])
        ones = place("ones", [P, P])
        tmp = [place(f"tmp{j}", [P, 264]) for j in range(6)]
        k2s, kcs = tmp[0:3], tmp[3]
        sinks = place("sinks", [P, 32])
        sp8 = place("sp8", [P, 2, NC_D])
        eps = place("eps", [P, 1])
        small = place("small", [P, 64])
        assert top[0] <= nc.sbuf_usable_end, (top[0], nc.sbuf_usable_end)
        ident = const[:, C_ID:C_ID + P]
        rot_t = const[:, C_ROT:C_ROT + P]
        pos_i = place("pos_i", [P, S], I32, at=reg_e)
        pos = place("pos", [P, S], at=reg_e + KB)
        ang = place("ang", [P, 4, S], at=reg_e + 2 * KB)
        onehot = place("onehot", [33, 4, 512], at=reg_d)
        table = place("table", [33, 32], at=reg_d + 8 * KB)
        rows = place("rows", [32, 4, 512], at=reg_d + 9 * KB)
        lam = place("lam", [P, 8, NC_D], at=reg_e + 8 * KB)

        bias_rows = nc.dram_tensor("bias_rows", (32, P, 512), F32, kind="Internal").ap()

        PS = ctx.enter_context(nc.psum_tensor("PS", [P, 8, 512], F32))

        def sem(name):
            return ctx.enter_context(nc.semaphore(name))

        def pcol(name, c, width=1):
            return par[:, bass.ds(PARAM_COLS[name] + c, width)]
        setup_landed = sem("setup_landed")
        w_landed = [sem(f"w_landed{s}") for s in range(2)]
        hi_ready = sem("hi_ready")
        lo_ready = sem("lo_ready")
        half_done = sem("half_done")
        acc_free = sem("acc_free")
        sq_ready = sem("sq_ready")
        ss_step = sem("ss_step")
        std_ready = sem("std_ready")
        hv_ready = sem("hv_ready")
        h_hi_ready = sem("h_hi_ready")
        h_ready = sem("h_ready")
        x_new = sem("x_new")
        rows_mm = sem("rows_mm")
        rows_ready = sem("rows_ready")
        bias_stored = sem("bias_stored")
        ang_ready = sem("ang_ready")
        rope_tab = sem("rope_tab")
        lam_exp_in = sem("lam_exp_in")
        lam_exp = sem("lam_exp")
        sp_ready = sem("sp_ready")
        setup_done = sem("setup_done")
        xr_ready = sem("xr_ready")
        xr_hi = sem("xr_hi")
        xr_lo = sem("xr_lo")
        rg_evac = sem("rg_evac")
        lru_act = sem("lru_act")
        lru_pre = sem("lru_pre")
        lru_mult = sem("lru_mult")
        rot_ready = sem("rot_ready")
        rope_done = sem("rope_done")
        yr_ready = sem("yr_ready")
        y_hi = sem("y_hi")
        y_lo = sem("y_lo")
        mask1_landed = sem("mask1_landed")
        q1_staged = sem("q1_staged")
        s1_ready = sem("s1_ready")
        s1_read = sem("s1_read")
        ng1_ready = sem("ng1_ready")
        e1_ready = sem("e1_ready")
        p1_ready = sem("p1_ready")
        t1_ready = sem("t1_ready")
        pt1_ready = sem("pt1_ready")
        o1_ready = sem("o1_ready")
        o1_free = sem("o1_free")
        sg_ready = sem("sg_ready")
        ya_hi = sem("ya_hi")
        ya_lo = sem("ya_lo")
        mix_ready = sem("mix_ready")
        mix_hi = sem("mix_hi")
        mix_lo = sem("mix_lo")
        relu_ready = sem("relu_ready")
        u_hi_ready = sem("u_hi_ready")
        u_ready = sem("u_ready")
        pad_ready = sem("pad_ready")
        av_ready = sem("av_ready")
        silu_ready = sem("silu_ready")
        uv_ready = sem("uv_ready")
        consts2_landed = sem("consts2_landed")
        gate2_ready = sem("gate2_ready")
        kpe_ready = sem("kpe_ready")
        hid_mm = sem("hid_mm")
        hid_ready = sem("hid_ready")
        kvc_mm = sem("kvc_mm")
        kvc_ready = sem("kvc_ready")
        stage2 = sem("stage2")
        bias_landed = [sem(f"bias_landed{e}") for e in range(2)]
        s2_ready = sem("s2_ready")
        s2_read = sem("s2_read")
        ng2_ready = sem("ng2_ready")
        e2_ready = sem("e2_ready")
        p2_ready = sem("p2_ready")
        t2_ready = sem("t2_ready")
        pt2_ready = sem("pt2_ready")
        o2_ready = sem("o2_ready")
        o2_hi = sem("o2_hi")
        o2_free = sem("o2_free")
        out_stored = sem("out_stored")
        dve_link, act_link = sem("dve_link"), sem("act_link")

        SETUP = 16 * 7

        def units_done(u):
            return 4 + 2 * u + 2

        block = ctx.enter_context(nc.Block())

        @block.sync
        def _(sp):
            sp.dma_start(x[:], dram["xt"]).then_inc(setup_landed, 16)
            sp.dma_start(par[:], dram["par"]).then_inc(setup_landed, 16)
            sp.dma_start(const[:], dram["const"]).then_inc(setup_landed, 16)
            sp.dma_start(onehot[:], dram["onehot"]).then_inc(setup_landed, 16)
            sp.dma_start(table[0:32, :], dram["table"]).then_inc(setup_landed, 16)
            sp.dma_start(pos_i[:], dram["pos"].partition_broadcast(P)).then_inc(setup_landed, 16)
            sp.dma_start(sinks[:], dram["sinks"].partition_broadcast(P)).then_inc(setup_landed, 16)

            def load(name, src, n, subs):
                u0 = U0[name]
                with sp.Fori(0, n // 2) as i:
                    for s in range(2):
                        sp.wait_ge(lo_ready, 2 * u0 + 2 + 4 * i + 2 * s)
                        sp.dma_start(w_raw[:, s, 0:subs * P], src[2 * i + s]).then_inc(w_landed[s], 16)

            for name, n, subs in STREAM:
                load(name, dram["w_" + name], n, subs)
            sp.wait_ge(x_new, 48)
            sp.dma_start(dram["out"], qy[:]).then_inc(out_stored, 16)
            sp.wait_ge(out_stored, 16)

        @block.gpsimd
        def _(pool):
            pool.wait_ge(rows_ready, 1)
            for var, (h0, h1) in enumerate([(0, 4), (4, 8), (8, 12), (12, 32)]):
                src = rows[h0:h1, var, :]
                rep = bass.AP(src.tensor, src.offset, [list(src.ap[0]), [0, P], [1, 512]])
                pool.dma_start(bias_rows[h0:h1], rep).then_inc(bias_stored, 16)

            pool.wait_ge(yr_ready, 2 + NC_D)
            pool.dma_start(mask1[:], dram["mask1"]).then_inc(mask1_landed, 16)
            pool.wait_ge(rope_done, 2 + 18)
            pool.tensor_copy(q1s[:], qy[:, 0, :]).then_inc(q1_staged, 1)
            with pool.Fori(1, NC_D) as t:
                pool.wait_ge(s1_ready, 2 * t)
                pool.tensor_copy(q1s[:], qy[:, t, :]).then_inc(q1_staged, 1)

            pool.wait_ge(std_ready, 4)
            pool.wait_ge(x_new, 32)
            pool.dma_start(cw1[:], dram["cw1"]).then_inc(consts2_landed, 16)
            pool.wait_ge(half_done, units_done(U0["P2"]))
            pool.dma_start(cw2[:], dram["cw2"]).then_inc(consts2_landed, 16)
            pool.dma_start(cpe[:], dram["cpe"]).then_inc(consts2_landed, 16)
            pool.dma_start(cmask[:], dram["cmask"]).then_inc(consts2_landed, 16)
            pool.wait_ge(bias_stored, 64)

            def load_bias(buf, e, slot, head):
                base = bias_rows[head]
                for blk, (c0, n) in enumerate([(0, P), (P, S)]):
                    src = bass.AP(base.tensor, base.offset + (S - 1 - P * blk), [[511, P], [1, n]])
                    pool.dma_start(buf[:, slot, c0:c0 + n], src).then_inc(bias_landed[e], 16)

            bias_buf = [bias_a, bias_b]
            pool.wait_ge(hid_mm, 1)
            with pool.Fori(0, 2) as jj:
                for e in range(2):
                    job = 2 * jj + e
                    pool.wait_ge(s2_read, job - 1 + 2)
                    for g in range(3):
                        load_bias(bias_buf[e], e, g, 4 * g + 2 * jj + e)
                    pool.wait_ge(o2_ready, job + 1)
                    pool.wait_ge(acc_free, 2 + T0["O2"])
                    if e == 0:
                        for g in range(3):
                            pool.tensor_copy(q2s[:, g, :], qk2[:, 4 * g + jj, :])
                            pool.tensor_copy(k2s[g][:, 0:S], qk2[:, 4 * g + 2 + jj, :])
                    for g in range(3):
                        last = pool.tensor_copy(v2s[:, e, g], v2[:, :, bass.ds(g * 256 + (2 * jj + e) * HD, HD)])
                    last.then_inc(stage2, 1)
            with pool.Fori(0, 4) as tt:
                for e in range(2):
                    job = 4 + 2 * tt + e
                    pool.wait_ge(s2_read, job - 1 + 2)
                    load_bias(bias_buf[e], e, 0, 12 + 2 * tt + e)
                    pool.wait_ge(o2_ready, job + 1)
                    pool.wait_ge(acc_free, 2 + T0["O2"])
                    if e == 0:
                        pool.tensor_copy(q2s[:, 0, :], qk2[:, 12 + tt, :])
                        pool.tensor_copy(k2s[0][:, 0:S], qk2[:, 16 + tt, :])
                    pool.tensor_copy(v2s[:, e, 0], v2[:, :, bass.ds(768 + (2 * tt + e) * HD, HD)]).then_inc(stage2, 1)
            with pool.Fori(0, KV_C) as kv:
                for uu in range(2):
                    for e in range(2):
                        job = 12 + 4 * kv + 2 * uu + e
                        pool.wait_ge(s2_read, job - 1 + 2)
                        load_bias(bias_buf[e], e, 0, 20 + 4 * kv + 2 * uu + e)
                        pool.wait_ge(kvc_ready, 1)
                        pool.wait_ge(o2_ready, job + 1)
                        if e == 0:
                            pool.tensor_copy(q2s[:, 0, :], qk2[:, 20 + 2 * kv + uu, :])
                        if uu == 0 and e == 0:
                            for br in range(2):
                                pool.tensor_copy(k2s[br][:, 0:S], ks2[:, br, kv, :])
                            pool.tensor_copy(kcs[:, 0:N_CMP], kc[:, bass.ds(kv * N_CMP, N_CMP)])
                            pool.tensor_copy(vcs[:], vc[:, kv, :])
                        for br in range(2):
                            last = pool.tensor_copy(v2s[:, e, br], v2[:, :, bass.ds(1280 + br * 192 + kv * HD, HD)])
                        last.then_inc(stage2, 1)

        @block.tensor
        def _(pe):
            pe.sem_inc(half_done, 4)
            pe.sem_inc(ss_step, 2)
            pe.sem_inc(t1_ready, 2)
            pe.sem_inc(o1_ready, 2)
            pe.sem_inc(o2_ready, 1)
            pe.wait_ge(setup_landed, SETUP)
            pe.wait_ge(setup_done, 1)

            def half_unit(u, s, hf, n, acc, rhs, k0, start, stop):
                pe.wait_ge(lo_ready, 4 + 2 * u + hf + 1)
                for k in range(n):
                    w0, w1 = (w[:, 2 * s + hf, k * P:(k + 1) * P] for w in (w_hi, w_lo))
                    r0, r1 = (r[:, k0 + k, :] for r in rhs)
                    pe.matmul(acc, w0, r0, start=start and k == 0, stop=False)
                    pe.matmul(acc, w0, r1, start=False, stop=False)
                    mm = pe.matmul(acc, w1, r0, start=False, stop=stop and k == n - 1)
                mm.then_inc(half_done, 1)

            def product(name, n, rhs, mid=None, peel=False, subs=SUB):
                n0, n1 = split_sizes(subs)

                def pair(i):
                    for s in range(2):
                        u = U0[name] + 2 * i + s
                        pe.wait_ge(acc_free, T0[name] + 2 * i + s + 1)
                        acc = PS[:, s, 0:S]
                        half_unit(u, s, 0, n0, acc, rhs, 0, True, False)
                        if mid is not None:
                            mid(i, s)
                        half_unit(u, s, 1, n1, acc, rhs, n0, False, True)

                if peel:
                    pair(0)
                with pe.Fori(1 if peel else 0, n // 2) as i:
                    pair(i)

            def product2(name, n, rhs, mid=None, peel=False, subs=SUB):
                n0, n1 = split_sizes(subs)

                def pair(i):
                    for s in range(2):
                        pe.wait_ge(acc_free, T0[name] + 2 * i + s + 1)
                        for part in range(2):
                            u = U0[name] + 4 * i + 2 * s + part
                            acc = PS[:, s, 0:S]
                            half_unit(u, part, 0, n0, acc, rhs, part * subs, part == 0, False)
                            if mid is not None and part == 0:
                                mid(i, s)
                            half_unit(u, part, 1, n1, acc, rhs, part * subs + n0, False, part == 1)

                if peel:
                    pair(0)
                with pe.Fori(1 if peel else 0, n // 2) as i:
                    pair(i)

            def product_v(name, n):
                with pe.Fori(0, n // 2) as i:
                    for s in range(2):
                        u = U0[name] + 2 * i + s
                        pe.wait_ge(acc_free, T0[name] + 2 * i + s + 1)
                        for hf in range(2):
                            pe.wait_ge(lo_ready, 4 + 2 * u + hf + 1)
                            for th in range(2):
                                acc = PS[:, s + 2 * th, 0:P]
                                for k in range(HALF):
                                    w0, w1 = (w[:, 2 * s + hf, k * P:(k + 1) * P] for w in (w_hi, w_lo))
                                    a0, a1 = (a[:, hf * HALF + k, th * P:(th + 1) * P] for a in (h_hi, h_lo))
                                    pe.matmul(acc, a0, w0, start=hf == 0 and k == 0, stop=False)
                                    pe.matmul(acc, a1, w0, start=False, stop=False)
                                    mm = pe.matmul(acc, a0, w1, start=False, stop=hf == 1 and k == HALF - 1)
                            mm.then_inc(half_done, 1)

            n_sq = [0]

            def sum_squares(c, s, start, stop):
                pe.wait_ge(sq_ready, n_sq[0] + c + 1)
                pe.matmul(PS[:, 7, 0:S], ones[:], tmp[s][:, 0:S], start=start, stop=stop).then_inc(ss_step, 1)

            def sums_alone(n_norm):
                if n_norm:
                    pe.wait_ge(std_ready, n_norm)
                for c in range(NC_D):
                    sum_squares(c, c % 2, c == 0, c == NC_D - 1)
                n_sq[0] += NC_D

            def sums_mid(n_norm):
                def mid(i, s):
                    if isinstance(i, int) and s == 0:
                        pe.wait_ge(std_ready, n_norm)
                        return
                    sum_squares(2 * i + s - 1, 1 - s, isinstance(i, int), False)
                return mid

            def sums_end():
                sum_squares(NC_D - 1, 1, False, True)
                n_sq[0] += NC_D

            for var in range(4):
                mm = pe.matmul(PS[0:32, var, :], table[:], onehot[:, var, :], start=True, stop=True)
            mm.then_inc(rows_mm, 1)

            sums_alone(0)
            pe.wait_ge(h_ready, 2 + NC_D)
            pe.wait_ge(rows_ready, 1)
            product("X", 16, (h_hi, h_lo))

            pe.wait_ge(xr_lo, NC_D)
            pe.wait_ge(acc_free, 2 + T0["Q"])
            with pe.Fori(0, 2) as bh:
                for hx in range(4):
                    s, hf = hx // 2, hx % 2
                    u = U0["RG"] + 2 * bh + s
                    pe.wait_ge(lo_ready, 4 + 2 * u + hf + 1)
                    pe.wait_ge(rg_evac, 4 * bh + hx + 1)
                    for b in range(2):
                        for m in range(2):
                            acc = PS[:, 2 * hf + b, m * S:(m + 1) * S]
                            for kk in range(2):
                                sub = (b * 2 + m) * 2 + kk
                                w0, w1 = (w[:, 2 * s + hf, sub * P:(sub + 1) * P] for w in (w_hi, w_lo))
                                r0, r1 = (r[:, 8 * bh + 4 * hf + 2 * b + kk, :] for r in (d_hi, d_lo))
                                pe.matmul(acc, w0, r0, start=kk == 0, stop=False)
                                pe.matmul(acc, w0, r1, start=False, stop=False)
                                mm = pe.matmul(acc, w1, r0, start=False, stop=kk == 1)
                    mm.then_inc(half_done, 1)

            pe.wait_ge(rg_evac, 2 + 8)

            def rotate(c, s):
                pe.wait_ge(acc_free, 2 + T0["Q"] + c + 1)
                pe.wait_ge(rope_done, c + 1)
                pe.matmul(PS[:, 6 + s, 0:S], rot_t, tmp[s][:, 0:S], start=True, stop=True).then_inc(rot_ready, 1)

            def rotate_mid(i, s):
                if not (isinstance(i, int) and s == 0):
                    rotate(2 * i + s - 1, 1 - s)

            product("Q", 18, (h_hi, h_lo), mid=rotate_mid, peel=True)
            rotate(17, 1)
            product("Y", 16, (h_hi, h_lo))
            product_v("V", 2)

            pe.wait_ge(acc_free, 2 + T0["G"])
            pe.wait_ge(rope_done, 2 + 18)

            def scores1(hd, gp, e, tile):
                if e == 0:
                    pe.wait_ge(q1_staged, tile + 1)
                pe.wait_ge(s1_read, hd + 1)
                lo, up = HD * e, HD * e + HD
                pe.matmul(PS[:, 2 + e, 0:P], q1s[lo:up, 0:P], kt[lo:up, gp, 0:P], start=True, stop=True)
                pe.matmul(PS[:, 2 + e, P:SC], q1s[lo:up, P:S], kt[lo:up, gp, :], start=True, stop=True)\
                    .then_inc(s1_ready, 1)

            def turn1(hd, e):
                pe.wait_ge(p1_ready, hd + 1)
                pe.wait_ge(pt1_ready, hd + 1)
                for b in range(3):
                    mm = pe.transpose(PS[:, 4 + e, b * P:(b + 1) * P], sb1[:, e, b * P:(b + 1) * P], ident)
                mm.then_inc(t1_ready, 1)

            def pv1(hd, gp, e, tile):
                pe.wait_ge(pt1_ready, 2 + hd + 1)
                if e == 0:
                    pe.wait_ge(o1_free, tile + 1)
                o = PS[HD * e:HD * e + HD, 6, :]
                g = 2 * gp + e
                pe.matmul(o[:, 0:S], vv[:, 0, g * HD:(g + 1) * HD], pt1[:, e, 0:S], start=True, stop=False,
                          skip_group_check=True)
                pe.matmul(o[:, P:S], vv[:, 1, g * HD:(g + 1) * HD], pt1[:, e, S:SC], start=False, stop=True,
                          skip_group_check=True).then_inc(o1_ready, 1)

            pe.wait_ge(mask1_landed, 16)
            for gp in range(2):
                def tile_units(i):
                    first = isinstance(i, int)
                    tile = 8 * gp + i
                    for e in range(2):
                        u = U0["G"] + 2 * tile + e
                        hd = 2 * tile + e
                        pe.wait_ge(acc_free, T0["G"] + 2 * tile + e + 1)
                        acc = PS[:, e, 0:S]
                        half_unit(u, e, 0, HALF, acc, (h_hi, h_lo), 0, True, False)
                        if not (first and e == 0):
                            turn1(hd - 1, 1 - e)
                        scores1(hd, gp, e, tile)
                        half_unit(u, e, 1, HALF, acc, (h_hi, h_lo), HALF, False, True)
                        if not (first and e == 0):
                            pv1(hd - 1, gp, 1 - e, tile - (1 - e))

                tile_units(0)
                with pe.Fori(1, 8) as i:
                    tile_units(i)
                turn1(16 * gp + 15, 1)
                pv1(16 * gp + 15, gp, 1, 8 * gp + 7)

            pe.wait_ge(y_lo, NC_D)
            product("MR", 16, (d_hi, d_lo))
            pe.wait_ge(ya_lo, NC_D)
            product("MA", 16, (h_hi, h_lo))
            pe.wait_ge(mix_lo, NC_D)
            product("O", 16, (d_hi, d_lo), mid=sums_mid(1), peel=True)
            sums_end()
            sums_alone(2)

            pe.wait_ge(h_ready, 2 + 2 * NC_D)
            for hx in range(2):
                product(f"UP{hx}", 32, (h_hi, h_lo))
                pe.wait_ge(u_ready, 2 + FF1_H * (hx + 1))
                product2(f"DN{hx}", 16, (u_hi, u_lo), mid=sums_mid(3) if hx else None, peel=bool(hx))
            sums_end()
            sums_alone(4)

            pe.wait_ge(h_ready, 2 + 3 * NC_D)
            product("P2", 32, (h_hi, h_lo))
            product_v("V2", 14)

            pe.wait_ge(consts2_landed, 64)
            pe.wait_ge(kpe_ready, KV_C)
            pe.wait_ge(acc_free, 2 + T0["O2"])
            for br in range(2):
                lo, up = HD * br, HD * br + HD
                for j in range(CMP_LEN):
                    mm = pe.matmul(PS[:, 2 + br, 0:KV_C * N_CMP], cw1[lo:up, j, :],
                                   kpe[lo:up].rearrange("p v n j -> p (v n) j")[:, :, j],
                                   start=j == 0, stop=j == CMP_LEN - 1)
            mm.then_inc(hid_mm, 1)
            pe.wait_ge(hid_ready, 1)
            pe.matmul(PS[0:HD, 4, 0:KV_C * N_CMP], cw2[:, 0, :], hid[:, 0, :], start=True, stop=True)
            for kv in range(KV_C):
                mm = pe.matmul(PS[0:N_CMP, 5, kv * HD:(kv + 1) * HD], hid[:, 1, kv * N_CMP:(kv + 1) * N_CMP],
                               cw2[:, 1, :], start=True, stop=True)
            mm.then_inc(kvc_mm, 1)
            pe.wait_ge(kvc_ready, 1)

            def scores2(bank, e, slot, k):
                lo, up = HD * e, HD * e + HD
                pe.matmul(PS[:, bank, 0:P], q2s[lo:up, slot, 0:P], k[:, 0:P], start=True, stop=True)
                return pe.matmul(PS[:, bank, P:SC], q2s[lo:up, slot, P:S], k, start=True, stop=True)

            def turn2(bank, e, slot):
                for b in range(3):
                    mm = pe.transpose(PS[:, bank, b * P:(b + 1) * P], sb2[:, e, slot, b * P:(b + 1) * P], ident)
                return mm

            def pv2(o, e, slot, start, stop):
                pe.matmul(o, v2s[:, e, slot, 0, :], pt2[:, slot, 0:S], start=start, stop=False, skip_group_check=True)
                return pe.matmul(o[:, P:S], v2s[:, e, slot, 1, :], pt2[:, slot, S:SC], start=False, stop=stop,
                                 skip_group_check=True)

            TURN = [5, 6, 0]
            with pe.Fori(0, 2) as jj:
                for e in range(2):
                    job = 2 * jj + e
                    lo, up = HD * e, HD * e + HD
                    pe.wait_ge(stage2, job + 1)
                    pe.wait_ge(s2_read, job + 1)
                    for g in range(3):
                        mm = scores2(2 + g, e, g, k2s[g][lo:up, 0:S])
                    mm.then_inc(s2_ready, 1)
                    pe.wait_ge(p2_ready, job + 1)
                    for g in range(3):
                        mm = turn2(TURN[g], e, g)
                    mm.then_inc(t2_ready, 1)
                    pe.wait_ge(pt2_ready, job + 1)
                    if e == 0:
                        pe.wait_ge(o2_free, jj + 1)
                    for g in range(3):
                        o = PS[lo:up, 7 if g < 2 else 1, (g % 2) * S:(g % 2 + 1) * S]
                        mm = pv2(o, e, g, True, True)
                    mm.then_inc(o2_ready, 1)
            with pe.Fori(0, 4) as tt:
                for e in range(2):
                    job = 4 + 2 * tt + e
                    lo, up = HD * e, HD * e + HD
                    pe.wait_ge(stage2, job + 1)
                    pe.wait_ge(s2_read, job + 1)
                    scores2(2, e, 0, k2s[0][lo:up, 0:S]).then_inc(s2_ready, 1)
                    pe.wait_ge(p2_ready, job + 1)
                    turn2(5, e, 0).then_inc(t2_ready, 1)
                    pe.wait_ge(pt2_ready, job + 1)
                    if e == 0:
                        pe.wait_ge(o2_free, 2 + tt + 1)
                    pv2(PS[lo:up, 7, 0:S], e, 0, True, True).then_inc(o2_ready, 1)
            with pe.Fori(0, KV_C) as kv:
                for uu in range(2):
                    for e in range(2):
                        job = 12 + 4 * kv + 2 * uu + e
                        lo, up = HD * e, HD * e + HD
                        pe.wait_ge(stage2, job + 1)
                        pe.wait_ge(s2_read, job + 1)
                        for qt in range(2):
                            pe.matmul(PS[:, 4, qt * N_CMP:(qt + 1) * N_CMP], q2s[lo:up, 0, qt * P:(qt + 1) * P],
                                      kcs[lo:up, 0:N_CMP], start=True, stop=True)
                        for br in range(2):
                            mm = scores2(2 + br, e, 0, k2s[br][lo:up, 0:S])
                        mm.then_inc(s2_ready, 1)
                        pe.wait_ge(p2_ready, job + 1)
                        for qt in range(2):
                            pe.transpose(PS[0:N_CMP, 0, qt * P:(qt + 1) * P], sbc[:, qt, :], ident)
                        for br in range(2):
                            mm = turn2(5 + br, e, br)
                        mm.then_inc(t2_ready, 1)
                        pe.wait_ge(pt2_ready, job + 1)
                        if e == 0:
                            pe.wait_ge(o2_free, 6 + 2 * kv + uu + 1)
                        o = PS[lo:up, 7, 0:S]
                        pv2(o, e, 0, True, False)
                        pv2(o, e, 1, False, False)
                        pe.matmul(o, vcs[:], ptc[:], start=False, stop=True, skip_group_check=True)\
                            .then_inc(o2_ready, 1)

            pe.wait_ge(o2_free, 1 + 12)
            product("O2", 16, (h_hi, h_lo), mid=sums_mid(5), peel=True)
            sums_end()

            pe.wait_ge(h_ready, 2 + 4 * NC_D)
            for hx in range(2):
                product(f"FU{hx}", 44, (h_hi, h_lo))
                pe.wait_ge(u_ready, 2 + 2 * FF1_H + FF2_H * (hx + 1))
                product2(f"FD{hx}", 16, (u_hi, u_lo), mid=sums_mid(6) if hx else None, peel=bool(hx), subs=DN2_SUB)
            sums_end()

        names = [n for n, _, _ in STREAM]
        subs_of = {n: k for n, _, k in STREAM}
        pairs_of = {n: k // 2 for n, k, _ in STREAM}

        def next_subs(name):
            at = names.index(name) + 1
            return subs_of[names[at]] if at < len(names) else 0

        def run_pairs(eng, name, trips, body, peel=False, link=None, per=0):
            lo = 0
            odd_end = next_subs(name) != subs_of[name]

            def one(i, n):
                if link:
                    link.begin(i, per)
                body(i, n)

            if peel:
                one(0, subs_of[name])
                lo = 1
            with eng.Fori(lo, trips - 1 if odd_end else trips) as i:
                one(i, subs_of[name])
            if odd_end:
                one(trips - 1, next_subs(name))
            if link:
                link.end(trips)

        @block.scalar
        def _(act):
            link = Link(act, act_link)
            act.sem_inc(acc_free, 2)
            act.sem_inc(rg_evac, 2)
            act.sem_inc(pt1_ready, 2)
            act.wait_ge(setup_landed, SETUP)
            act.wait_ge(setup_done, 1)

            def half_hi(pair, s, hf, subs):
                n0, n1 = split_sizes(subs)
                n, off = (n0, 0) if hf == 0 else (n1, n0)
                if hf == 0:
                    act.wait_ge(w_landed[s], 16 * pair + 16)
                act.wait_ge(half_done, 4 * pair + 2 * s + hf + 1)
                act.activation(w_hi[:, 2 * s + hf, 0:n * P], w_raw[:, s, off * P:(off + n) * P], ACT.Copy)\
                    .then_inc(hi_ready, 1)

            def unit_hi(pair, s, subs):
                if subs:
                    half_hi(pair, s, 0, subs)
                    half_hi(pair, s, 1, subs)

            def next_hi(pair, s, subs, hf=None):
                at = (pair, 1) if s == 0 else (pair + 1, 0)
                for k in (0, 1) if hf is None else (hf,):
                    if subs:
                        half_hi(*at, k, subs)

            n_sq, n_norm, n_h, n_x = [0], [0], [0], [0]

            def squares(src_ready):
                with act.Fori(0, NC_D // 2) as i:
                    for s in range(2):
                        c = 2 * i + s
                        if src_ready:
                            act.wait_ge(x_new, n_x[0] + c + 1)
                        act.wait_ge(ss_step, n_sq[0] + c + 1)
                        if not src_ready:
                            act.wait_ge(setup_landed, SETUP)
                        act.activation(tmp[s][:, 0:S], x[:, c, :], ACT.Square).then_inc(sq_ready, 1)
                n_sq[0] += NC_D
                n_x[0] += NC_D if src_ready else 0

            def deviation():
                act.wait_ge(ss_step, 2 + n_sq[0])
                act.activation(tmp[2][:, 0:S], PS[:, 7, 0:S], ACT.Sqrt, bias=eps[:, 0:1], scale=1.0 / D)\
                    .then_inc(std_ready, 1)
                n_norm[0] += 1

            def round_h():
                with act.Fori(0, NC_D // 2) as i:
                    for s in range(2):
                        c = 2 * i + s
                        act.wait_ge(hv_ready, n_h[0] + c + 1)
                        act.activation(h_hi[:, c, :], tmp[4 + s][:, 0:S], ACT.Copy).then_inc(h_hi_ready, 1)
                n_h[0] += NC_D

            act.wait_ge(ang_ready, 1)
            act.activation(sin[:], ang[:, 2, :], ACT.Sin)
            act.activation(cos[:], ang[:, 3, :], ACT.Sin).then_inc(rope_tab, 1)
            act.wait_ge(lam_exp_in, 1)
            act.activation(lam[:, 2, :], lam[:, 1, :], ACT.Exp).then_inc(lam_exp, 1)
            act.wait_ge(rows_mm, 1)
            act.activation(rows[:], PS[0:32, 0:4, :], ACT.Copy).then_inc(rows_ready, 1)
            squares(False)
            deviation()
            round_h()
            unit_hi(0, 0, SUB)

            def body(i, n):
                for s in range(2):
                    c, pair = 2 * i + s, U0["X"] // 2 + i
                    next_hi(pair, s, n)
                    act.wait_ge(half_done, units_done(U0["X"] + c))
                    act.wait_ge(xr_ready, c + 1)
                    act.activation(tmp[s][:, 3:3 + S], PS[:, s, 0:S], ACT.Copy).then_inc(acc_free, 1)
                    act.wait_ge(xr_ready, 2 + c + 1)
                    act.activation(d_hi[:, c, :], xr[:, c, :], ACT.Copy).then_inc(xr_hi, 1)
            act.wait_ge(bias_stored, 64)
            run_pairs(act, "X", 8, body)

            act.preload_act_table(ACT.Sigmoid)
            with act.Fori(0, 2) as bh:
                for mat in range(2):
                    u, pair = U0["RG"] + 2 * bh + mat, U0["RG"] // 2 + bh
                    next_hi(pair, mat, SUB)
                    for hf in range(2):
                        act.wait_ge(half_done, 4 + 2 * u + hf + 1)
                        for t in range(4):
                            c = 8 * bh + 4 * hf + t
                            ins = act.activation(gates[:, 16 * mat + c, :], PS[:, 2 * hf + t // 2, t % 2 * S:(t % 2 + 1) * S],
                                                 ACT.Sigmoid, bias=pcol("b_rg_x" if mat else "b_rg_a", c))
                        ins.then_inc(rg_evac, 1)

            act.preload_act_table(ACT.Exp)
            act.wait_ge(sp_ready, 1)
            act.wait_ge(xr_lo, NC_D)

            def rope_in(c, s):
                act.wait_ge(half_done, units_done(U0["Q"] + c))
                act.wait_ge(rope_done, c + 1)
                act.activation(tmp[s][:, 0:S], PS[:, s, 0:S], ACT.Copy).then_inc(acc_free, 1)

            act.wait_ge(rg_evac, 2 + 8)
            with act.Fori(0, 8) as i:
                for s in range(2):
                    c = 2 * i + s
                    next_hi(U0["Q"] // 2 + i, s, SUB)
                    act.activation(a_lru[:, c, :], gates[:, c, :], ACT.Exp, scale=sp8[:, 1, bass.ds(c, 1)])
                    act.wait_ge(lru_pre, c + 1)
                    act.activation(tmp[4 + s][:, 0:S], gates[:, c, :], ACT.Tanh, scale=sp8[:, 0, bass.ds(c, 1)])\
                        .then_inc(lru_act, 1)
                    rope_in(c, s)
            for s in range(2):
                next_hi(U0["Q"] // 2 + 8, s, SUB)
                rope_in(16 + s, s)
            act.wait_ge(lru_pre, 2 + NC_D)
            act.activation(gates[:, 0:NC_D, :], gates[:, 0:NC_D, :], ACT.Sqrt).then_inc(lru_mult, 1)
            act.wait_ge(rope_done, 2 + 18)

            act.preload_act_table(ACT.Gelu_apprx_tanh)

            def body(i, n):
                for s in range(2):
                    c = 2 * i + s
                    next_hi(U0["Y"] // 2 + i, s, n)
                    act.wait_ge(half_done, units_done(U0["Y"] + c))
                    act.wait_ge(yr_ready, c + 1)
                    act.activation(tmp[s][:, 0:S], PS[:, s, 0:S], ACT.Gelu_apprx_tanh).then_inc(acc_free, 1)
                    act.wait_ge(yr_ready, 2 + c + 1)
                    act.activation(d_hi[:, c, :], tmp[4 + s][:, 0:S], ACT.Copy).then_inc(y_hi, 1)
            run_pairs(act, "Y", 8, body)

            for s in range(2):
                next_hi(U0["V"] // 2, s, SUB)
                act.wait_ge(half_done, units_done(U0["V"] + s))
                act.activation(vv[:, 0, s * P:(s + 1) * P], PS[:, s, 0:P], ACT.Copy)
                act.activation(vv[:, 1, s * P:(s + 1) * P], PS[:, 2 + s, 0:P], ACT.Copy).then_inc(acc_free, 1)

            act.preload_act_table(ACT.Exp)

            def copy_pt1(hd, e):
                act.wait_ge(t1_ready, 2 + hd + 1)
                act.wait_ge(o1_ready, hd + 1)
                act.activation(pt1[:, e, :], PS[:, 4 + e, 0:SC], ACT.Copy).then_inc(pt1_ready, 1)

            def exp1(hd, e):
                mx, ng, den, es, rd = (small[:, 10 * e + 2 * j:10 * e + 2 * j + 2] for j in range(5))
                act.wait_ge(ng1_ready, hd + 1)
                act.activation(sb1[:, e, 0:P], sb1[:, e, 0:P], ACT.Exp, bias=ng[:, 0:1], accum_out=den[:, 0:1])
                act.activation(sb1[:, e, P:SC], sb1[:, e, P:SC], ACT.Exp, bias=ng[:, 1:2], accum_out=den[:, 1:2])
                act.activation(es, ng, ACT.Exp, bias=sinks[:, bass.ds(hd, 1)]).then_inc(e1_ready, 1)

            for gp in range(2):
                def body(i):
                    first = isinstance(i, int)
                    for e in range(2):
                        hd = 16 * gp + 2 * i + e
                        pair = U0["G"] // 2 + 8 * gp + i
                        next_hi(pair, e, SUB, 0)
                        if not (first and e == 0):
                            copy_pt1(hd - 1, 1 - e)
                        next_hi(pair, e, SUB, 1)
                        exp1(hd, e)
                        act.wait_ge(half_done, units_done(U0["G"] + hd))
                        act.activation(gates[:, hd, :], PS[:, e, 0:S], ACT.Copy).then_inc(acc_free, 1)
                body(0)
                with act.Fori(1, 8) as i:
                    body(i)
                copy_pt1(16 * gp + 15, 1)

            act.preload_act_table(ACT.Sigmoid)
            act.wait_ge(o1_free, 1 + NC_D)

            def body(i, n):
                for s in range(2):
                    c = 2 * i + s
                    next_hi(U0["MR"] // 2 + i, s, n)
                    act.wait_ge(acc_free, T0["MR"] + c + 1)
                    act.activation(tmp[s][:, 0:S], gates[:, c, :], ACT.Sigmoid).then_inc(sg_ready, 1)
                    act.activation(h_hi[:, c, :], qy[:, c, :], ACT.Copy).then_inc(ya_hi, 1)
            run_pairs(act, "MR", 8, body)

            def body(i, n):
                for s in range(2):
                    c = 2 * i + s
                    next_hi(U0["MA"] // 2 + i, s, n)
                    act.wait_ge(acc_free, T0["MA"] + c + 1)
                    act.activation(tmp[s][:, 0:S], gates[:, NC_D + c, :], ACT.Sigmoid).then_inc(sg_ready, 1)
                    act.wait_ge(mix_ready, c + 1)
                    act.activation(d_hi[:, c, :], tmp[4 + s][:, 0:S], ACT.Copy).then_inc(mix_hi, 1)
            run_pairs(act, "MA", 8, body)

            act.preload_act_table(ACT.Sqrt)
            act.wait_ge(ya_lo, NC_D)

            def body(i, n):
                for s in range(2):
                    c = 2 * i + s
                    next_hi(U0["O"] // 2 + i, s, n)
                    act.wait_ge(half_done, units_done(U0["O"] + c))
                    act.wait_ge(ss_step, n_sq[0] + c + 1)
                    act.activation(tmp[s][:, 0:S], PS[:, s, 0:S], ACT.Square).then_inc(sq_ready, 1)
                    act.activation(qy[:, c, :], PS[:, s, 0:S], ACT.Copy).then_inc(acc_free, 1)
            run_pairs(act, "O", 8, body)
            n_sq[0] += NC_D
            deviation()
            squares(True)
            deviation()
            round_h()

            n_u = 0
            for hx in range(2):
                def body(i, n):
                    for s in range(2):
                        c, name = 2 * i + s, f"UP{hx}"
                        next_hi(U0[name] // 2 + i, s, n)
                        act.wait_ge(half_done, units_done(U0[name] + c))
                        act.wait_ge(u_ready, n_u + c + 1)
                        act.activation(tmp[s][:, 0:S], PS[:, s, 0:S], ACT.Relu).then_inc(acc_free, 1)
                        act.wait_ge(acc_free, 2 + T0[name] + c + 1)
                        act.activation(u_hi[:, c, :], tmp[s][:, 0:S], ACT.Square).then_inc(u_hi_ready, 1)
                run_pairs(act, f"UP{hx}", FF1_H // 2, body)
                n_u += FF1_H

                def body(i, n):
                    for s in range(2):
                        c, name = 2 * i + s, f"DN{hx}"
                        pair = U0[name] // 2 + 2 * i + s
                        next_hi(pair, 0, n)
                        next_hi(pair, 1, n)
                        if hx == 0:
                            act.wait_ge(half_done, units_done(2 * pair + 1))
                            act.activation(qy[:, c, :], PS[:, s, 0:S], ACT.Copy).then_inc(acc_free, 1)
                        else:
                            act.wait_ge(acc_free, 2 + T0[name] + c + 1)
                            act.wait_ge(ss_step, n_sq[0] + c + 1)
                            act.activation(tmp[s][:, 0:S], qy[:, c, :], ACT.Square).then_inc(sq_ready, 1)
                run_pairs(act, f"DN{hx}", 8, body)
            n_sq[0] += NC_D
            deviation()
            squares(True)
            deviation()
            round_h()

            def body(i, n):
                for s in range(2):
                    c = 2 * i + s
                    next_hi(U0["P2"] // 2 + i, s, SUB)
                    act.wait_ge(half_done, units_done(U0["P2"] + c))
                    act.activation(qk2[:, c, :], PS[:, s, 0:S], ACT.Copy).then_inc(acc_free, 1)

            with act.Fori(0, 14) as i:
                body(i, SUB)
            for c in range(28, 32):
                s = c % 2
                next_hi(U0["P2"] // 2 + c // 2, s, SUB)
                act.wait_ge(half_done, units_done(U0["P2"] + c))
                if c == 28:
                    ins = act.activation(qk2[:, c, :], PS[:, s, 0:S], ACT.Copy)
                else:
                    for br in range(2):
                        for half in range(2):
                            ins = act.activation(ks2[HD * half:HD * half + HD, br, c - 29, :],
                                                 PS[HD * br:HD * br + HD, s, 0:S], ACT.Copy)
                ins.then_inc(acc_free, 1)

            def body(i, n):
                for s in range(2):
                    c = 2 * i + s
                    next_hi(U0["V2"] // 2 + i, s, n)
                    act.wait_ge(half_done, units_done(U0["V2"] + c))
                    act.activation(v2[:, 0, bass.ds(c * P, P)], PS[:, s, 0:P], ACT.Copy)
                    act.activation(v2[:, 1, bass.ds(c * P, P)], PS[:, 2 + s, 0:P], ACT.Copy).then_inc(acc_free, 1)
            run_pairs(act, "V2", 7, body)
            act.wait_ge(acc_free, 2 + T0["O2"])
            act.activation(gate2[:], v2[:, :, 13 * P:13 * P + 36], ACT.Sigmoid).then_inc(gate2_ready, 1)

            act.wait_ge(hid_mm, 1)
            act.activation(hid[:], PS[:, 2:4, 0:KV_C * N_CMP], ACT.Gelu_apprx_tanh).then_inc(hid_ready, 1)
            act.wait_ge(kvc_mm, 1)
            act.activation(kc[0:HD], PS[0:HD, 4, 0:KV_C * N_CMP], ACT.Copy)
            act.activation(kc[HD:P], PS[0:HD, 4, 0:KV_C * N_CMP], ACT.Copy)
            act.activation(vc[:], PS[0:N_CMP, 5, 0:KV_C * HD].rearrange("p (v d) -> p v d", v=KV_C), ACT.Copy)\
                .then_inc(kvc_ready, 1)
            act.preload_act_table(ACT.Exp)

            def exp2(src, ng, den):
                return act.activation(src, src, ACT.Exp, bias=ng, accum_out=den)

            def out_hi(chunk, src):
                act.activation(h_hi[:, chunk, :], src, ACT.Copy).then_inc(o2_hi, 1)

            TURN = [5, 6, 0]
            with act.Fori(0, 2) as jj:
                for e in range(2):
                    job = 2 * jj + e
                    act.wait_ge(ng2_ready, job + 1)
                    exp2(sb2[:, e, :, 0:P], small[:, 22:23], small[:, 24:25])
                    exp2(sb2[:, e, :, P:SC], small[:, 23:24], small[:, 25:26]).then_inc(e2_ready, 1)
                    act.wait_ge(t2_ready, job + 1)
                    for g in range(3):
                        ins = act.activation(pt2[:, g, :], PS[:, TURN[g], 0:SC], ACT.Copy)
                    ins.then_inc(pt2_ready, 1)
                act.wait_ge(o2_ready, 1 + 2 * jj + 2)
                for g in range(3):
                    out_hi(2 * g + jj, PS[:, 7 if g < 2 else 1, (g % 2) * S:(g % 2 + 1) * S])
            with act.Fori(0, 4) as tt:
                for e in range(2):
                    job = 4 + 2 * tt + e
                    act.wait_ge(ng2_ready, job + 1)
                    exp2(sb2[:, e, 0, 0:P], small[:, 22:23], small[:, 24:25])
                    exp2(sb2[:, e, 0, P:SC], small[:, 23:24], small[:, 25:26]).then_inc(e2_ready, 1)
                    act.wait_ge(t2_ready, job + 1)
                    act.activation(pt2[:, 0, :], PS[:, 5, 0:SC], ACT.Copy).then_inc(pt2_ready, 1)
                act.wait_ge(o2_ready, 1 + 4 + 2 * tt + 2)
                out_hi(6 + tt, PS[:, 7, 0:S])
            with act.Fori(0, KV_C) as kv:
                for uu in range(2):
                    for e in range(2):
                        job = 12 + 4 * kv + 2 * uu + e
                        act.wait_ge(ng2_ready, job + 1)
                        for br in range(2):
                            exp2(sb2[:, e, br, 0:P], small[:, 26 + 2 * br:27 + 2 * br], small[:, 32 + 2 * br:33 + 2 * br])
                            exp2(sb2[:, e, br, P:SC], small[:, 27 + 2 * br:28 + 2 * br], small[:, 33 + 2 * br:34 + 2 * br])
                        for qt in range(2):
                            ins = act.activation(sbc[:, qt, :], sbc[:, qt, :], ACT.Exp, bias=small[:, 30 + qt:31 + qt])
                        ins.then_inc(e2_ready, 1)
                        act.wait_ge(t2_ready, job + 1)
                        for br in range(2):
                            act.activation(pt2[:, br, :], PS[:, 5 + br, 0:SC], ACT.Copy)
                        act.activation(ptc[:], PS[0:N_CMP, 0, 0:S], ACT.Copy).then_inc(pt2_ready, 1)
                    act.wait_ge(o2_ready, 1 + 12 + 4 * kv + 2 * uu + 2)
                    out_hi(10 + 2 * kv + uu, PS[:, 7, 0:S])

            act.preload_act_table(ACT.Sqrt)

            def sums_of_x(name, units):
                def body(i, n):
                    for s in range(2):
                        c = 2 * i + s
                        pair = U0[name] // 2 + (i if units == 1 else 2 * i + s)
                        next_hi(pair, s if units == 1 else 0, n if units == 1 else subs_of[name])
                        if units == 2:
                            next_hi(pair, 1, n if s else subs_of[name])
                        act.wait_ge(acc_free, 2 + T0[name] + c + 1)
                        act.wait_ge(ss_step, n_sq[0] + c + 1)
                        act.activation(tmp[s][:, 0:S], x[:, c, :], ACT.Square).then_inc(sq_ready, 1)
                run_pairs(act, name, 8, body)
                n_sq[0] += NC_D

            sums_of_x("O2", 1)
            deviation()
            round_h()

            act.preload_act_table(ACT.Silu)
            n_v = 0
            for hx in range(2):
                def body(i, n):
                    name = f"FU{hx}"
                    for s in range(2):
                        next_hi(U0[name] // 2 + i, s, subs_of[name] if s == 0 else n)
                        act.wait_ge(half_done, units_done(U0[name] + 2 * i + s))
                        act.activation(tmp[s][:, 2:2 + S], PS[:, s, 0:S], ACT.Copy).then_inc(acc_free, 1)
                    act.wait_ge(av_ready, n_v + i + 1)
                    act.activation(tmp[5][:, 0:S], tmp[4][:, 0:S], ACT.Silu).then_inc(silu_ready, 1)
                    act.wait_ge(uv_ready, n_v + i + 1)
                    act.activation(u_hi[:, i, :], tmp[2][:, 0:S], ACT.Copy).then_inc(u_hi_ready, 1)
                run_pairs(act, f"FU{hx}", FF2_H, body)
                n_v += FF2_H
                if hx == 0:
                    def body(i, n):
                        for s in range(2):
                            pair = U0["FD0"] // 2 + 2 * i + s
                            next_hi(pair, 0, DN2_SUB)
                            next_hi(pair, 1, n if s else DN2_SUB)
                    run_pairs(act, "FD0", 8, body)
                    act.wait_ge(acc_free, 2 + T0["FU1"])
                else:
                    act.preload_act_table(ACT.Sqrt)
                    sums_of_x("FD1", 2)
            deviation()

        @block.vector
        def _(dve):
            link = Link(dve, dve_link)
            tt, ts, stt = dve.tensor_tensor, dve.tensor_scalar, dve.scalar_tensor_tensor

            dve.memset(ones[:], 1.0)
            dve.memset(eps[:], EPS)
            dve.memset(table[32:33, :], NEG)
            for credit, n in [(lo_ready, 4), (xr_ready, 2), (lru_pre, 2), (rope_done, 2), (yr_ready, 2), (s1_read, 2),
                              (o1_free, 1), (s2_read, 1), (o2_free, 1), (u_ready, 2), (h_ready, 2)]:
                dve.sem_inc(credit, n)
            link(dve.memset(tmp[0][:, 0:3], 0.0))
            dve.sem_inc(setup_done, 1)
            dve.wait_ge(setup_landed, SETUP)

            TWO_PI = 2 * np.pi
            c1 = 6.28125
            c2 = float(np.float32(np.round((TWO_PI - c1) * 2 ** 21) / 2 ** 21))
            c3 = float(np.float32(TWO_PI - c1 - c2))
            magic = 1.5 * 2 ** 23
            edge = 3.1415925
            link(dve.tensor_copy(pos[:], pos_i[:]))
            link(ts(ang[:, 0, :], pos[:], const[:, C_FREQ:C_FREQ + 1], None, ALU.mult))
            for dst, turn in ((2, 0.0), (3, 0.25)):
                link(ts(ang[:, 1, :], ang[:, 0, :], 1 / TWO_PI, turn, ALU.mult, ALU.add))
                link(ts(ang[:, 1, :], ang[:, 1, :], magic, None, ALU.add))
                link(ts(ang[:, 1, :], ang[:, 1, :], magic, None, ALU.subtract))
                link(stt(ang[:, dst, :], ang[:, 1, :], -c1, ang[:, 0, :], ALU.mult, ALU.add))
                link(stt(ang[:, dst, :], ang[:, 1, :], -c2, ang[:, dst, :], ALU.mult, ALU.add))
                link(stt(ang[:, dst, :], ang[:, 1, :], -c3, ang[:, dst, :], ALU.mult, ALU.add))
                if turn:
                    link(ts(ang[:, dst, :], ang[:, dst, :], np.pi / 2, None, ALU.add))
                ins = ts(ang[:, dst, :], ang[:, dst, :], edge, -edge, ALU.min, ALU.max)
                if not turn:
                    link(ins)
            ins.then_inc(ang_ready, 1)
            link(ts(is_reset[:], pos[:], 0.0, None, ALU.is_equal))

            lm = pcol("lru_lambda", 0, NC_D)
            link(ts(lam[:, 0, :], lm, -1.0, None, ALU.mult))
            tt(lam[:, 1, :], lam[:, 0, :], lm, ALU.min).then_inc(lam_exp_in, 1)
            dve.wait_ge(lam_exp, 1)
            link(ts(lam[:, 3, :], lam[:, 2, :], 2.0, None, ALU.add))
            link(dve.reciprocal(lam[:, 3, :], lam[:, 3, :]))
            link(tt(lam[:, 4, :], lam[:, 2, :], lam[:, 3, :], ALU.mult))
            link(tt(lam[:, 5, :], lam[:, 4, :], lam[:, 4, :], ALU.mult))
            link(ts(lam[:, 6, :], lam[:, 5, :], 1.0 / 17, None, ALU.mult))
            for k in range(7, 0, -1):
                link(stt(lam[:, 6, :], lam[:, 6, :], 1.0 / (2 * k + 1), lam[:, 5, :], ALU.add, ALU.mult))
            link(stt(lam[:, 6, :], lam[:, 6, :], 1.0, lam[:, 4, :], ALU.add, ALU.mult))
            link(ts(lam[:, 7, :], lam[:, 0, :], 0.0, 0.5, ALU.max, ALU.mult))
            link(tt(lam[:, 6, :], lam[:, 6, :], lam[:, 7, :], ALU.add))
            ts(sp8[:, 0, :], lam[:, 6, :], 16.0, None, ALU.mult)
            ts(sp8[:, 1, :], lam[:, 6, :], -16.0, None, ALU.mult).then_inc(sp_ready, 1)
            link.flush()

            def half_lo(pair, s, hf, subs):
                n0, n1 = split_sizes(subs)
                n, off = (n0, 0) if hf == 0 else (n1, n0)
                slot = 2 * s + hf
                dve.wait_ge(hi_ready, 4 * pair + 2 * s + hf + 1)
                tt(w_lo[:, slot, 0:n * P], w_raw[:, s, off * P:(off + n) * P],
                   w_hi[:, slot, 0:n * P].bitcast(F32), ALU.subtract).then_inc(lo_ready, 1)

            def next_lo(pair, s, subs, hf=None):
                at = (pair, 1) if s == 0 else (pair + 1, 0)
                for k in (0, 1) if hf is None else (hf,):
                    if subs:
                        half_lo(*at, k, subs)

            n_norm, n_h = [0], [0]
            rstd = tmp[3][:, 0:S]

            def inverse_deviation():
                n_norm[0] += 1
                dve.wait_ge(std_ready, n_norm[0])
                link(dve.reciprocal(rstd, tmp[2][:, 0:S]))
                link.flush()

            def normalise(gain):
                inverse_deviation()

                def scaled(c, s):
                    dve.wait_ge(h_ready, n_h[0] + c + 1)
                    stt(tmp[4 + s][:, 0:S], x[:, c, :], pcol(gain, c), rstd, ALU.mult, ALU.mult).then_inc(hv_ready, 1)

                def lo(c, s):
                    dve.wait_ge(h_hi_ready, n_h[0] + c + 1)
                    tt(h_lo[:, c, :], tmp[4 + s][:, 0:S], h_hi[:, c, :].bitcast(F32), ALU.subtract).then_inc(h_ready, 1)

                scaled(0, 0)
                with dve.Fori(0, NC_D // 2 - 1) as i:
                    for s in range(2):
                        scaled(2 * i + s + 1, 1 - s)
                        lo(2 * i + s, s)
                scaled(NC_D - 1, 1)
                lo(NC_D - 2, 0)
                lo(NC_D - 1, 1)
                n_h[0] += NC_D

            def add_branch(gain):
                inverse_deviation()

                def scaled(c, s):
                    link(stt(tmp[4 + s][:, 0:S], qy[:, c, :], pcol(gain, c), rstd, ALU.mult, ALU.mult))

                def add(c, s):
                    tt(x[:, c, :], x[:, c, :], tmp[4 + s][:, 0:S], ALU.add).then_inc(x_new, 1)

                with dve.Fori(0, NC_D // 2) as i:
                    link.begin(i, 2)
                    for s in range(2):
                        scaled(2 * i + s, s)
                        add(2 * i + s, s)
                link.end(NC_D // 2)

            normalise("norm_mix_pre")
            half_lo(0, 0, 0, SUB)
            half_lo(0, 0, 1, SUB)

            link(dve.memset(tmp[0][:, 0:3], 0.0))
            link(dve.memset(tmp[1][:, 0:3], 0.0))
            link.flush()

            def body(i, n):
                for s in range(2):
                    c = 2 * i + s
                    next_lo(U0["X"] // 2 + i, s, n)
                    dve.wait_ge(acc_free, 2 + T0["X"] + c + 1)
                    pad, t2, t3 = tmp[s], tmp[2][:, 0:S], tmp[3][:, 0:S]
                    w = [pcol("conv_w", 4 * c + k) for k in range(4)]
                    link(ts(t2, pad[:, 3:3 + S], w[3], pcol("conv_b", c), ALU.mult, ALU.add))
                    link(stt(t3, pad[:, 2:2 + S], w[2], t2, ALU.mult, ALU.add))
                    link(stt(t2, pad[:, 1:1 + S], w[1], t3, ALU.mult, ALU.add))
                    stt(xr[:, c, :], pad[:, 0:S], w[0], t2, ALU.mult, ALU.add).then_inc(xr_ready, 1)
                    dve.wait_ge(xr_hi, c + 1)
                    tt(d_lo[:, c, :], xr[:, c, :], d_hi[:, c, :].bitcast(F32), ALU.subtract).then_inc(xr_lo, 1)
            run_pairs(dve, "X", 8, body, link=link, per=6)

            with dve.Fori(0, 2) as bh:
                for mat in range(2):
                    next_lo(U0["RG"] // 2 + bh, mat, SUB)

            def decay(c, s):
                a, r, th = a_lru[:, c, :], gates[:, c, :], tmp[4 + s][:, 0:S]
                dve.wait_ge(lru_act, c + 1)
                link(stt(a, is_reset[:], 1.0, a, ALU.subtract, ALU.mult, reverse0=True))
                link(tt(th, th, is_reset[:], ALU.max))
                link(tt(r, a, a, ALU.mult))
                stt(r, r, 1.0, th, ALU.add, ALU.mult).then_inc(lru_pre, 1)

            def rope(c, s, out):
                dve.wait_ge(rope_done, 2 + c)
                link(tt(tmp[2][:, 0:S], tmp[s][:, 0:S], cos[:], ALU.mult))
                dve.wait_ge(rot_ready, c + 1)
                link(tt(tmp[3][:, 0:S], PS[:, 6 + s, 0:S], sin[:], ALU.mult))
                tt(out, tmp[2][:, 0:S], tmp[3][:, 0:S], ALU.add).then_inc(rope_done, 1)

            dve.wait_ge(rope_tab, 1)

            def body(i):
                for s in range(2):
                    c = 2 * i + s
                    next_lo(U0["Q"] // 2 + i, s, SUB)
                    decay(c, s)
                    if not (isinstance(i, int) and s == 0):
                        dve.wait_ge(acc_free, 2 + T0["Q"] + c)
                        rope(c - 1, 1 - s, qy[:, c - 1, :])

            link.begin(0, 5 + 3 + 2)
            body(0)
            link.k = 0
            link.flush()
            link.base += 8
            with dve.Fori(1, 8) as i:
                link.begin(i - 1, 10)
                body(i)
            link.end(7)
            next_lo(U0["Q"] // 2 + 8, 0, SUB)
            dve.wait_ge(acc_free, 2 + T0["Q"] + 16)
            rope(15, 1, qy[:, 15, :])
            next_lo(U0["Q"] // 2 + 8, 1, SUB)
            for t in range(2):
                dve.wait_ge(acc_free, 2 + T0["Q"] + 17 + t)
                rope(16 + t, t, kt[:, t, :])
            link.flush()

            dve.wait_ge(lru_mult, 1)

            def body(i, n):
                for s in range(2):
                    c = 2 * i + s
                    next_lo(U0["Y"] // 2 + i, s, n)
                    t2, t3, y = tmp[2][:, 0:S], tmp[3][:, 0:S], tmp[4 + s][:, 0:S]
                    link(tt(t2, gates[:, c, :], gates[:, NC_D + c, :], ALU.mult))
                    link(tt(t3, t2, xr[:, c, :], ALU.mult))
                    link(dve.tensor_tensor_scan(t2, a_lru[:, c, :], t3, 0.0, ALU.mult, ALU.add))
                    dve.wait_ge(acc_free, 2 + T0["Y"] + c + 1)
                    tt(y, t2, tmp[s][:, 0:S], ALU.mult).then_inc(yr_ready, 1)
                    dve.wait_ge(y_hi, c + 1)
                    tt(d_lo[:, c, :], y, d_hi[:, c, :].bitcast(F32), ALU.subtract).then_inc(y_lo, 1)
            run_pairs(dve, "Y", 8, body, link=link, per=6)

            for s in range(2):
                next_lo(U0["V"] // 2, s, SUB)

            dve.wait_ge(mask1_landed, 16)

            def soft1(hd, e):
                mx, ng = (small[:, 10 * e + 2 * j:10 * e + 2 * j + 2] for j in range(2))
                dve.wait_ge(s1_ready, hd + 1)
                dve.wait_ge(t1_ready, hd + 1)
                stt(sb1[:, e, :], PS[:, 2 + e, 0:SC], QS, mask1[:], ALU.mult, ALU.add).then_inc(s1_read, 1)
                dve.wait_ge(s1_read, 2 + hd + 1)
                dve.tensor_reduce(mx[:, 0:1], sb1[:, e, 0:P], AX.X, ALU.max)
                link(dve.tensor_reduce(mx[:, 1:2], sb1[:, e, P:SC], AX.X, ALU.max))
                ts(ng, mx, sinks[:, bass.ds(hd, 1)], -1.0, ALU.max, ALU.mult).then_inc(ng1_ready, 1)

            def norm1(hd, e):
                den, es, rd = (small[:, 10 * e + 2 * j:10 * e + 2 * j + 2] for j in range(2, 5))
                dve.wait_ge(e1_ready, hd + 1)
                link(tt(den, den, es, ALU.add))
                link(dve.reciprocal(rd, den))
                ts(sb1[:, e, 0:P], sb1[:, e, 0:P], rd[:, 0:1], None, ALU.mult)
                ts(sb1[:, e, P:SC], sb1[:, e, P:SC], rd[:, 1:2], None, ALU.mult).then_inc(p1_ready, 1)

            def out1(tile):
                dve.wait_ge(o1_ready, 2 + 2 * tile + 2)
                dve.tensor_copy(qy[:, tile, :], PS[:, 6, 0:S]).then_inc(o1_free, 1)

            for gp in range(2):
                def body(i):
                    first = isinstance(i, int)
                    for e in range(2):
                        hd = 16 * gp + 2 * i + e
                        pair = U0["G"] // 2 + 8 * gp + i
                        next_lo(pair, e, SUB, 0)
                        if e == 1 and not first:
                            out1(8 * gp + i - 1)
                        soft1(hd, e)
                        next_lo(pair, e, SUB, 1)
                        norm1(hd, e)
                link.begin(0, 6)
                body(0)
                with dve.Fori(1, 8) as i:
                    link.begin(i, 6)
                    body(i)
                link.end(8)
                out1(8 * gp + 7)

            def body(i, n):
                for s in range(2):
                    c = 2 * i + s
                    next_lo(U0["MR"] // 2 + i, s, n)
                    dve.wait_ge(ya_hi, c + 1)
                    tt(h_lo[:, c, :], qy[:, c, :], h_hi[:, c, :].bitcast(F32), ALU.subtract).then_inc(ya_lo, 1)
                    dve.wait_ge(sg_ready, c + 1)
                    dve.wait_ge(half_done, units_done(U0["MR"] + c))
                    tt(gates[:, c, :], PS[:, s, 0:S], tmp[s][:, 0:S], ALU.mult).then_inc(acc_free, 1)
            run_pairs(dve, "MR", 8, body)

            def body(i, n):
                for s in range(2):
                    c = 2 * i + s
                    next_lo(U0["MA"] // 2 + i, s, n)
                    dve.wait_ge(sg_ready, NC_D + c + 1)
                    dve.wait_ge(half_done, units_done(U0["MA"] + c))
                    tt(tmp[2][:, 0:S], PS[:, s, 0:S], tmp[s][:, 0:S], ALU.mult).then_inc(acc_free, 1)
                    dve.wait_ge(acc_free, 2 + T0["MA"] + c + 1)
                    tt(tmp[4 + s][:, 0:S], tmp[2][:, 0:S], gates[:, c, :], ALU.add).then_inc(mix_ready, 1)
                    dve.wait_ge(mix_hi, c + 1)
                    tt(d_lo[:, c, :], tmp[4 + s][:, 0:S], d_hi[:, c, :].bitcast(F32), ALU.subtract).then_inc(mix_lo, 1)
            run_pairs(dve, "MA", 8, body)

            def body(i, n):
                for s in range(2):
                    next_lo(U0["O"] // 2 + i, s, n)
            run_pairs(dve, "O", 8, body)
            add_branch("norm_mix_post")
            normalise("norm_mlp_pre")

            n_u = 0
            for hx in range(2):
                def body(i, n):
                    for s in range(2):
                        c, name = 2 * i + s, f"UP{hx}"
                        next_lo(U0[name] // 2 + i, s, n)
                        dve.wait_ge(acc_free, 2 + T0[name] + c + 1)
                        link(tt(tmp[4 + s][:, 0:S], tmp[s][:, 0:S], tmp[s][:, 0:S], ALU.mult))
                        dve.wait_ge(u_hi_ready, n_u + c + 1)
                        tt(u_lo[:, c, :], tmp[4 + s][:, 0:S], u_hi[:, c, :].bitcast(F32), ALU.subtract)\
                            .then_inc(u_ready, 1)
                run_pairs(dve, f"UP{hx}", FF1_H // 2, body, link=link, per=2)
                n_u += FF1_H

                def body(i, n):
                    for s in range(2):
                        c, name = 2 * i + s, f"DN{hx}"
                        pair = U0[name] // 2 + 2 * i + s
                        next_lo(pair, 0, n)
                        next_lo(pair, 1, n)
                        if hx:
                            dve.wait_ge(half_done, units_done(2 * pair + 1))
                            tt(qy[:, c, :], PS[:, s, 0:S], qy[:, c, :], ALU.add).then_inc(acc_free, 1)
                run_pairs(dve, f"DN{hx}", 8, body)
            add_branch("norm_mlp_post")
            normalise("norm_attn_2")

            for name in ("P2", "V2"):
                def body(i, n):
                    for s in range(2):
                        next_lo(U0[name] // 2 + i, s, n)
                run_pairs(dve, name, pairs_of[name], body)

            dve.wait_ge(consts2_landed, 64)
            dve.wait_ge(acc_free, 2 + T0["O2"])
            for kv in range(KV_C):
                tt(kpe[:, kv], windows(qk2[:, 26 + kv, :], 0, P, 0, [[16, N_CMP], [1, CMP_LEN]]),
                   windows(cpe[:], 0, P, 0, [[0, N_CMP], [1, CMP_LEN]]), ALU.add).then_inc(kpe_ready, 1)
            dve.wait_ge(gate2_ready, 1)
            dve.wait_ge(hid_ready, 1)

            mxa, nga, dena, rda = (small[:, c:c + 2] for c in (20, 22, 24, 56))

            def biased(bank, e, slot, bias):
                return stt(sb2[:, e, slot, :], PS[:, bank, 0:SC], QS, bias, ALU.mult, ALU.add)

            bias_buf = [bias_a, bias_b]

            def scores_in(job, e, landed):
                dve.wait_ge(s2_ready, job + 1)
                dve.wait_ge(bias_landed[e], landed)

            def out_lo(chunk, bank, col, count):
                dve.wait_ge(o2_hi, count)
                return tt(h_lo[:, chunk, :], PS[:, bank, col:col + S], h_hi[:, chunk, :].bitcast(F32), ALU.subtract)

            with dve.Fori(0, 2) as jj:
                link.begin(jj, 4)
                for e in range(2):
                    job = 2 * jj + e
                    scores_in(job, e, 96 * jj + 96)
                    for g in range(3):
                        ins = biased(2 + g, e, g, bias_buf[e][:, g, :])
                    ins.then_inc(s2_read, 1)
                    dve.wait_ge(s2_read, 1 + job + 1)
                    dve.tensor_reduce(mxa[:, 0:1], sb2[:, e, :, 0:P], AX.XY, ALU.max)
                    link(dve.tensor_reduce(mxa[:, 1:2], sb2[:, e, :, P:SC], AX.XY, ALU.max))
                    ts(nga, mxa, -1.0, None, ALU.mult).then_inc(ng2_ready, 1)
                    dve.wait_ge(e2_ready, job + 1)
                    link(dve.reciprocal(rda, dena))
                    ts(sb2[:, e, :, 0:P], sb2[:, e, :, 0:P], rda[:, 0:1], None, ALU.mult)
                    ts(sb2[:, e, :, P:SC], sb2[:, e, :, P:SC], rda[:, 1:2], None, ALU.mult).then_inc(p2_ready, 1)
                for g in range(3):
                    ins = out_lo(2 * g + jj, 7 if g < 2 else 1, (g % 2) * S, 3 * jj + 3)
                ins.then_inc(o2_free, 1)
            link.end(2)
            with dve.Fori(0, 4) as b:
                link.begin(b, 4)
                for e in range(2):
                    job = 4 + 2 * b + e
                    scores_in(job, e, 192 + 32 * b + 32)
                    biased(2, e, 0, bias_buf[e][:, 0, :]).then_inc(s2_read, 1)
                    dve.wait_ge(s2_read, 1 + job + 1)
                    dve.tensor_reduce(mxa[:, 0:1], sb2[:, e, 0, 0:P], AX.X, ALU.max)
                    link(dve.tensor_reduce(mxa[:, 1:2], sb2[:, e, 0, P:SC], AX.X, ALU.max))
                    ts(nga, mxa, -1.0, None, ALU.mult).then_inc(ng2_ready, 1)
                    dve.wait_ge(e2_ready, job + 1)
                    link(dve.reciprocal(rda, dena))
                    ts(sb2[:, e, 0, 0:P], sb2[:, e, 0, 0:P], rda[:, 0:1], None, ALU.mult)
                    ts(sb2[:, e, 0, P:SC], sb2[:, e, 0, P:SC], rda[:, 1:2], None, ALU.mult).then_inc(p2_ready, 1)
                out_lo(6 + b, 7, 0, 6 + b + 1).then_inc(o2_free, 1)
            link.end(4)
            mxc, ngc, denc, cfc = (small[:, c:c + 6] for c in (38, 26, 32, 44))
            with dve.Fori(0, KV_C) as kv:
                link.begin(kv, 24)
                for uu in range(2):
                    for e in range(2):
                        job = 12 + 4 * kv + 2 * uu + e
                        head = 4 * kv + 2 * uu + e
                        scores_in(job, e, 320 + 64 * kv + 32 * uu + 32)
                        for br in range(2):
                            biased(2 + br, e, br, bias_buf[e][:, 0, :])
                        stt(sbc[:], PS[:, 4, 0:2 * N_CMP].rearrange("p (q n) -> p q n", q=2), QS, cmask[:, 0], ALU.mult, ALU.add)\
                            .then_inc(s2_read, 1)
                        dve.wait_ge(s2_read, 1 + job + 1)
                        for br in range(2):
                            dve.tensor_reduce(mxc[:, 2 * br:2 * br + 1], sb2[:, e, br, 0:P], AX.X, ALU.max)
                            dve.tensor_reduce(mxc[:, 2 * br + 1:2 * br + 2], sb2[:, e, br, P:SC], AX.X, ALU.max)
                        link(dve.tensor_reduce(mxc[:, 4:6], sbc[:], AX.X, ALU.max))
                        ts(ngc, mxc, -1.0, None, ALU.mult).then_inc(ng2_ready, 1)
                        dve.wait_ge(e2_ready, job + 1)
                        link(tt(sbc[:], sbc[:], cmask[:, 1], ALU.mult))
                        link(dve.tensor_reduce(denc[:, 4:6], sbc[:], AX.X, ALU.add))
                        link(ts(denc[:, 4:6], denc[:, 4:6], 1e-30, None, ALU.max))
                        link(dve.reciprocal(cfc, denc))
                        for br, col in ((0, 1), (1, 2), (2, 0)):
                            ins = tt(cfc[:, 2 * br:2 * br + 2], cfc[:, 2 * br:2 * br + 2],
                                     gate2[:, :, bass.ds(3 * head + col, 1)].rearrange("p a b -> p (a b)"), ALU.mult)
                        link(ins)
                        for br in range(2):
                            ts(sb2[:, e, br, 0:P], sb2[:, e, br, 0:P], cfc[:, 2 * br:2 * br + 1], None, ALU.mult)
                            ts(sb2[:, e, br, P:SC], sb2[:, e, br, P:SC], cfc[:, 2 * br + 1:2 * br + 2], None, ALU.mult)
                        for qt in range(2):
                            ins = ts(sbc[:, qt, :], sbc[:, qt, :], cfc[:, 4 + qt:5 + qt], None, ALU.mult)
                        ins.then_inc(p2_ready, 1)
                    out_lo(10 + 2 * kv + uu, 7, 0, 10 + 2 * kv + uu + 1).then_inc(o2_free, 1)
            link.end(KV_C)

            def join_x(name, units):
                def body(i, n):
                    for s in range(2):
                        c = 2 * i + s
                        if units == 1:
                            unit = U0[name] + 2 * i + s
                            next_lo(U0[name] // 2 + i, s, n)
                        else:
                            pair = U0[name] // 2 + 2 * i + s
                            unit = 2 * pair + 1
                            next_lo(pair, 0, subs_of[name])
                            next_lo(pair, 1, n if s else subs_of[name])
                        dve.wait_ge(half_done, units_done(unit))
                        tt(x[:, c, :], PS[:, s, 0:S], x[:, c, :], ALU.add).then_inc(acc_free, 1)
                run_pairs(dve, name, 8, body)

            join_x("O2", 1)
            normalise("norm_mlp_2")

            link(dve.memset(tmp[0][:, 0:2], 0.0))
            link(dve.memset(tmp[1][:, 0:2], 0.0))
            link.flush()
            n_v = 0
            for hx in range(2):
                def body(i, n):
                    name = f"FU{hx}"
                    for s, t in ((0, 3), (1, 4)):
                        next_lo(U0[name] // 2 + i, s, subs_of[name] if s == 0 else n)
                        c = 44 * s + FF2_H * hx + i
                        dve.wait_ge(acc_free, 2 + T0[name] + 2 * i + s + 1)
                        v, w = tmp[t][:, 0:S], [pcol("conv_w_2", 3 * c + k) for k in range(3)]
                        link(ts(v, tmp[s][:, 2:2 + S], w[0], pcol("conv_b_2", c), ALU.mult, ALU.add))
                        link(stt(v, tmp[s][:, 1:1 + S], w[1], v, ALU.mult, ALU.add))
                        ins = stt(v, tmp[s][:, 0:S], w[2], v, ALU.mult, ALU.add)
                        if s == 0:
                            link(ins)
                    ins.then_inc(av_ready, 1)
                    dve.wait_ge(silu_ready, n_v + i + 1)
                    tt(tmp[2][:, 0:S], tmp[5][:, 0:S], tmp[3][:, 0:S], ALU.mult).then_inc(uv_ready, 1)
                    dve.wait_ge(u_hi_ready, 2 * FF1_H + n_v + i + 1)
                    tt(u_lo[:, i, :], tmp[2][:, 0:S], u_hi[:, i, :].bitcast(F32), ALU.subtract).then_inc(u_ready, 1)
                run_pairs(dve, f"FU{hx}", FF2_H, body, link=link, per=5)
                n_v += FF2_H
                join_x(f"FD{hx}", 2)

            inverse_deviation()
            with dve.Fori(0, NC_D // 2) as i:
                for s in range(2):
                    c = 2 * i + s
                    stt(qy[:, c, :], x[:, c, :], pcol("norm_final_2", c), rstd, ALU.mult, ALU.mult).then_inc(x_new, 1)


def shape_constants():
    const = np.zeros((P, N_CONST), np.float32)
    const[:, C_ID:C_ID + P] = np.eye(P)
    for m in range(P):
        first = m % HD < HD // 2
        const[m + 32 if first else m - 32, C_ROT + m] = -1.0 if first else 1.0
    const[:, C_FREQ] = np.float32(10000.0) ** (-(2 * (np.arange(P) % (HD // 2))).astype(np.float32) / np.float32(HD))
    p, k = np.arange(P)[:, None], np.arange(S)[None, :]
    dist = np.concatenate([(p - k)[:, :P], p + P - k], 1)
    mask1 = np.where((dist >= 0) & (dist < 128), 0.0, NEG).astype(np.float32)
    ok = np.stack([16 * np.arange(N_CMP)[None, :] + CMP_LEN - 1 <= p + P * q for q in range(2)], 1)
    cmask = np.stack([np.where(ok, 0.0, NEG), ok], 1).astype(np.float32)
    dist = S - 1 - np.arange(512)
    n = np.maximum(dist, 1)
    large = 16 + (np.log(n / 16) / np.log(2048 / 16) * 16).astype(np.int64)
    bucket = np.where(dist < 16, np.maximum(dist, 0), np.minimum(large, 31))
    onehot = np.zeros((33, 4, 512), np.float32)
    for var, valid in enumerate([(dist >= 0) & (dist <= 128), (dist >= 0) & (dist % 4 == 0),
                                 (dist >= 0) & (dist % 16 == 0), dist >= 0]):
        onehot[bucket[valid], var, np.arange(512)[valid]] = 1.0
        onehot[32, var, ~valid] = 1.0
    return {"const": const, "mask1": mask1, "cmask": cmask, "onehot": onehot}


def kernel(**inputs):
    import concourse.bacc as bacc
    from concourse.bass_utils import run_bass_kernel_spmd

    a = {k: np.asarray(v) for k, v in inputs.items()}

    def units(w, subs=SUB):
        k, n = w.shape
        t = w.reshape(k // P, P, n // P, P).transpose(2, 0, 1, 3)
        t = t.reshape(n // P, k // P // subs, subs, P, P).transpose(0, 1, 3, 2, 4)
        return np.ascontiguousarray(t).reshape(-1, P, subs * P)

    def feature(v):
        v = v.reshape(-1, v.shape[-1] // P, P)
        return np.ascontiguousarray(v.transpose(2, 1, 0)).reshape(P, -1)

    arrays = shape_constants()
    arrays["xt"] = np.ascontiguousarray(a["x"][0].T.reshape(NC_D, P, S).transpose(1, 0, 2))
    arrays["pos"] = a["positions"][0]

    order = np.array([[8 * (2 * gp + e) + j for e in range(2)] for gp in range(2) for j in range(8)]).reshape(-1)
    q_cols = (order[:, None] * HD + np.arange(HD)[None, :]).reshape(-1)
    arrays["sinks"] = a["attn_sinks"][0][order]
    w = a["w_in"][0]
    o = np.cumsum([0, 2048, 2048, 2048, 256, 256, 2048, 2048])
    arrays["w_X"] = units(w[:, o[0]:o[1]])
    arrays["w_Q"] = np.concatenate([units(w[:, o[2]:o[3]][:, q_cols]), units(w[:, o[3]:o[4]])])
    arrays["w_Y"] = units(w[:, o[1]:o[2]])
    arrays["w_V"] = units(w[:, o[4]:o[5]])
    arrays["w_G"] = units(w[:, o[5]:o[7]])
    rg = np.stack([a["w_rg_a"][0], a["w_rg_x"][0]])
    rg = rg.reshape(2, 2, 4, 2, P, 2, P).transpose(1, 0, 4, 2, 5, 3, 6)
    arrays["w_RG"] = np.ascontiguousarray(rg).reshape(4, P, SUB * P)
    arrays["w_MR"] = units(a["w_rnn_proj"][0])
    arrays["w_MA"] = units(a["w_attn_proj"][0][q_cols])
    arrays["w_O"] = units(a["w_out"][0])
    up, down = a["w_mlp_up"][0], a["w_mlp_down"][0]
    for hx in range(2):
        arrays[f"w_UP{hx}"] = units(up[:, hx * FF1 // 2:(hx + 1) * FF1 // 2])
        arrays[f"w_DN{hx}"] = units(down[hx * FF1 // 2:(hx + 1) * FF1 // 2])

    w = a["w_in_2"][0]
    b0, c0 = 2304, 3840
    kv0 = c0 + 768
    branch = lambda i, kv: w[:, kv0 + 192 * i + HD * kv:kv0 + 192 * i + HD * (kv + 1)]
    cols = [w[:, 768 * g + 256 * part:768 * g + 256 * (part + 1)] for g in range(3) for part in range(2)]
    cols += [w[:, b0:b0 + 1024], w[:, c0:kv0]]
    cols += [branch(i, kv) for kv in range(KV_C) for i in (0, 1)]
    cols += [branch(i, kv) for kv in range(KV_C) for i in (2, 4)]
    arrays["w_P2"] = units(np.concatenate(cols, 1))
    cols = [w[:, 768 * g + 512:768 * g + 768] for g in range(3)] + [w[:, b0 + 1024:c0]]
    cols += [branch(i, kv) for i in (3, 5) for kv in range(KV_C)]
    cols += [w[:, kv0 + 1152:], np.zeros((D, P - 36), np.float32)]
    arrays["w_V2"] = units(np.concatenate(cols, 1))
    arrays["w_O2"] = units(a["w_out_2"][0])
    up, down = a["w_up_2"][0], a["w_down_2"][0]
    both = units(up).reshape(2, 2, FF2_H, P, SUB * P)
    for hx in range(2):
        arrays[f"w_FU{hx}"] = np.ascontiguousarray(both[:, hx].transpose(1, 0, 2, 3)).reshape(-1, P, SUB * P)
        arrays[f"w_FD{hx}"] = units(down[hx * FF2 // 2:(hx + 1) * FF2 // 2], DN2_SUB)
    arrays["cw1"] = np.ascontiguousarray(a["cmp_w1_2"][0].reshape(2, CMP_LEN, HD, P).transpose(0, 2, 1, 3)).reshape(P, CMP_LEN, P)
    arrays["cw2"] = np.ascontiguousarray(a["cmp_w2_2"][0].transpose(1, 0, 2))
    arrays["cpe"] = np.ascontiguousarray(a["cmp_pe_2"][0].transpose(0, 2, 1)).reshape(P, CMP_LEN)
    arrays["table"] = np.ascontiguousarray(a["rel_table_2"].T)
    named = {k: a[k] for k in ("norm_mix_pre", "conv_w", "conv_b", "b_rg_a", "b_rg_x", "lru_lambda", "norm_mix_post",
                               "norm_mlp_pre", "norm_mlp_post")}
    named |= {k: a[k] for k in ("norm_attn_2", "norm_mlp_2", "norm_final_2", "conv_w_2", "conv_b_2")}
    arrays["par"] = np.concatenate([feature(named[k]) for k in PARAM_COLS], 1)

    nc = bacc.Bacc("TRN2", target_bir_lowering=False, num_devices=1)
    dram = {k: nc.dram_tensor(f"in_{k}", v.shape, mybir.dt.from_np(v.dtype), kind="ExternalInput").ap()
            for k, v in arrays.items()}
    dram["out"] = nc.dram_tensor("out", (P, NC_D, S), F32, kind="ExternalOutput").ap()
    program(nc, dram)
    r = run_bass_kernel_spmd(nc, [{f"in_{k}": v for k, v in arrays.items()}], core_ids=[0])
    out = np.asarray(r.results[0]["out"])
    return np.ascontiguousarray(out.transpose(2, 1, 0).reshape(1, S, D))
```

```python
from contextlib import ExitStack

import concourse.bass as bass
import numpy as np
from concourse import mybir

F32 = mybir.dt.float32
F32R = mybir.dt.float32r
I32 = mybir.dt.int32
ALU = mybir.AluOpType
ACT = mybir.ActivationFunctionType
AX = mybir.AxisListType

P = 128
S = 256
D = 2048
NC_D = D // P
EPS = 1e-6
HD = 64
QS = HD ** -0.5
NEG = -1e30
SUB = 16
HALF = SUB // 2
FF1, FF2 = 8192, 5632
FF1_H = FF1 // P // 2
FF2_H = FF2 // P // 2
DN2_SUB = FF2_H // 2
SC = 384
JOB_C, JOB_A, JOB_B = 0, 12, 16
N_CMP = S // 16 - 1
CMP_LEN = 32
KV_C = 3

STREAM = [("X", 16, 16), ("RG", 4, 16), ("Q", 18, 16), ("Y", 16, 16), ("V", 2, 16), ("G", 32, 16),
          ("MR", 16, 16), ("MA", 16, 16), ("O", 16, 16),
          ("UP0", 32, 16), ("DN0", 32, 16), ("UP1", 32, 16), ("DN1", 32, 16),
          ("C2", 12, 16), ("VC", 4, 16), ("A2", 12, 16), ("B2", 8, 16), ("VAB", 10, 16), ("O2", 16, 16),
          ("FU0", 44, 16), ("FD0", 32, DN2_SUB), ("FU1", 44, 16), ("FD1", 32, DN2_SUB)]
U0, N_UNITS, T0 = {}, 0, {}
_t = 0
for _name, _n, _ in STREAM:
    U0[_name], T0[_name] = N_UNITS, _t
    N_UNITS += _n
    _t += {"RG": 0}.get(_name, _n // 2 if _name[:2] in ("DN", "FD") else _n)

PARAM_COLS = {}
N_PARAM = 0
for _name, _n in [("norm_mix_pre", 16), ("conv_w", 64), ("conv_b", 16), ("b_rg_a", 16), ("b_rg_x", 16),
                  ("lru_lambda", 16), ("norm_mix_post", 16), ("norm_mlp_pre", 16), ("norm_mlp_post", 16),
                  ("norm_attn_2", 16), ("norm_mlp_2", 16), ("norm_final_2", 16), ("conv_w_2", 264),
                  ("conv_b_2", 88)]:
    PARAM_COLS[_name] = N_PARAM
    N_PARAM += _n

C_ID, C_ROT, C_FREQ, N_CONST = 0, 128, 256, 257


class Link:

    def __init__(self, eng, sem):
        self.eng, self.sem, self.base, self.i, self.per, self.k = eng, sem, 0, 0, 0, 0

    def begin(self, i, per):
        self.i, self.per, self.k = i, per, 0

    def end(self, trips):
        assert self.k == self.per, f"{self.k} links in the loop"
        self.base, self.i, self.per, self.k = self.base + trips * self.per, 0, 0, 0

    def flush(self):
        self.base, self.k = self.base + self.k, 0

    def __call__(self, ins):
        self.k += 1
        ins.then_inc(self.sem, 1)
        self.eng.wait_ge(self.sem, self.base + self.i * self.per + self.k)


def split_sizes(n):
    return (n // 2 + n % 2, n // 2)


def windows(t, part, n_part, col, dims):
    a = t[part:part + n_part, col:col + 1]
    return bass.AP(a.tensor, a.offset, [list(a.ap[0])] + [list(d) for d in dims])


def program(nc, dram):
    with ExitStack() as ctx:
        top = [(nc.sbuf_base + 31) // 32 * 32]

        def place(name, shape, dtype=F32, at=None):
            size = int(np.prod(shape[1:])) * 4
            off = top[0] if at is None else at
            if at is None:
                top[0] += (size + 31) // 32 * 32
            return nc.alloc_sbuf_tensor_at(name, shape, dtype, offset=off)

        def region(size):
            off = top[0]
            top[0] += size
            assert top[0] <= nc.sbuf_usable_end, top[0]
            return off

        KB = 1024
        w_raw = place("w_raw", [P, 2, SUB * P])
        w_hi = place("w_hi", [P, 4, HALF * P], F32R)
        w_lo = place("w_lo", [P, 4, HALF * P], F32R)
        x = place("x", [P, NC_D, S])
        h_hi = place("h_hi", [P, NC_D, S], F32R)
        h_lo = place("h_lo", [P, NC_D, S], F32R)
        reg_c = region(16 * KB)
        qy = place("qy", [P, NC_D, S], at=reg_c)
        cw1 = place("cw1", [P, CMP_LEN, P], at=reg_c)
        oc_hi = place("oc_hi", [P, 6, S], F32R, at=reg_c)
        oc_lo = place("oc_lo", [P, 6, S], F32R, at=reg_c + 6 * KB)
        reg_d = region(64 * KB)
        d_hi = place("d_hi", [P, NC_D, S], F32R, at=reg_d)
        d_lo = place("d_lo", [P, NC_D, S], F32R, at=reg_d + 16 * KB)
        a_lru = place("a_lru", [P, NC_D, S], at=reg_d + 16 * KB)
        gates = place("gates", [P, 2 * NC_D, S], at=reg_d + 32 * KB)
        u_hi = place("u_hi", [P, FF1_H, S], F32R, at=reg_d)
        u_lo = place("u_lo", [P, FF1_H, S], F32R, at=reg_d + 32 * KB)
        qk2 = place("qk2", [P, 29, S], at=reg_d)
        ks2 = place("ks2", [P, 2, KV_C, S], at=reg_d + 29 * KB)
        v2 = place("v2", [P, 2, 14 * P], at=reg_d + 35 * KB)
        spare = [reg_d + 49 * KB]

        def in_spare(name, shape, dtype=F32):
            t = place(name, shape, dtype, at=spare[0])
            spare[0] += (int(np.prod(shape[1:])) * 4 + 31) // 32 * 32
            assert spare[0] <= reg_d + 64 * KB
            return t

        q2s = in_spare("q2s", [P, 3, S])
        v2s = in_spare("v2s", [P, 2, 3, 2, HD])
        pt2 = in_spare("pt2", [P, 3, SC])
        hid = in_spare("hid", [P, 2, KV_C * N_CMP])
        kc = in_spare("kc", [P, KV_C * N_CMP])
        vc = in_spare("vc", [N_CMP, KV_C, HD])
        vcs = in_spare("vcs", [N_CMP, HD])
        cw2 = in_spare("cw2", [P, 2, HD])
        gate2 = in_spare("gate2", [P, 2, 36])
        ptc = in_spare("ptc", [N_CMP, S])
        cpe = in_spare("cpe", [P, CMP_LEN])
        reg_e = region(16 * KB)
        xr = place("xr", [P, NC_D, S], at=reg_e)
        vv = place("vv", [P, 2, S], at=reg_e)
        mask1 = place("mask1", [P, SC], at=reg_e + 2 * KB)
        sb1 = place("sb1", [P, 2, SC], at=reg_e + 4 * KB)
        pt1 = place("pt1", [P, 2, SC], at=reg_e + 7 * KB)
        q1s = place("q1s", [P, S], at=reg_e + 10 * KB)
        kpe = place("kpe", [P, KV_C, N_CMP, CMP_LEN], at=reg_e)
        sb2 = place("sb2", [P, 2, 3, SC], at=reg_e)
        bias_a = place("bias_a", [P, 3, SC], at=reg_e + 9 * KB + 256)
        sbc = place("sbc", [P, 2, 2, N_CMP], at=reg_e + 14 * KB)
        cmask = place("cmask", [P, 2, 2, N_CMP], at=reg_e + 14 * KB + 256)
        reg_k = region(5 * KB)
        kt = place("kt", [P, 2, S], at=reg_k)
        sq_sum = place("sq_sum", [P, S], at=reg_k)
        cos = place("cos", [P, S], at=reg_k + 2 * KB)
        sin = place("sin", [P, S], at=reg_k + 3 * KB)
        is_reset = place("is_reset", [P, S], at=reg_k + 4 * KB)
        bias_b = place("bias_b", [P, 3, SC], at=reg_k)
        par = place("par", [P, N_PARAM])
        const = place("const", [P, N_CONST])
        ones = place("ones", [P, P])
        tmp = [place(f"tmp{j}", [P, 264]) for j in range(6)]
        k2s, kcs = tmp[0:3], tmp[3]
        sinks = place("sinks", [P, 32])
        sp8 = place("sp8", [P, 2, NC_D])
        eps = place("eps", [P, 1])
        small = place("small", [P, 64])
        assert top[0] <= nc.sbuf_usable_end, (top[0], nc.sbuf_usable_end)
        ident = const[:, C_ID:C_ID + P]
        rot_t = const[:, C_ROT:C_ROT + P]
        pos_i = place("pos_i", [P, S], I32, at=reg_e)
        pos = place("pos", [P, S], at=reg_e + KB)
        ang = place("ang", [P, 4, S], at=reg_e + 2 * KB)
        onehot = place("onehot", [33, 4, 512], at=reg_d + 32 * KB)
        table = place("table", [33, 32], at=reg_d + 40 * KB)
        rows = place("rows", [32, 4, 512], at=reg_d + 41 * KB)
        lam = place("lam", [P, 8, NC_D], at=reg_e + 8 * KB)

        bias_rows = nc.dram_tensor("bias_rows", (32, P, 512), F32, kind="Internal").ap()

        PS = ctx.enter_context(nc.psum_tensor("PS", [P, 8, 512], F32))

        def sem(name):
            return ctx.enter_context(nc.semaphore(name))

        def pcol(name, c, width=1):
            return par[:, bass.ds(PARAM_COLS[name] + c, width)]
        small_landed = sem("small_landed")
        x_landed = [sem(f"x_landed{k}") for k in range(4)]
        late_landed = sem("late_landed")
        w_landed = [sem(f"w_landed{s}") for s in range(2)]
        hi_ready = sem("hi_ready")
        lo_ready = sem("lo_ready")
        half_done = sem("half_done")
        acc_free = sem("acc_free")
        sq_ready = sem("sq_ready")
        ss_step = sem("ss_step")
        sums_ready = sem("sums_ready")
        std_ready = sem("std_ready")
        hv_ready = sem("hv_ready")
        h_hi_ready = sem("h_hi_ready")
        h_ready = sem("h_ready")
        branch_scaled = sem("branch_scaled")
        x_new = sem("x_new")
        rows_mm = sem("rows_mm")
        rows_ready = sem("rows_ready")
        bias_stored = sem("bias_stored")
        ang_ready = sem("ang_ready")
        rope_tab = sem("rope_tab")
        lam_exp_in = sem("lam_exp_in")
        lam_exp = sem("lam_exp")
        sp_ready = sem("sp_ready")
        setup_done = sem("setup_done")
        xr_ready = sem("xr_ready")
        xr_hi = sem("xr_hi")
        xr_lo = sem("xr_lo")
        rg_evac = sem("rg_evac")
        lru_act = sem("lru_act")
        lru_pre = sem("lru_pre")
        lru_mult = sem("lru_mult")
        rot_ready = sem("rot_ready")
        rope_done = sem("rope_done")
        yr_ready = sem("yr_ready")
        y_hi = sem("y_hi")
        y_lo = sem("y_lo")
        mask1_landed = sem("mask1_landed")
        q1_staged = sem("q1_staged")
        s1_ready = sem("s1_ready")
        s1_read = sem("s1_read")
        ng1_ready = sem("ng1_ready")
        e1_ready = sem("e1_ready")
        p1_ready = sem("p1_ready")
        t1_ready = sem("t1_ready")
        pt1_ready = sem("pt1_ready")
        o1_ready = sem("o1_ready")
        o1_free = sem("o1_free")
        sg_ready = sem("sg_ready")
        ya_hi = sem("ya_hi")
        ya_lo = sem("ya_lo")
        mix_ready = sem("mix_ready")
        mix_hi = sem("mix_hi")
        mix_lo = sem("mix_lo")
        relu_ready = sem("relu_ready")
        u_hi_ready = sem("u_hi_ready")
        u_ready = sem("u_ready")
        pad_ready = sem("pad_ready")
        av_ready = sem("av_ready")
        silu_ready = sem("silu_ready")
        uv_ready = sem("uv_ready")
        consts2_landed = sem("consts2_landed")
        gate2_ready = sem("gate2_ready")
        kpe_ready = sem("kpe_ready")
        hid_mm = sem("hid_mm")
        hid_ready = sem("hid_ready")
        kvc_mm = sem("kvc_mm")
        kvc_ready = sem("kvc_ready")
        qk2_staged = sem("qk2_staged")
        v2_staged = sem("v2_staged")
        bias_landed = [sem(f"bias_landed{e}") for e in range(2)]
        s2_ready = sem("s2_ready")
        s2_read = sem("s2_read")
        ng2_ready = sem("ng2_ready")
        e2_ready = sem("e2_ready")
        p2_ready = sem("p2_ready")
        t2_ready = sem("t2_ready")
        pt2_ready = sem("pt2_ready")
        o2_ready = sem("o2_ready")
        o2_hi = sem("o2_hi")
        o2_free = sem("o2_free")
        out_stored = sem("out_stored")
        dve_link, act_link = sem("dve_link"), sem("act_link")

        def units_done(u):
            return 4 + 2 * u + 2

        block = ctx.enter_context(nc.Block())

        @block.sync
        def _(sp):
            sp.dma_start(const[:], dram["const"]).then_inc(small_landed, 16)
            sp.dma_start(pos_i[:], dram["pos"].partition_broadcast(P)).then_inc(small_landed, 16)
            sp.dma_start(par[:], dram["par"]).then_inc(small_landed, 16)
            for k in range(4):
                sp.dma_start(x[:, 4 * k:4 * k + 4, :], dram["xt"][:, 4 * k:4 * k + 4, :]).then_inc(x_landed[k], 16)
            sp.dma_start(onehot[:], dram["onehot"]).then_inc(late_landed, 16)
            sp.dma_start(table[0:32, :], dram["table"]).then_inc(late_landed, 16)
            sp.dma_start(sinks[:], dram["sinks"].partition_broadcast(P)).then_inc(late_landed, 16)

            def load_unit(name, i, s, subs):
                sp.wait_ge(lo_ready, 2 * U0[name] + 2 + 4 * i + 2 * s)
                sp.dma_start(w_raw[:, s, 0:subs * P], dram["w_" + name][2 * i + s]).then_inc(w_landed[s], 16)

            def load(name, lo, hi, subs):
                with sp.Fori(lo, hi) as i:
                    for s in range(2):
                        load_unit(name, i, s, subs)

            def load_bias(buf, e, slot, head):
                base = bias_rows[head]
                for blk, (c0, n) in enumerate([(0, P), (P, S)]):
                    src = bass.AP(base.tensor, base.offset + (S - 1 - P * blk), [[511, P], [1, n]])
                    sp.dma_start(buf[:, slot, c0:c0 + n], src).then_inc(bias_landed[e], 16)

            bias_buf = [bias_a, bias_b]

            def load_biases(job0, head0, slots, t, e):
                sp.wait_ge(s2_read, job0 + 2 * t + e + 1)
                for g in range(slots):
                    load_bias(bias_buf[e], e, g, head0 + 4 * g + 2 * t + e)

            for name, n, subs in STREAM:
                if name == "A2":
                    sp.wait_ge(bias_stored, 64)
                    sp.wait_ge(std_ready, 5)
                    with sp.Fori(0, n // 2) as i:
                        for e in range(2):
                            load_unit(name, i, e, subs)
                            load_biases(JOB_C, 20, 1, i, e)
                else:
                    load(name, 0, 1 if name == "O2" else n // 2, subs)
                if name == "O2":
                    with sp.Fori(0, 2) as t:
                        for e in range(2):
                            load_biases(JOB_A, 0, 3, t, e)
                    with sp.Fori(0, 4) as t:
                        for e in range(2):
                            load_biases(JOB_B, 12, 1, t, e)
                    load(name, 1, n // 2, subs)
            sp.wait_ge(x_new, 48)
            sp.dma_start(dram["out"], qy[:]).then_inc(out_stored, 16)
            sp.wait_ge(out_stored, 16)

        @block.gpsimd
        def _(pool):
            pool.sem_inc(ss_step, 2)

            def add_squares(norm):
                n = NC_D * norm
                if norm:
                    pool.wait_ge(sums_ready, norm)
                pool.wait_ge(sq_ready, n + 1)
                pool.tensor_copy(sq_sum[:], tmp[0][:, 0:S]).then_inc(ss_step, 1)

                def add(c, s):
                    pool.wait_ge(sq_ready, n + c + 1)
                    pool.wait_ge(ss_step, 2 + n + c)
                    pool.tensor_tensor(sq_sum[:], sq_sum[:], tmp[s][:, 0:S], ALU.add).then_inc(ss_step, 1)

                add(1, 1)
                with pool.Fori(1, NC_D // 2) as i:
                    for s in range(2):
                        add(2 * i + s, s)

            add_squares(0)
            pool.wait_ge(rows_ready, 1)
            for var, (h0, h1) in enumerate([(0, 4), (4, 8), (8, 12), (12, 32)]):
                src = rows[h0:h1, var, :]
                rep = bass.AP(src.tensor, src.offset, [list(src.ap[0]), [0, P], [1, 512]])
                pool.dma_start(bias_rows[h0:h1], rep).then_inc(bias_stored, 16)

            pool.wait_ge(yr_ready, 2 + NC_D)
            pool.dma_start(mask1[:], dram["mask1"]).then_inc(mask1_landed, 16)
            pool.wait_ge(rope_done, 2 + 18)
            pool.tensor_copy(q1s[:], qy[:, 0, :]).then_inc(q1_staged, 1)
            with pool.Fori(1, NC_D) as t:
                pool.wait_ge(s1_ready, 2 * t)
                pool.tensor_copy(q1s[:], qy[:, t, :]).then_inc(q1_staged, 1)

            for norm in range(1, 5):
                add_squares(norm)

            pool.wait_ge(std_ready, 4)
            pool.wait_ge(x_new, 32)
            pool.dma_start(cw1[:], dram["cw1"]).then_inc(consts2_landed, 16)
            pool.wait_ge(half_done, units_done(U0["C2"]))
            pool.dma_start(cw2[:], dram["cw2"]).then_inc(consts2_landed, 16)
            pool.dma_start(cpe[:], dram["cpe"]).then_inc(consts2_landed, 16)
            pool.dma_start(cmask[:], dram["cmask"]).then_inc(consts2_landed, 16)

            with pool.Fori(0, KV_C) as kv:
                for uu in range(2):
                    job = JOB_C + 4 * kv + 2 * uu
                    pool.wait_ge(kvc_ready, 1)
                    pool.wait_ge(s2_ready, 2 + job)
                    last = pool.tensor_copy(q2s[:, 0, :], qk2[:, 20 + 2 * kv + uu, :])
                    if uu == 0:
                        pool.tensor_copy(kcs[:, 0:N_CMP], kc[:, bass.ds(kv * N_CMP, N_CMP)])
                        for br in range(2):
                            last = pool.tensor_copy(k2s[br][:, 0:S], ks2[:, br, kv, :])
                    last.then_inc(qk2_staged, 1)
                    if uu == 0:
                        pool.wait_ge(o2_ready, 2 + job)
                        pool.tensor_copy(vcs[:], vc[:, kv, :])
                        for br in range(2):
                            last = pool.tensor_copy(v2s[:, 0, br], v2[:, :, bass.ds(1280 + br * 192 + kv * HD, HD)])
                        last.then_inc(v2_staged, 4)
            with pool.Fori(0, 2) as t:
                for e in range(2):
                    job = JOB_A + 2 * t + e
                    if e == 0:
                        pool.wait_ge(s2_ready, 2 + job)
                        pool.wait_ge(acc_free, 2 + T0["O2"])
                        for g in range(3):
                            pool.tensor_copy(q2s[:, g, :], qk2[:, 4 * g + t, :])
                            last = pool.tensor_copy(k2s[g][:, 0:S], qk2[:, 4 * g + 2 + t, :])
                        last.then_inc(qk2_staged, 1)
                    pool.wait_ge(o2_ready, job + 1)
                    pool.wait_ge(acc_free, 2 + T0["O2"])
                    for g in range(3):
                        last = pool.tensor_copy(v2s[:, e, g], v2[:, :, bass.ds(g * 256 + (2 * t + e) * HD, HD)])
                    last.then_inc(v2_staged, 1)
            with pool.Fori(0, 4) as t:
                for e in range(2):
                    job = JOB_B + 2 * t + e
                    if e == 0:
                        pool.wait_ge(acc_free, 2 + T0["O2"])
                        pool.wait_ge(s2_ready, 2 + job)
                        pool.tensor_copy(q2s[:, 0, :], qk2[:, 12 + t, :])
                        pool.tensor_copy(k2s[0][:, 0:S], qk2[:, 16 + t, :]).then_inc(qk2_staged, 1)
                    pool.wait_ge(acc_free, 2 + T0["O2"])
                    pool.wait_ge(o2_ready, job + 1)
                    pool.tensor_copy(v2s[:, e, 0], v2[:, :, bass.ds(768 + (2 * t + e) * HD, HD)]).then_inc(v2_staged, 1)
            for norm in range(5, 7):
                add_squares(norm)

        @block.tensor
        def _(pe):
            pe.sem_inc(half_done, 4)
            pe.sem_inc(t1_ready, 2)
            pe.sem_inc(o1_ready, 2)
            pe.sem_inc(o2_ready, 2)
            pe.sem_inc(s2_ready, 2)
            pe.wait_ge(small_landed, 48)
            pe.wait_ge(setup_done, 1)

            def half_unit(u, s, hf, n, acc, rhs, k0, start, stop, ready=None):
                pe.wait_ge(lo_ready, 4 + 2 * u + hf + 1)
                for k in range(n):
                    if ready:
                        pe.wait_ge(ready[0], ready[1] + k0 + k + 1)
                    w0, w1 = (w[:, 2 * s + hf, k * P:(k + 1) * P] for w in (w_hi, w_lo))
                    r0, r1 = rhs(k0 + k) if callable(rhs) else (r[:, k0 + k, :] for r in rhs)
                    pe.matmul(acc, w0, r0, start=start and k == 0, stop=False)
                    pe.matmul(acc, w0, r1, start=False, stop=False)
                    mm = pe.matmul(acc, w1, r0, start=False, stop=stop and k == n - 1)
                mm.then_inc(half_done, 1)

            def product(name, n, rhs, mid=None, peel=False, subs=SUB, ready=None):
                n0, n1 = split_sizes(subs)

                def pair(i):
                    for s in range(2):
                        u = U0[name] + 2 * i + s
                        pe.wait_ge(acc_free, T0[name] + 2 * i + s + 1)
                        acc = PS[:, s, 0:S]
                        follow = ready if isinstance(i, int) and s == 0 else None
                        half_unit(u, s, 0, n0, acc, rhs, 0, True, False, follow)
                        if mid is not None:
                            mid(i, s)
                        half_unit(u, s, 1, n1, acc, rhs, n0, False, True, follow)

                if peel or ready:
                    pair(0)
                with pe.Fori(1 if peel or ready else 0, n // 2) as i:
                    pair(i)

            def product2(name, n, rhs, ready, subs=SUB):
                n0, n1 = split_sizes(subs)

                def pair(i):
                    for s in range(2):
                        pe.wait_ge(acc_free, T0[name] + 2 * i + s + 1)
                        for part in range(2):
                            u = U0[name] + 4 * i + 2 * s + part
                            acc = PS[:, s, 0:S]
                            follow = ready if isinstance(i, int) and s == 0 else None
                            half_unit(u, part, 0, n0, acc, rhs, part * subs, part == 0, False, follow)
                            half_unit(u, part, 1, n1, acc, rhs, part * subs + n0, False, part == 1, follow)

                pair(0)
                with pe.Fori(1, n // 2) as i:
                    pair(i)

            def pair_v(name, i, first, odd):
                if first:
                    pe.wait_ge(acc_free, T0[name] + 2)
                else:
                    pe.wait_ge(acc_free, T0[name] + 2 * i)
                for s in range(2):
                    for hf in range(2):
                        pe.wait_ge(lo_ready, 4 + 2 * (U0[name] + 2 * i + s) + hf + 1)
                        for k in range(HALF // 2):
                            w0, w1 = (w[:, 2 * s + hf, k * S:(k + 1) * S] for w in (w_hi, w_lo))
                            c = HALF * s + HALF // 2 * hf + k
                            for th in range(2):
                                acc = PS[:, 2 * odd + th, 0:S]
                                a0, a1 = (a[:, c, th * P:(th + 1) * P] for a in (h_hi, h_lo))
                                pe.matmul(acc, a0, w0, start=c == 0, stop=False)
                                pe.matmul(acc, a0, w1, start=False, stop=False)
                                mm = pe.matmul(acc, a1, w0, start=False, stop=c == NC_D - 1)
                        mm.then_inc(half_done, 1)

            def sum_features(norm):
                pe.wait_ge(ss_step, 2 + NC_D * (norm + 1))
                if norm:
                    pe.wait_ge(std_ready, norm)
                pe.matmul(PS[:, 7, 0:S], ones[:], sq_sum[:], start=True, stop=True).then_inc(sums_ready, 1)

            sum_features(0)
            pe.wait_ge(late_landed, 48)
            for var in range(4):
                mm = pe.matmul(PS[0:32, 2 + var, :], table[:], onehot[:, var, :], start=True, stop=True)
            mm.then_inc(rows_mm, 1)

            product("X", 16, (h_hi, h_lo), ready=(h_ready, 4))
            pe.wait_ge(rows_ready, 1)

            pe.wait_ge(xr_lo, NC_D)
            pe.wait_ge(acc_free, 2 + T0["Q"])
            with pe.Fori(0, 2) as bh:
                for hx in range(4):
                    s, hf = hx // 2, hx % 2
                    u = U0["RG"] + 2 * bh + s
                    pe.wait_ge(lo_ready, 4 + 2 * u + hf + 1)
                    pe.wait_ge(rg_evac, 4 * bh + hx + 1)
                    for b in range(2):
                        for m in range(2):
                            acc = PS[:, 2 * hf + b, m * S:(m + 1) * S]
                            for kk in range(2):
                                sub = (b * 2 + m) * 2 + kk
                                w0, w1 = (w[:, 2 * s + hf, sub * P:(sub + 1) * P] for w in (w_hi, w_lo))
                                r0, r1 = (r[:, 8 * bh + 4 * hf + 2 * b + kk, :] for r in (d_hi, d_lo))
                                pe.matmul(acc, w0, r0, start=kk == 0, stop=False)
                                pe.matmul(acc, w0, r1, start=False, stop=False)
                                mm = pe.matmul(acc, w1, r0, start=False, stop=kk == 1)
                    mm.then_inc(half_done, 1)

            pe.wait_ge(rg_evac, 2 + 8)

            def rotate(c, s):
                pe.wait_ge(acc_free, 2 + T0["Q"] + c + 1)
                pe.wait_ge(rope_done, c + 1)
                pe.matmul(PS[:, 6 + s, 0:S], rot_t, tmp[s][:, 0:S], start=True, stop=True).then_inc(rot_ready, 1)

            def rotate_mid(i, s):
                if not (isinstance(i, int) and s == 0):
                    rotate(2 * i + s - 1, 1 - s)

            product("Q", 18, (h_hi, h_lo), mid=rotate_mid, peel=True)
            rotate(17, 1)
            product("Y", 16, (h_hi, h_lo))
            pair_v("V", 0, True, 0)

            pe.wait_ge(acc_free, 2 + T0["G"])
            pe.wait_ge(rope_done, 2 + 18)

            def scores1(hd, gp, e, tile):
                if e == 0:
                    pe.wait_ge(q1_staged, tile + 1)
                pe.wait_ge(s1_read, hd + 1)
                lo, up = HD * e, HD * e + HD
                pe.matmul(PS[:, 2 + e, 0:P], q1s[lo:up, 0:P], kt[lo:up, gp, 0:P], start=True, stop=True)
                pe.matmul(PS[:, 2 + e, P:SC], q1s[lo:up, P:S], kt[lo:up, gp, :], start=True, stop=True)\
                    .then_inc(s1_ready, 1)

            def turn1(hd, e):
                pe.wait_ge(p1_ready, hd + 1)
                pe.wait_ge(pt1_ready, hd + 1)
                for b in range(3):
                    mm = pe.transpose(PS[:, 4 + e, b * P:(b + 1) * P], sb1[:, e, b * P:(b + 1) * P], ident)
                mm.then_inc(t1_ready, 1)

            def pv1(hd, gp, e, tile):
                pe.wait_ge(pt1_ready, 2 + hd + 1)
                if e == 0:
                    pe.wait_ge(o1_free, tile + 1)
                o = PS[HD * e:HD * e + HD, 6, :]
                g = 2 * gp + e
                pe.matmul(o[:, 0:S], vv[:, 0, g * HD:(g + 1) * HD], pt1[:, e, 0:S], start=True, stop=False,
                          skip_group_check=True)
                pe.matmul(o[:, P:S], vv[:, 1, g * HD:(g + 1) * HD], pt1[:, e, S:SC], start=False, stop=True,
                          skip_group_check=True).then_inc(o1_ready, 1)

            pe.wait_ge(mask1_landed, 16)
            for gp in range(2):
                def tile_units(i):
                    first = isinstance(i, int)
                    tile = 8 * gp + i
                    for e in range(2):
                        u = U0["G"] + 2 * tile + e
                        hd = 2 * tile + e
                        pe.wait_ge(acc_free, T0["G"] + 2 * tile + e + 1)
                        acc = PS[:, e, 0:S]
                        half_unit(u, e, 0, HALF, acc, (h_hi, h_lo), 0, True, False)
                        if not (first and e == 0):
                            turn1(hd - 1, 1 - e)
                        scores1(hd, gp, e, tile)
                        half_unit(u, e, 1, HALF, acc, (h_hi, h_lo), HALF, False, True)
                        if not (first and e == 0):
                            pv1(hd - 1, gp, 1 - e, tile - (1 - e))

                tile_units(0)
                with pe.Fori(1, 8) as i:
                    tile_units(i)
                turn1(16 * gp + 15, 1)
                pv1(16 * gp + 15, gp, 1, 8 * gp + 7)

            pe.wait_ge(y_lo, NC_D)
            product("MR", 16, (d_hi, d_lo))
            pe.wait_ge(ya_lo, NC_D)
            product("MA", 16, (h_hi, h_lo))
            product("O", 16, (d_hi, d_lo), ready=(mix_lo, 0))
            sum_features(1)
            sum_features(2)

            for hx in range(2):
                product(f"UP{hx}", 32, (h_hi, h_lo), ready=None if hx else (h_ready, 4 + NC_D))
                product2(f"DN{hx}", 16, (u_hi, u_lo), (u_ready, 2 + FF1_H * hx))
            sum_features(3)
            sum_features(4)

            product("C2", 12, (h_hi, h_lo), ready=(h_ready, 4 + 2 * NC_D))
            pair_v("VC", 0, True, 0)

            pe.wait_ge(consts2_landed, 64)
            pe.wait_ge(kpe_ready, KV_C)
            for br in range(2):
                lo, up = HD * br, HD * br + HD
                for j in range(CMP_LEN):
                    mm = pe.matmul(PS[:, 4 + br, 0:KV_C * N_CMP], cw1[lo:up, j, :],
                                   kpe[lo:up].rearrange("p v n j -> p (v n) j")[:, :, j],
                                   start=j == 0, stop=j == CMP_LEN - 1)
            mm.then_inc(hid_mm, 1)
            pair_v("VC", 1, False, 1)
            pe.wait_ge(hid_ready, 1)
            pe.matmul(PS[0:HD, 6, 0:KV_C * N_CMP], cw2[:, 0, :], hid[:, 0, :], start=True, stop=True)
            for kv in range(KV_C):
                mm = pe.matmul(PS[0:N_CMP, 7, kv * HD:(kv + 1) * HD], hid[:, 1, kv * N_CMP:(kv + 1) * N_CMP],
                               cw2[:, 1, :], start=True, stop=True)
            mm.then_inc(kvc_mm, 1)

            def scores2(bank, e, slot, k):
                lo, up = HD * e, HD * e + HD
                pe.matmul(PS[:, bank, 0:P], q2s[lo:up, slot, 0:P], k[:, 0:P], start=True, stop=True)
                return pe.matmul(PS[:, bank, P:SC], q2s[lo:up, slot, P:S], k, start=True, stop=True)

            def turn2(bank, e, slot):
                for b in range(3):
                    mm = pe.transpose(PS[:, bank, b * P:(b + 1) * P], sb2[:, e, slot, b * P:(b + 1) * P], ident)
                return mm

            def pv2(o, e, slot, start, stop):
                pe.matmul(o, v2s[:, e, slot, 0, :], pt2[:, slot, 0:S], start=start, stop=False, skip_group_check=True)
                return pe.matmul(o[:, P:S], v2s[:, e, slot, 1, :], pt2[:, slot, S:SC], start=False, stop=stop,
                                 skip_group_check=True)

            TURN = [5, 6, 0]

            def scores_step(job0, t, e, scores):
                job = job0 + 2 * t + e
                if e == 0:
                    pe.wait_ge(qk2_staged, job0 // 2 + t + 1)
                pe.wait_ge(s2_read, 2 + job)
                scores(e).then_inc(s2_ready, 1)

            def turn_step(job0, t, e, turn):
                pe.wait_ge(p2_ready, job0 + 2 * t + e + 1)
                turn(e).then_inc(t2_ready, 1)

            def weigh_step(job0, t, e, weigh):
                job = job0 + 2 * t + e
                pe.wait_ge(v2_staged, job + 1)
                pe.wait_ge(pt2_ready, job + 1)
                if e == 0:
                    pe.wait_ge(o2_free, job0 // 2 + t + 1)
                weigh(e).then_inc(o2_ready, 1)

            def scores_c(e):
                lo, up = HD * e, HD * e + HD
                for qt in range(2):
                    pe.matmul(PS[:, 2, SC + qt * N_CMP:SC + (qt + 1) * N_CMP], q2s[lo:up, 0, qt * P:(qt + 1) * P],
                              kcs[lo:up, 0:N_CMP], start=True, stop=True)
                for br in range(2):
                    mm = scores2(2 + br, e, 0, k2s[br][lo:up, 0:S])
                return mm

            def turn_c(e):
                for qt in range(2):
                    pe.transpose(PS[0:N_CMP, 4, qt * P:(qt + 1) * P], sbc[:, e, qt, :], ident)
                for br in range(2):
                    mm = turn2(5 + br, e, br)
                return mm

            def weigh_c(e):
                o = PS[HD * e:HD * e + HD, 7, 0:S]
                pv2(o, 0, 0, True, False)
                pv2(o, 0, 1, False, False)
                return pe.matmul(o, vcs[:], ptc[:], start=False, stop=True, skip_group_check=True)

            pe.wait_ge(acc_free, 2 + T0["A2"])
            pe.wait_ge(kvc_ready, 1)
            scores_step(JOB_C, 0, 0, scores_c)
            scores_step(JOB_C, 0, 1, scores_c)

            def tile_c(t, more):
                for e in range(2):
                    u = U0["A2"] + 2 * t + e
                    pe.wait_ge(acc_free, T0["A2"] + 2 * t + e + 1)
                    acc = PS[:, e, 0:S]
                    half_unit(u, e, 0, HALF, acc, (h_hi, h_lo), 0, True, False)
                    turn_step(JOB_C, t, e, turn_c)
                    if more:
                        scores_step(JOB_C, t + 1, e, scores_c)
                    half_unit(u, e, 1, HALF, acc, (h_hi, h_lo), HALF, False, True)
                    weigh_step(JOB_C, t, e, weigh_c)

            with pe.Fori(0, 2 * KV_C - 1) as t:
                tile_c(t, True)
            tile_c(2 * KV_C - 1, False)

            product("B2", 8, (h_hi, h_lo))
            pair_v("VAB", 0, True, 0)
            with pe.Fori(0, 2) as j:
                pair_v("VAB", 2 * j + 1, False, 1)
                pair_v("VAB", 2 * j + 2, False, 0)

            def tiles2(tiles, job0, scores, turn, weigh):

                def tile(t, more):
                    for e in range(2):
                        turn_step(job0, t, e, turn)
                        if more:
                            scores_step(job0, t + 1, e, scores)
                        weigh_step(job0, t, e, weigh)

                scores_step(job0, 0, 0, scores)
                scores_step(job0, 0, 1, scores)
                with pe.Fori(0, tiles - 1) as t:
                    tile(t, True)
                tile(tiles - 1, False)

            def scores_a(e):
                for g in range(3):
                    mm = scores2(2 + g, e, g, k2s[g][HD * e:HD * e + HD, 0:S])
                return mm

            def turn_a(e):
                for g in range(3):
                    mm = turn2(TURN[g], e, g)
                return mm

            def weigh_a(e):
                for g in range(3):
                    mm = pv2(PS[HD * e:HD * e + HD, 7 if g < 2 else 1, (g % 2) * S:(g % 2 + 1) * S], e, g, True, True)
                return mm

            pe.wait_ge(acc_free, 2 + T0["O2"])
            tiles2(2, JOB_A, scores_a, turn_a, weigh_a)
            tiles2(4, JOB_B, lambda e: scores2(2, e, 0, k2s[0][HD * e:HD * e + HD, 0:S]), lambda e: turn2(5, e, 0),
                   lambda e: pv2(PS[HD * e:HD * e + HD, 7, 0:S], e, 0, True, True))

            pe.wait_ge(o2_free, 1 + 12)
            mixed = [(h_hi[:, c, :], h_lo[:, c, :]) for c in range(10)] + [(oc_hi[:, c, :], oc_lo[:, c, :]) for c in range(6)]
            product("O2", 16, mixed.__getitem__)
            sum_features(5)

            for hx in range(2):
                product(f"FU{hx}", 44, (h_hi, h_lo), ready=None if hx else (h_ready, 4 + 3 * NC_D))
                product2(f"FD{hx}", 16, (u_hi, u_lo), (u_ready, 2 + 2 * FF1_H + FF2_H * hx), subs=DN2_SUB)
            sum_features(6)

        names = [n for n, _, _ in STREAM]
        subs_of = {n: k for n, _, k in STREAM}
        pairs_of = {n: k // 2 for n, k, _ in STREAM}

        def next_subs(name):
            at = names.index(name) + 1
            return subs_of[names[at]] if at < len(names) else 0

        def run_pairs(eng, name, trips, body, peel=False, link=None, per=0):
            lo = 0
            odd_end = next_subs(name) != subs_of[name]

            def one(i, n):
                if link:
                    link.begin(i, per)
                body(i, n)

            if peel:
                one(0, subs_of[name])
                lo = 1
            with eng.Fori(lo, trips - 1 if odd_end else trips) as i:
                one(i, subs_of[name])
            if odd_end:
                one(trips - 1, next_subs(name))
            if link:
                link.end(trips)

        @block.scalar
        def _(act):
            link = Link(act, act_link)
            act.sem_inc(acc_free, 2)
            act.sem_inc(rg_evac, 2)
            act.sem_inc(pt1_ready, 2)
            act.wait_ge(small_landed, 48)
            act.wait_ge(setup_done, 1)

            def half_hi(pair, s, hf, subs):
                n0, n1 = split_sizes(subs)
                n, off = (n0, 0) if hf == 0 else (n1, n0)
                if hf == 0:
                    act.wait_ge(w_landed[s], 16 * pair + 16)
                act.wait_ge(half_done, 4 * pair + 2 * s + hf + 1)
                act.activation(w_hi[:, 2 * s + hf, 0:n * P], w_raw[:, s, off * P:(off + n) * P], ACT.Copy)\
                    .then_inc(hi_ready, 1)

            def unit_hi(pair, s, subs):
                if subs:
                    half_hi(pair, s, 0, subs)
                    half_hi(pair, s, 1, subs)

            def next_hi(pair, s, subs, hf=None):
                at = (pair, 1) if s == 0 else (pair + 1, 0)
                for k in (0, 1) if hf is None else (hf,):
                    if subs:
                        half_hi(*at, k, subs)

            n_sq, n_norm, n_h, n_x = [0], [0], [0], [0]

            def squares(first):
                for k in range(4 if first else 1):
                    with act.Fori(2 * k if first else 0, 2 * k + 2 if first else NC_D // 2) as i:
                        for s in range(2):
                            c = 2 * i + s
                            if not first:
                                act.wait_ge(x_new, n_x[0] + c + 1)
                            act.wait_ge(ss_step, n_sq[0] + c + 1)
                            if first:
                                act.wait_ge(x_landed[k], 16)
                            act.activation(tmp[s][:, 0:S], x[:, c, :], ACT.Square).then_inc(sq_ready, 1)
                n_sq[0] += NC_D
                n_x[0] += 0 if first else NC_D

            def deviation():
                act.wait_ge(sums_ready, n_norm[0] + 1)
                act.activation(tmp[2][:, 0:S], PS[:, 7, 0:S], ACT.Sqrt, bias=eps[:, 0:1], scale=1.0 / D)\
                    .then_inc(std_ready, 1)
                n_norm[0] += 1

            def round_h():
                with act.Fori(0, NC_D // 4) as i:
                    for s in range(4):
                        c = 4 * i + s
                        act.wait_ge(hv_ready, n_h[0] + c + 1)
                        act.activation(h_hi[:, c, :], tmp[(4, 5, 0, 1)[s]][:, 0:S], ACT.Copy).then_inc(h_hi_ready, 1)
                n_h[0] += NC_D

            act.wait_ge(lam_exp_in, 1)
            act.activation(lam[:, 2, :], lam[:, 1, :], ACT.Exp).then_inc(lam_exp, 1)
            squares(True)
            act.wait_ge(ang_ready, 1)
            act.activation(sin[:], ang[:, 2, :], ACT.Sin)
            act.activation(cos[:], ang[:, 3, :], ACT.Sin).then_inc(rope_tab, 1)
            deviation()
            unit_hi(0, 0, SUB)
            round_h()
            act.wait_ge(rows_mm, 1)
            act.activation(rows[:], PS[0:32, 2:6, :], ACT.Copy).then_inc(rows_ready, 1)

            def body(i, n):
                for s in range(2):
                    c, pair = 2 * i + s, U0["X"] // 2 + i
                    next_hi(pair, s, n)
                    act.wait_ge(half_done, units_done(U0["X"] + c))
                    act.wait_ge(xr_ready, c + 1)
                    act.activation(tmp[2 + s][:, 0:S], PS[:, s, 0:S], ACT.Identity, scale=pcol("conv_w", 4 * c + 3),
                                   bias=pcol("conv_b", c))
                    act.activation(tmp[s][:, 3:3 + S], PS[:, s, 0:S], ACT.Copy).then_inc(acc_free, 1)
                    act.wait_ge(xr_ready, 2 + c + 1)
                    act.activation(d_hi[:, c, :], xr[:, c, :], ACT.Copy).then_inc(xr_hi, 1)
            run_pairs(act, "X", 8, body)

            act.wait_ge(bias_stored, 64)
            act.preload_act_table(ACT.Sigmoid)
            with act.Fori(0, 2) as bh:
                for mat in range(2):
                    u, pair = U0["RG"] + 2 * bh + mat, U0["RG"] // 2 + bh
                    next_hi(pair, mat, SUB)
                    for hf in range(2):
                        act.wait_ge(half_done, 4 + 2 * u + hf + 1)
                        for t in range(4):
                            c = 8 * bh + 4 * hf + t
                            ins = act.activation(gates[:, 16 * mat + c, :], PS[:, 2 * hf + t // 2, t % 2 * S:(t % 2 + 1) * S],
                                                 ACT.Sigmoid, bias=pcol("b_rg_x" if mat else "b_rg_a", c))
                        ins.then_inc(rg_evac, 1)

            act.preload_act_table(ACT.Exp)
            act.wait_ge(sp_ready, 1)
            act.wait_ge(xr_lo, NC_D)

            def rope_in(c, s):
                act.wait_ge(half_done, units_done(U0["Q"] + c))
                act.wait_ge(rope_done, c + 1)
                act.activation(tmp[s][:, 0:S], PS[:, s, 0:S], ACT.Copy).then_inc(acc_free, 1)

            act.wait_ge(rg_evac, 2 + 8)
            with act.Fori(0, 8) as i:
                for s in range(2):
                    c = 2 * i + s
                    next_hi(U0["Q"] // 2 + i, s, SUB)
                    act.activation(a_lru[:, c, :], gates[:, c, :], ACT.Exp, scale=sp8[:, 1, bass.ds(c, 1)])
                    act.wait_ge(lru_pre, c + 1)
                    act.activation(tmp[4 + s][:, 0:S], gates[:, c, :], ACT.Tanh, scale=sp8[:, 0, bass.ds(c, 1)])\
                        .then_inc(lru_act, 1)
                    rope_in(c, s)
            for s in range(2):
                next_hi(U0["Q"] // 2 + 8, s, SUB)
                rope_in(16 + s, s)
            act.wait_ge(lru_pre, 2 + NC_D)
            act.activation(gates[:, 0:NC_D, :], gates[:, 0:NC_D, :], ACT.Sqrt).then_inc(lru_mult, 1)
            act.wait_ge(rope_done, 2 + 18)

            act.preload_act_table(ACT.Gelu_apprx_tanh)

            def body(i, n):
                for s in range(2):
                    c = 2 * i + s
                    next_hi(U0["Y"] // 2 + i, s, n)
                    act.wait_ge(half_done, units_done(U0["Y"] + c))
                    act.wait_ge(yr_ready, c + 1)
                    act.activation(tmp[s][:, 0:S], PS[:, s, 0:S], ACT.Gelu_apprx_tanh).then_inc(acc_free, 1)
                    act.wait_ge(yr_ready, 2 + c + 1)
                    act.activation(d_hi[:, c, :], tmp[4 + s][:, 0:S], ACT.Copy).then_inc(y_hi, 1)
            run_pairs(act, "Y", 8, body)

            next_hi(U0["V"] // 2, 0, SUB)
            next_hi(U0["V"] // 2, 1, SUB)
            act.wait_ge(half_done, units_done(U0["V"] + 1))
            for th in range(2):
                act.activation(vv[:, th, :], PS[:, th, 0:S], ACT.Copy).then_inc(acc_free, 1)

            act.preload_act_table(ACT.Exp)

            def copy_pt1(hd, e):
                act.wait_ge(t1_ready, 2 + hd + 1)
                act.wait_ge(o1_ready, hd + 1)
                act.activation(pt1[:, e, :], PS[:, 4 + e, 0:SC], ACT.Copy).then_inc(pt1_ready, 1)

            def exp1(hd, e):
                mx, ng, den, es, rd = (small[:, 10 * e + 2 * j:10 * e + 2 * j + 2] for j in range(5))
                act.wait_ge(ng1_ready, hd + 1)
                act.activation(sb1[:, e, 0:P], sb1[:, e, 0:P], ACT.Exp, bias=ng[:, 0:1], accum_out=den[:, 0:1])
                act.activation(sb1[:, e, P:SC], sb1[:, e, P:SC], ACT.Exp, bias=ng[:, 1:2], accum_out=den[:, 1:2])
                act.activation(es, ng, ACT.Exp, bias=sinks[:, bass.ds(hd, 1)]).then_inc(e1_ready, 1)

            for gp in range(2):
                def body(i):
                    first = isinstance(i, int)
                    for e in range(2):
                        hd = 16 * gp + 2 * i + e
                        pair = U0["G"] // 2 + 8 * gp + i
                        next_hi(pair, e, SUB, 0)
                        if not (first and e == 0):
                            copy_pt1(hd - 1, 1 - e)
                        next_hi(pair, e, SUB, 1)
                        exp1(hd, e)
                        act.wait_ge(half_done, units_done(U0["G"] + hd))
                        act.activation(gates[:, hd, :], PS[:, e, 0:S], ACT.Copy).then_inc(acc_free, 1)
                body(0)
                with act.Fori(1, 8) as i:
                    body(i)
                copy_pt1(16 * gp + 15, 1)

            act.preload_act_table(ACT.Sigmoid)
            act.wait_ge(o1_free, 1 + NC_D)

            def body(i, n):
                for s in range(2):
                    c = 2 * i + s
                    next_hi(U0["MR"] // 2 + i, s, n)
                    act.wait_ge(acc_free, T0["MR"] + c + 1)
                    act.activation(tmp[s][:, 0:S], gates[:, c, :], ACT.Sigmoid).then_inc(sg_ready, 1)
                    act.activation(h_hi[:, c, :], qy[:, c, :], ACT.Copy).then_inc(ya_hi, 1)
            run_pairs(act, "MR", 8, body)

            def body(i, n):
                for s in range(2):
                    c = 2 * i + s
                    next_hi(U0["MA"] // 2 + i, s, n)
                    act.wait_ge(acc_free, T0["MA"] + c + 1)
                    act.activation(tmp[s][:, 0:S], gates[:, NC_D + c, :], ACT.Sigmoid).then_inc(sg_ready, 1)
                    act.wait_ge(mix_ready, c + 1)
                    act.activation(d_hi[:, c, :], tmp[4 + s][:, 0:S], ACT.Copy).then_inc(mix_hi, 1)
            run_pairs(act, "MA", 8, body)

            act.preload_act_table(ACT.Sqrt)
            act.wait_ge(ya_lo, NC_D)

            def body(i, n):
                for s in range(2):
                    c = 2 * i + s
                    next_hi(U0["O"] // 2 + i, s, n)
                    act.wait_ge(half_done, units_done(U0["O"] + c))
                    act.wait_ge(ss_step, n_sq[0] + c + 1)
                    act.activation(tmp[s][:, 0:S], PS[:, s, 0:S], ACT.Square).then_inc(sq_ready, 1)
                    act.activation(qy[:, c, :], PS[:, s, 0:S], ACT.Copy).then_inc(acc_free, 1)
            run_pairs(act, "O", 8, body)
            n_sq[0] += NC_D
            deviation()
            squares(False)
            deviation()
            round_h()

            n_u = 0
            for hx in range(2):
                def body(i, n):
                    for s in range(2):
                        c, name = 2 * i + s, f"UP{hx}"
                        next_hi(U0[name] // 2 + i, s, n)
                        act.wait_ge(half_done, units_done(U0[name] + c))
                        act.wait_ge(u_ready, n_u + c + 1)
                        act.activation(tmp[s][:, 0:S], PS[:, s, 0:S], ACT.Relu).then_inc(acc_free, 1)
                        act.wait_ge(acc_free, 2 + T0[name] + c + 1)
                        act.activation(u_hi[:, c, :], tmp[s][:, 0:S], ACT.Square).then_inc(u_hi_ready, 1)
                run_pairs(act, f"UP{hx}", FF1_H // 2, body)
                n_u += FF1_H

                def body(i, n):
                    for s in range(2):
                        c, name = 2 * i + s, f"DN{hx}"
                        pair = U0[name] // 2 + 2 * i + s
                        next_hi(pair, 0, n)
                        next_hi(pair, 1, n)
                        if hx == 0:
                            act.wait_ge(half_done, units_done(2 * pair + 1))
                            act.activation(qy[:, c, :], PS[:, s, 0:S], ACT.Copy).then_inc(acc_free, 1)
                        else:
                            act.wait_ge(acc_free, 2 + T0[name] + c + 1)
                            act.wait_ge(ss_step, n_sq[0] + c + 1)
                            act.activation(tmp[s][:, 0:S], qy[:, c, :], ACT.Square).then_inc(sq_ready, 1)
                run_pairs(act, f"DN{hx}", 8, body)
            n_sq[0] += NC_D
            deviation()
            squares(False)
            deviation()
            round_h()

            def project(name, i, col):
                for s in range(2):
                    c = 2 * i + s
                    next_hi(U0[name] // 2 + i, s, SUB)
                    act.wait_ge(half_done, units_done(U0[name] + c))
                    act.activation(qk2[:, bass.ds(col + c, 1), :].rearrange("p a b -> p (a b)"), PS[:, s, 0:S], ACT.Copy)\
                        .then_inc(acc_free, 1)

            with act.Fori(0, 4) as i:
                project("C2", i, 20)
            for c in range(8, 12):
                s = c % 2
                next_hi(U0["C2"] // 2 + c // 2, s, SUB)
                act.wait_ge(half_done, units_done(U0["C2"] + c))
                if c == 8:
                    ins = act.activation(qk2[:, 28, :], PS[:, s, 0:S], ACT.Copy)
                else:
                    for br in range(2):
                        for half in range(2):
                            ins = act.activation(ks2[HD * half:HD * half + HD, br, c - 9, :],
                                                 PS[HD * br:HD * br + HD, s, 0:S], ACT.Copy)
                ins.then_inc(acc_free, 1)

            def values(name, i, odd, col):
                next_hi(U0[name] // 2 + i, 0, SUB)
                next_hi(U0[name] // 2 + i, 1, SUB)
                act.wait_ge(half_done, units_done(U0[name] + 2 * i + 1))
                for th in range(2):
                    act.activation(v2[:, th, bass.ds(col + i * S, S)], PS[:, 2 * odd + th, 0:S], ACT.Copy)\
                        .then_inc(acc_free, 1)
            values("VC", 0, 0, 1280)
            act.wait_ge(hid_mm, 1)
            act.activation(hid[:], PS[:, 4:6, 0:KV_C * N_CMP], ACT.Gelu_apprx_tanh).then_inc(hid_ready, 1)
            values("VC", 1, 1, 1280)
            act.wait_ge(acc_free, 2 + T0["A2"])
            act.activation(gate2[:], v2[:, :, 13 * P:13 * P + 36], ACT.Sigmoid).then_inc(gate2_ready, 1)
            act.wait_ge(kvc_mm, 1)
            act.activation(kc[0:HD], PS[0:HD, 6, 0:KV_C * N_CMP], ACT.Copy)
            act.activation(kc[HD:P], PS[0:HD, 6, 0:KV_C * N_CMP], ACT.Copy)
            act.activation(vc[:], PS[0:N_CMP, 7, 0:KV_C * HD].rearrange("p (v d) -> p v d", v=KV_C), ACT.Copy)\
                .then_inc(kvc_ready, 1)
            act.preload_act_table(ACT.Exp)

            TURN = [5, 6, 0]

            def small2(e, j, n):
                return small[:, 32 * e + j:32 * e + j + n]

            def exp2(src, ng, den):
                return act.activation(src, src, ACT.Exp, bias=ng, accum_out=den)

            def exp_rows(e, cols, j):
                for blk in range(2):
                    ins = exp2(cols(slice(0, P) if blk == 0 else slice(P, SC)), small2(e, 6 + 2 * j + blk, 1),
                               small2(e, 12 + 2 * j + blk, 1))
                return ins

            def exp_a(e):
                return exp_rows(e, lambda c: sb2[:, e, :, c], 0)

            def exp_b(e):
                return exp_rows(e, lambda c: sb2[:, e, 0, c], 0)

            def exp_c(e):
                for br in range(2):
                    exp_rows(e, lambda c: sb2[:, e, br, c], br)
                for qt in range(2):
                    ins = act.activation(sbc[:, e, qt, :], sbc[:, e, qt, :], ACT.Exp, bias=small2(e, 10 + qt, 1))
                return ins

            def copy_slots(n):
                for g in range(n):
                    ins = act.activation(pt2[:, g, :], PS[:, TURN[g], 0:SC], ACT.Copy)
                return ins

            def copy_c():
                copy_slots(2)
                return act.activation(ptc[:], PS[0:N_CMP, 4, 0:S], ACT.Copy)

            def out_hi(hi, bank, col):
                act.activation(hi, PS[:, bank, col:col + S], ACT.Copy).then_inc(o2_hi, 1)

            def exp_step(job0, t, e, exps):
                act.wait_ge(ng2_ready, job0 + 2 * t + e + 1)
                exps(e).then_inc(e2_ready, 1)

            def copy_step(job0, t, e, copies):
                act.wait_ge(t2_ready, job0 + 2 * t + e + 1)
                copies().then_inc(pt2_ready, 1)

            def out_c(t):
                act.wait_ge(o2_ready, 2 + JOB_C + 2 * t + 2)
                out_hi(oc_hi[:, t, :], 7, 0)

            def tile_c(t, more):
                for e in range(2):
                    k, pair = 2 * t + e, U0["A2"] // 2 + t
                    next_hi(pair, e, SUB, 0)
                    if e == 0 and not isinstance(t, int) or e == 0 and t:
                        out_c(t - 1)
                    next_hi(pair, e, SUB, 1)
                    copy_step(JOB_C, t, e, copy_c)
                    act.wait_ge(half_done, units_done(U0["A2"] + k))
                    act.activation(qk2[:, k, :], PS[:, e, 0:S], ACT.Copy).then_inc(acc_free, 1)
                    if more:
                        exp_step(JOB_C, t + 1, e, exp_c)

            exp_step(JOB_C, 0, 0, exp_c)
            exp_step(JOB_C, 0, 1, exp_c)
            tile_c(0, True)
            with act.Fori(1, 2 * KV_C - 1) as t:
                tile_c(t, True)
            tile_c(2 * KV_C - 1, False)
            out_c(2 * KV_C - 1)

            with act.Fori(0, 4) as i:
                project("B2", i, 12)
            values("VAB", 0, 0, 0)
            with act.Fori(0, 2) as j:
                values("VAB", 2 * j + 1, 1, 0)
                values("VAB", 2 * j + 2, 0, 0)

            def tiles2(tiles, job0, exps, copies, out):
                def tile(t, more):
                    for e in range(2):
                        if e == 0:
                            exp_step(job0, t, 1, exps)
                        elif more:
                            exp_step(job0, t + 1, 0, exps)
                        copy_step(job0, t, e, copies)
                    act.wait_ge(o2_ready, 2 + job0 + 2 * t + 2)
                    out(t)

                exp_step(job0, 0, 0, exps)
                with act.Fori(0, tiles - 1) as t:
                    tile(t, True)
                tile(tiles - 1, False)

            def out_a(t):
                for g in range(3):
                    out_hi(h_hi[:, 2 * g + t, :], 7 if g < 2 else 1, (g % 2) * S)

            tiles2(2, JOB_A, exp_a, lambda: copy_slots(3), out_a)
            tiles2(4, JOB_B, exp_b, lambda: copy_slots(1), lambda t: out_hi(h_hi[:, 6 + t, :], 7, 0))

            act.preload_act_table(ACT.Sqrt)

            def sums_of_x(name, units):
                def body(i, n):
                    for s in range(2):
                        c = 2 * i + s
                        pair = U0[name] // 2 + (i if units == 1 else 2 * i + s)
                        next_hi(pair, s if units == 1 else 0, n if units == 1 else subs_of[name])
                        if units == 2:
                            next_hi(pair, 1, n if s else subs_of[name])
                        act.wait_ge(acc_free, 2 + T0[name] + c + 1)
                        act.wait_ge(ss_step, n_sq[0] + c + 1)
                        act.activation(tmp[s][:, 0:S], x[:, c, :], ACT.Square).then_inc(sq_ready, 1)
                run_pairs(act, name, 8, body)
                n_sq[0] += NC_D

            sums_of_x("O2", 1)
            deviation()
            round_h()

            act.preload_act_table(ACT.Silu)
            n_v = 0
            for hx in range(2):
                name = f"FU{hx}"

                def silu(i):
                    act.wait_ge(av_ready, n_v + i + 1)
                    act.activation(tmp[5][:, 0:S], tmp[4][:, 0:S], ACT.Silu).then_inc(silu_ready, 1)

                def hidden_hi(i):
                    act.wait_ge(uv_ready, n_v + i + 1)
                    act.activation(u_hi[:, i, :], tmp[2][:, 0:S], ACT.Copy).then_inc(u_hi_ready, 1)

                def conv_in(i, s):
                    c = 44 * s + FF2_H * hx + i
                    act.wait_ge(half_done, units_done(U0[name] + 2 * i + s))
                    act.activation(tmp[3 + s][:, 0:S], PS[:, s, 0:S], ACT.Identity, scale=pcol("conv_w_2", 3 * c),
                                   bias=pcol("conv_b_2", c))
                    act.activation(tmp[s][:, 2:2 + S], PS[:, s, 0:S], ACT.Copy).then_inc(acc_free, 1)

                def body(i, n):
                    first = isinstance(i, int) and i == 0
                    next_hi(U0[name] // 2 + i, 0, SUB)
                    if not first:
                        silu(i - 1)
                        act.wait_ge(uv_ready, n_v + i)
                    conv_in(i, 0)
                    next_hi(U0[name] // 2 + i, 1, n)
                    if not first:
                        hidden_hi(i - 1)
                    conv_in(i, 1)
                run_pairs(act, name, FF2_H, body, peel=True)
                silu(FF2_H - 1)
                hidden_hi(FF2_H - 1)
                n_v += FF2_H
                if hx == 0:
                    def body(i, n):
                        for s in range(2):
                            pair = U0["FD0"] // 2 + 2 * i + s
                            next_hi(pair, 0, DN2_SUB)
                            next_hi(pair, 1, n if s else DN2_SUB)
                    run_pairs(act, "FD0", 8, body)
                    act.wait_ge(acc_free, 2 + T0["FU1"])
                else:
                    act.preload_act_table(ACT.Sqrt)
                    sums_of_x("FD1", 2)
            deviation()

        @block.vector
        def _(dve):
            link = Link(dve, dve_link)
            tt, ts, stt = dve.tensor_tensor, dve.tensor_scalar, dve.scalar_tensor_tensor

            dve.memset(ones[:], 1.0)
            dve.memset(eps[:], EPS)
            dve.memset(table[32:33, :], NEG)
            for credit, n in [(lo_ready, 4), (xr_ready, 2), (lru_pre, 2), (rope_done, 2), (yr_ready, 2), (s1_read, 2),
                              (o1_free, 1), (s2_read, 2), (o2_free, 1), (u_ready, 2), (h_ready, 4)]:
                dve.sem_inc(credit, n)
            link(dve.memset(tmp[0][:, 0:3], 0.0))
            dve.sem_inc(setup_done, 1)
            dve.wait_ge(small_landed, 48)

            lm = pcol("lru_lambda", 0, NC_D)
            link(ts(lam[:, 0, :], lm, -1.0, None, ALU.mult))
            tt(lam[:, 1, :], lam[:, 0, :], lm, ALU.min).then_inc(lam_exp_in, 1)

            TWO_PI = 2 * np.pi
            c1 = 6.28125
            c2 = float(np.float32(np.round((TWO_PI - c1) * 2 ** 21) / 2 ** 21))
            c3 = float(np.float32(TWO_PI - c1 - c2))
            magic = 1.5 * 2 ** 23
            edge = 3.1415925
            link(dve.tensor_copy(pos[:], pos_i[:]))
            link(ts(ang[:, 0, :], pos[:], const[:, C_FREQ:C_FREQ + 1], None, ALU.mult))
            for dst, turn in ((2, 0.0), (3, 0.25)):
                link(ts(ang[:, 1, :], ang[:, 0, :], 1 / TWO_PI, turn, ALU.mult, ALU.add))
                link(ts(ang[:, 1, :], ang[:, 1, :], magic, None, ALU.add))
                link(ts(ang[:, 1, :], ang[:, 1, :], magic, None, ALU.subtract))
                link(stt(ang[:, dst, :], ang[:, 1, :], -c1, ang[:, 0, :], ALU.mult, ALU.add))
                link(stt(ang[:, dst, :], ang[:, 1, :], -c2, ang[:, dst, :], ALU.mult, ALU.add))
                link(stt(ang[:, dst, :], ang[:, 1, :], -c3, ang[:, dst, :], ALU.mult, ALU.add))
                if turn:
                    link(ts(ang[:, dst, :], ang[:, dst, :], np.pi / 2, None, ALU.add))
                ins = ts(ang[:, dst, :], ang[:, dst, :], edge, -edge, ALU.min, ALU.max)
                if not turn:
                    link(ins)
            ins.then_inc(ang_ready, 1)
            link(ts(is_reset[:], pos[:], 0.0, None, ALU.is_equal))


            dve.wait_ge(lam_exp, 1)
            link(ts(lam[:, 3, :], lam[:, 2, :], 2.0, None, ALU.add))
            link(dve.reciprocal(lam[:, 3, :], lam[:, 3, :]))
            link(tt(lam[:, 4, :], lam[:, 2, :], lam[:, 3, :], ALU.mult))
            link(tt(lam[:, 5, :], lam[:, 4, :], lam[:, 4, :], ALU.mult))
            link(ts(lam[:, 6, :], lam[:, 5, :], 1.0 / 17, None, ALU.mult))
            for k in range(7, 0, -1):
                link(stt(lam[:, 6, :], lam[:, 6, :], 1.0 / (2 * k + 1), lam[:, 5, :], ALU.add, ALU.mult))
            link(stt(lam[:, 6, :], lam[:, 6, :], 1.0, lam[:, 4, :], ALU.add, ALU.mult))
            link(ts(lam[:, 7, :], lam[:, 0, :], 0.0, 0.5, ALU.max, ALU.mult))
            link(tt(lam[:, 6, :], lam[:, 6, :], lam[:, 7, :], ALU.add))
            ts(sp8[:, 0, :], lam[:, 6, :], 16.0, None, ALU.mult)
            ts(sp8[:, 1, :], lam[:, 6, :], -16.0, None, ALU.mult).then_inc(sp_ready, 1)
            link.flush()

            def half_lo(pair, s, hf, subs):
                n0, n1 = split_sizes(subs)
                n, off = (n0, 0) if hf == 0 else (n1, n0)
                slot = 2 * s + hf
                dve.wait_ge(hi_ready, 4 * pair + 2 * s + hf + 1)
                tt(w_lo[:, slot, 0:n * P], w_raw[:, s, off * P:(off + n) * P],
                   w_hi[:, slot, 0:n * P].bitcast(F32), ALU.subtract).then_inc(lo_ready, 1)

            def next_lo(pair, s, subs, hf=None):
                at = (pair, 1) if s == 0 else (pair + 1, 0)
                for k in (0, 1) if hf is None else (hf,):
                    if subs:
                        half_lo(*at, k, subs)

            n_norm, n_h, n_b = [0], [0], [0]
            rstd = tmp[3][:, 0:S]

            def inverse_deviation():
                n_norm[0] += 1
                dve.wait_ge(std_ready, n_norm[0])
                link(dve.reciprocal(rstd, tmp[2][:, 0:S]))
                link.flush()

            def normalise(gain):
                inverse_deviation()

                bufs = [tmp[k][:, 0:S] for k in (4, 5, 0, 1)]

                def scaled(c, s):
                    dve.wait_ge(h_ready, n_h[0] + c + 1)
                    stt(bufs[s], x[:, c, :], pcol(gain, c), rstd, ALU.mult, ALU.mult).then_inc(hv_ready, 1)

                def lo(c, s):
                    dve.wait_ge(h_hi_ready, n_h[0] + c + 1)
                    tt(h_lo[:, c, :], bufs[s], h_hi[:, c, :].bitcast(F32), ALU.subtract).then_inc(h_ready, 1)

                scaled(0, 0)
                scaled(1, 1)
                with dve.Fori(0, NC_D // 4 - 1) as i:
                    for s in range(4):
                        scaled(4 * i + s + 2, (s + 2) % 4)
                        lo(4 * i + s, s)
                for c in range(NC_D - 4, NC_D):
                    if c + 2 < NC_D:
                        scaled(c + 2, (c + 2) % 4)
                    lo(c, c % 4)
                n_h[0] += NC_D
                dve.wait_ge(h_ready, 4 + n_h[0])

            def add_branch(gain):
                inverse_deviation()

                def scaled(c):
                    stt(qy[:, c, :], qy[:, c, :], pcol(gain, c), rstd, ALU.mult, ALU.mult).then_inc(branch_scaled, 1)

                def add(c):
                    dve.wait_ge(branch_scaled, n_b[0] + c + 1)
                    tt(x[:, c, :], x[:, c, :], qy[:, c, :], ALU.add).then_inc(x_new, 1)

                scaled(0)
                scaled(1)
                with dve.Fori(0, NC_D // 2 - 1) as i:
                    for s in range(2):
                        scaled(2 * i + s + 2)
                        add(2 * i + s)
                add(NC_D - 2)
                add(NC_D - 1)
                n_b[0] += NC_D

            half_lo(0, 0, 0, SUB)
            half_lo(0, 0, 1, SUB)
            normalise("norm_mix_pre")

            link(dve.memset(tmp[0][:, 0:3], 0.0))
            link(dve.memset(tmp[1][:, 0:3], 0.0))
            link.flush()

            def body(i, n):
                for s in range(2):
                    c = 2 * i + s
                    next_lo(U0["X"] // 2 + i, s, n)
                    dve.wait_ge(acc_free, 2 + T0["X"] + c + 1)
                    pad, t2 = tmp[s], tmp[2 + s][:, 0:S]
                    w = [pcol("conv_w", 4 * c + k) for k in range(3)]
                    link(stt(t2, pad[:, 2:2 + S], w[2], t2, ALU.mult, ALU.add))
                    link(stt(t2, pad[:, 1:1 + S], w[1], t2, ALU.mult, ALU.add))
                    stt(xr[:, c, :], pad[:, 0:S], w[0], t2, ALU.mult, ALU.add).then_inc(xr_ready, 1)
                    dve.wait_ge(xr_hi, c + 1)
                    tt(d_lo[:, c, :], xr[:, c, :], d_hi[:, c, :].bitcast(F32), ALU.subtract).then_inc(xr_lo, 1)
            run_pairs(dve, "X", 8, body, link=link, per=4)

            with dve.Fori(0, 2) as bh:
                for mat in range(2):
                    next_lo(U0["RG"] // 2 + bh, mat, SUB)

            def decay(c, s):
                a, r, th = a_lru[:, c, :], gates[:, c, :], tmp[4 + s][:, 0:S]
                dve.wait_ge(lru_act, c + 1)
                link(stt(a, is_reset[:], 1.0, a, ALU.subtract, ALU.mult, reverse0=True))
                link(tt(th, th, is_reset[:], ALU.max))
                link(tt(r, a, a, ALU.mult))
                stt(r, r, 1.0, th, ALU.add, ALU.mult).then_inc(lru_pre, 1)

            def rope(c, s, out):
                dve.wait_ge(rope_done, 2 + c)
                link(tt(tmp[2][:, 0:S], tmp[s][:, 0:S], cos[:], ALU.mult))
                dve.wait_ge(rot_ready, c + 1)
                link(tt(tmp[3][:, 0:S], PS[:, 6 + s, 0:S], sin[:], ALU.mult))
                tt(out, tmp[2][:, 0:S], tmp[3][:, 0:S], ALU.add).then_inc(rope_done, 1)

            dve.wait_ge(rope_tab, 1)

            def body(i):
                for s in range(2):
                    c = 2 * i + s
                    next_lo(U0["Q"] // 2 + i, s, SUB)
                    decay(c, s)
                    if not (isinstance(i, int) and s == 0):
                        dve.wait_ge(acc_free, 2 + T0["Q"] + c)
                        rope(c - 1, 1 - s, qy[:, c - 1, :])

            link.begin(0, 5 + 3 + 2)
            body(0)
            link.k = 0
            link.flush()
            link.base += 8
            with dve.Fori(1, 8) as i:
                link.begin(i - 1, 10)
                body(i)
            link.end(7)
            next_lo(U0["Q"] // 2 + 8, 0, SUB)
            dve.wait_ge(acc_free, 2 + T0["Q"] + 16)
            rope(15, 1, qy[:, 15, :])
            next_lo(U0["Q"] // 2 + 8, 1, SUB)
            for t in range(2):
                dve.wait_ge(acc_free, 2 + T0["Q"] + 17 + t)
                rope(16 + t, t, kt[:, t, :])
            link.flush()

            dve.wait_ge(lru_mult, 1)

            def body(i, n):
                for s in range(2):
                    c = 2 * i + s
                    next_lo(U0["Y"] // 2 + i, s, n)
                    t2, t3, y = tmp[2][:, 0:S], tmp[3][:, 0:S], tmp[4 + s][:, 0:S]
                    link(tt(t2, gates[:, c, :], gates[:, NC_D + c, :], ALU.mult))
                    link(tt(t3, t2, xr[:, c, :], ALU.mult))
                    link(dve.tensor_tensor_scan(t2, a_lru[:, c, :], t3, 0.0, ALU.mult, ALU.add))
                    dve.wait_ge(acc_free, 2 + T0["Y"] + c + 1)
                    tt(y, t2, tmp[s][:, 0:S], ALU.mult).then_inc(yr_ready, 1)
                    dve.wait_ge(y_hi, c + 1)
                    tt(d_lo[:, c, :], y, d_hi[:, c, :].bitcast(F32), ALU.subtract).then_inc(y_lo, 1)
            run_pairs(dve, "Y", 8, body, link=link, per=6)

            for s in range(2):
                next_lo(U0["V"] // 2, s, SUB)

            dve.wait_ge(mask1_landed, 16)

            def soft1(hd, e):
                mx, ng = (small[:, 10 * e + 2 * j:10 * e + 2 * j + 2] for j in range(2))
                dve.wait_ge(s1_ready, hd + 1)
                dve.wait_ge(t1_ready, hd + 1)
                stt(sb1[:, e, :], PS[:, 2 + e, 0:SC], QS, mask1[:], ALU.mult, ALU.add).then_inc(s1_read, 1)
                dve.wait_ge(s1_read, 2 + hd + 1)
                dve.tensor_reduce(mx[:, 0:1], sb1[:, e, 0:P], AX.X, ALU.max)
                link(dve.tensor_reduce(mx[:, 1:2], sb1[:, e, P:SC], AX.X, ALU.max))
                ts(ng, mx, sinks[:, bass.ds(hd, 1)], -1.0, ALU.max, ALU.mult).then_inc(ng1_ready, 1)

            def norm1(hd, e):
                den, es, rd = (small[:, 10 * e + 2 * j:10 * e + 2 * j + 2] for j in range(2, 5))
                dve.wait_ge(e1_ready, hd + 1)
                link(tt(den, den, es, ALU.add))
                link(dve.reciprocal(rd, den))
                ts(sb1[:, e, 0:P], sb1[:, e, 0:P], rd[:, 0:1], None, ALU.mult)
                ts(sb1[:, e, P:SC], sb1[:, e, P:SC], rd[:, 1:2], None, ALU.mult).then_inc(p1_ready, 1)

            def out1(tile):
                dve.wait_ge(o1_ready, 2 + 2 * tile + 2)
                dve.tensor_copy(qy[:, tile, :], PS[:, 6, 0:S]).then_inc(o1_free, 1)

            for gp in range(2):
                def body(i):
                    first = isinstance(i, int)
                    for e in range(2):
                        hd = 16 * gp + 2 * i + e
                        pair = U0["G"] // 2 + 8 * gp + i
                        next_lo(pair, e, SUB, 0)
                        if e == 1 and not first:
                            out1(8 * gp + i - 1)
                        soft1(hd, e)
                        next_lo(pair, e, SUB, 1)
                        norm1(hd, e)
                link.begin(0, 6)
                body(0)
                with dve.Fori(1, 8) as i:
                    link.begin(i, 6)
                    body(i)
                link.end(8)
                out1(8 * gp + 7)

            def body(i, n):
                for s in range(2):
                    c = 2 * i + s
                    next_lo(U0["MR"] // 2 + i, s, n)
                    dve.wait_ge(ya_hi, c + 1)
                    tt(h_lo[:, c, :], qy[:, c, :], h_hi[:, c, :].bitcast(F32), ALU.subtract).then_inc(ya_lo, 1)
                    dve.wait_ge(sg_ready, c + 1)
                    dve.wait_ge(half_done, units_done(U0["MR"] + c))
                    tt(gates[:, c, :], PS[:, s, 0:S], tmp[s][:, 0:S], ALU.mult).then_inc(acc_free, 1)
            run_pairs(dve, "MR", 8, body)

            def body(i, n):
                for s in range(2):
                    c = 2 * i + s
                    next_lo(U0["MA"] // 2 + i, s, n)
                    dve.wait_ge(sg_ready, NC_D + c + 1)
                    dve.wait_ge(half_done, units_done(U0["MA"] + c))
                    tt(tmp[2][:, 0:S], PS[:, s, 0:S], tmp[s][:, 0:S], ALU.mult).then_inc(acc_free, 1)
                    dve.wait_ge(acc_free, 2 + T0["MA"] + c + 1)
                    tt(tmp[4 + s][:, 0:S], tmp[2][:, 0:S], gates[:, c, :], ALU.add).then_inc(mix_ready, 1)
                    dve.wait_ge(mix_hi, c + 1)
                    tt(d_lo[:, c, :], tmp[4 + s][:, 0:S], d_hi[:, c, :].bitcast(F32), ALU.subtract).then_inc(mix_lo, 1)
            run_pairs(dve, "MA", 8, body)

            def body(i, n):
                for s in range(2):
                    next_lo(U0["O"] // 2 + i, s, n)
            run_pairs(dve, "O", 8, body)
            add_branch("norm_mix_post")
            normalise("norm_mlp_pre")

            n_u = 0
            for hx in range(2):
                def body(i, n):
                    for s in range(2):
                        c, name = 2 * i + s, f"UP{hx}"
                        next_lo(U0[name] // 2 + i, s, n)
                        dve.wait_ge(acc_free, 2 + T0[name] + c + 1)
                        link(tt(tmp[4 + s][:, 0:S], tmp[s][:, 0:S], tmp[s][:, 0:S], ALU.mult))
                        dve.wait_ge(u_hi_ready, n_u + c + 1)
                        tt(u_lo[:, c, :], tmp[4 + s][:, 0:S], u_hi[:, c, :].bitcast(F32), ALU.subtract)\
                            .then_inc(u_ready, 1)
                run_pairs(dve, f"UP{hx}", FF1_H // 2, body, link=link, per=2)
                n_u += FF1_H

                def body(i, n):
                    for s in range(2):
                        c, name = 2 * i + s, f"DN{hx}"
                        pair = U0[name] // 2 + 2 * i + s
                        next_lo(pair, 0, n)
                        next_lo(pair, 1, n)
                        if hx:
                            dve.wait_ge(half_done, units_done(2 * pair + 1))
                            tt(qy[:, c, :], PS[:, s, 0:S], qy[:, c, :], ALU.add).then_inc(acc_free, 1)
                run_pairs(dve, f"DN{hx}", 8, body)
            add_branch("norm_mlp_post")
            normalise("norm_attn_2")

            def splits(name):
                def body(i, n):
                    for s in range(2):
                        next_lo(U0[name] // 2 + i, s, n)
                run_pairs(dve, name, pairs_of[name], body)

            splits("C2")
            dve.wait_ge(consts2_landed, 64)
            dve.wait_ge(acc_free, 2 + T0["C2"] + 9)
            for kv in range(KV_C):
                tt(kpe[:, kv], windows(qk2[:, 26 + kv, :], 0, P, 0, [[16, N_CMP], [1, CMP_LEN]]),
                   windows(cpe[:], 0, P, 0, [[0, N_CMP], [1, CMP_LEN]]), ALU.add).then_inc(kpe_ready, 1)
            splits("VC")
            dve.wait_ge(gate2_ready, 1)
            dve.wait_ge(hid_ready, 1)

            bias_buf = [bias_a, bias_b]

            def small2(e, j, n):
                return small[:, 32 * e + j:32 * e + j + n]

            def biased(bank, e, slot, bias):
                return stt(sb2[:, e, slot, :], PS[:, bank, 0:SC], QS, bias, ALU.mult, ALU.add)

            def maxima(e, cols, j, axis):
                for blk in range(2):
                    ins = dve.tensor_reduce(small2(e, 2 * j + blk, 1), cols(slice(0, P) if blk == 0 else slice(P, SC)),
                                            axis, ALU.max)
                return ins

            def times(e, cols, j):
                for blk in range(2):
                    src = cols(slice(0, P) if blk == 0 else slice(P, SC))
                    ins = ts(src, src, small2(e, 18 + 2 * j + blk, 1), None, ALU.mult)
                return ins

            def out_lo(lo, hi, bank, col):
                return tt(lo, PS[:, bank, col:col + S], hi.bitcast(F32), ALU.subtract)

            def soft(job0, t, e, landed, read, top):
                job = job0 + 2 * t + e
                dve.wait_ge(bias_landed[e], landed)
                dve.wait_ge(s2_ready, 2 + job + 1)
                read(e).then_inc(s2_read, 1)
                dve.wait_ge(s2_read, 2 + job + 1)
                n, ins = top(e)
                link(ins)
                ts(small2(e, 6, n), small2(e, 0, n), -1.0, None, ALU.mult).then_inc(ng2_ready, 1)

            def normal_step(job0, t, e, normal):
                dve.wait_ge(e2_ready, job0 + 2 * t + e + 1)
                normal(t, e).then_inc(p2_ready, 1)

            def read_c(e):
                for br in range(2):
                    biased(2 + br, e, br, bias_buf[e][:, 0, :])
                return stt(sbc[:, e], PS[:, 2, SC:SC + 2 * N_CMP].rearrange("p (q n) -> p q n", q=2), QS, cmask[:, 0],
                           ALU.mult, ALU.add)

            def top_c(e):
                for br in range(2):
                    maxima(e, lambda c: sb2[:, e, br, c], br, AX.X)
                return 6, dve.tensor_reduce(small2(e, 4, 2), sbc[:, e], AX.X, ALU.max)

            def normal_c(t, e):
                link(tt(sbc[:, e], sbc[:, e], cmask[:, 1], ALU.mult))
                link(dve.tensor_reduce(small2(e, 16, 2), sbc[:, e], AX.X, ALU.add))
                link(ts(small2(e, 16, 2), small2(e, 16, 2), 1e-30, None, ALU.max))
                link(dve.reciprocal(small2(e, 18, 6), small2(e, 12, 6)))
                for br, col in ((0, 1), (1, 2), (2, 0)):
                    coef = small2(e, 18 + 2 * br, 2)
                    ins = tt(coef, coef, gate2[:, :, bass.ds(3 * (2 * t + e) + col, 1)].rearrange("p a b -> p (a b)"), ALU.mult)
                link(ins)
                for br in range(2):
                    times(e, lambda c: sb2[:, e, br, c], br)
                for qt in range(2):
                    ins = ts(sbc[:, e, qt, :], sbc[:, e, qt, :], small2(e, 22 + qt, 1), None, ALU.mult)
                return ins

            def soft_c(t, e):
                soft(JOB_C, t, e, 32 * (t + 1), read_c, top_c)

            def out_c(t):
                dve.wait_ge(o2_hi, t + 1)
                out_lo(oc_lo[:, t, :], oc_hi[:, t, :], 7, 0).then_inc(o2_free, 1)

            def tile_c(t, more):
                for e in range(2):
                    normal_step(JOB_C, t, e, normal_c)
                    next_lo(U0["A2"] // 2 + t, e, SUB)
                    if e == 0 and not isinstance(t, int) or e == 0 and t:
                        out_c(t - 1)
                    if more:
                        soft_c(t + 1, e)

            soft_c(0, 0)
            soft_c(0, 1)
            link.flush()
            tile_c(0, True)
            link.flush()
            with dve.Fori(1, 2 * KV_C - 1) as t:
                link.begin(t - 1, 2 + 2 * 5)
                tile_c(t, True)
            link.end(2 * KV_C - 2)
            tile_c(2 * KV_C - 1, False)
            out_c(2 * KV_C - 1)
            link.flush()
            splits("B2")
            splits("VAB")

            def tiles2(tiles, job0, bias_base, bias_step, outs, read, top, normal, out):
                def soft2(t, e):
                    soft(job0, t, e, bias_base + bias_step * (t + 1), read, top)

                def tile(t, more):
                    for e in range(2):
                        if e == 0:
                            soft2(t, 1)
                        elif more:
                            soft2(t + 1, 0)
                        normal_step(job0, t, e, normal)
                    dve.wait_ge(o2_hi, outs[0] + outs[1] * (t + 1))
                    out(t).then_inc(o2_free, 1)

                soft2(0, 0)
                link.flush()
                with dve.Fori(0, tiles - 1) as t:
                    link.begin(t, 4)
                    tile(t, True)
                link.end(tiles - 1)
                tile(tiles - 1, False)
                link.flush()

            def read_a(e):
                for g in range(3):
                    ins = biased(2 + g, e, g, bias_buf[e][:, g, :])
                return ins

            def normal_a(t, e):
                link(dve.reciprocal(small2(e, 18, 2), small2(e, 12, 2)))
                return times(e, lambda c: sb2[:, e, :, c], 0)

            def out_a(t):
                for g in range(3):
                    ins = out_lo(h_lo[:, 2 * g + t, :], h_hi[:, 2 * g + t, :], 7 if g < 2 else 1, (g % 2) * S)
                return ins

            def normal_b(t, e):
                link(dve.reciprocal(small2(e, 18, 2), small2(e, 12, 2)))
                return times(e, lambda c: sb2[:, e, 0, c], 0)

            tiles2(2, JOB_A, 192, 96, (6, 3), read_a, lambda e: (2, maxima(e, lambda c: sb2[:, e, :, c], 0, AX.XY)),
                   normal_a, out_a)
            tiles2(4, JOB_B, 384, 32, (12, 1), lambda e: biased(2, e, 0, bias_buf[e][:, 0, :]),
                   lambda e: (2, maxima(e, lambda c: sb2[:, e, 0, c], 0, AX.X)), normal_b, lambda t: out_lo(h_lo[:, 6 + t, :], h_hi[:, 6 + t, :], 7, 0))

            def join_x(name, units):
                def body(i, n):
                    for s in range(2):
                        c = 2 * i + s
                        if units == 1:
                            unit = U0[name] + 2 * i + s
                            next_lo(U0[name] // 2 + i, s, n)
                        else:
                            pair = U0[name] // 2 + 2 * i + s
                            unit = 2 * pair + 1
                            next_lo(pair, 0, subs_of[name])
                            next_lo(pair, 1, n if s else subs_of[name])
                        dve.wait_ge(half_done, units_done(unit))
                        tt(x[:, c, :], PS[:, s, 0:S], x[:, c, :], ALU.add).then_inc(acc_free, 1)
                run_pairs(dve, name, 8, body)

            join_x("O2", 1)
            normalise("norm_mlp_2")

            link(dve.memset(tmp[0][:, 0:2], 0.0))
            link(dve.memset(tmp[1][:, 0:2], 0.0))
            link.flush()
            n_v = 0
            for hx in range(2):
                name = f"FU{hx}"

                def gated(i):
                    dve.wait_ge(silu_ready, n_v + i + 1)
                    tt(tmp[2][:, 0:S], tmp[5][:, 0:S], tmp[3][:, 0:S], ALU.mult).then_inc(uv_ready, 1)

                def hidden_lo(i):
                    dve.wait_ge(u_hi_ready, 2 * FF1_H + n_v + i + 1)
                    tt(u_lo[:, i, :], tmp[2][:, 0:S], u_hi[:, i, :].bitcast(F32), ALU.subtract).then_inc(u_ready, 1)

                def conv(i, s):
                    c = 44 * s + FF2_H * hx + i
                    dve.wait_ge(acc_free, 2 + T0[name] + 2 * i + s + 1)
                    v = tmp[3 + s][:, 0:S]
                    link(stt(v, tmp[s][:, 1:1 + S], pcol("conv_w_2", 3 * c + 1), v, ALU.mult, ALU.add))
                    return stt(v, tmp[s][:, 0:S], pcol("conv_w_2", 3 * c + 2), v, ALU.mult, ALU.add)

                def body(i, n):
                    first = isinstance(i, int) and i == 0
                    next_lo(U0[name] // 2 + i, 0, SUB)
                    if not first:
                        gated(i - 1)
                    conv(i, 0)
                    next_lo(U0[name] // 2 + i, 1, n)
                    if not first:
                        hidden_lo(i - 1)
                    conv(i, 1).then_inc(av_ready, 1)
                run_pairs(dve, name, FF2_H, body, peel=True, link=link, per=2)
                gated(FF2_H - 1)
                hidden_lo(FF2_H - 1)
                n_v += FF2_H
                join_x(f"FD{hx}", 2)

            inverse_deviation()
            with dve.Fori(0, NC_D // 2) as i:
                for s in range(2):
                    c = 2 * i + s
                    stt(qy[:, c, :], x[:, c, :], pcol("norm_final_2", c), rstd, ALU.mult, ALU.mult).then_inc(x_new, 1)


def shape_constants():
    const = np.zeros((P, N_CONST), np.float32)
    const[:, C_ID:C_ID + P] = np.eye(P)
    for m in range(P):
        first = m % HD < HD // 2
        const[m + 32 if first else m - 32, C_ROT + m] = -1.0 if first else 1.0
    const[:, C_FREQ] = np.float32(10000.0) ** (-(2 * (np.arange(P) % (HD // 2))).astype(np.float32) / np.float32(HD))
    p, k = np.arange(P)[:, None], np.arange(S)[None, :]
    dist = np.concatenate([(p - k)[:, :P], p + P - k], 1)
    mask1 = np.where((dist >= 0) & (dist < 128), 0.0, NEG).astype(np.float32)
    ok = np.stack([16 * np.arange(N_CMP)[None, :] + CMP_LEN - 1 <= p + P * q for q in range(2)], 1)
    cmask = np.stack([np.where(ok, 0.0, NEG), ok], 1).astype(np.float32)
    dist = S - 1 - np.arange(512)
    n = np.maximum(dist, 1)
    large = 16 + (np.log(n / 16) / np.log(2048 / 16) * 16).astype(np.int64)
    bucket = np.where(dist < 16, np.maximum(dist, 0), np.minimum(large, 31))
    onehot = np.zeros((33, 4, 512), np.float32)
    for var, valid in enumerate([(dist >= 0) & (dist <= 128), (dist >= 0) & (dist % 4 == 0),
                                 (dist >= 0) & (dist % 16 == 0), dist >= 0]):
        onehot[bucket[valid], var, np.arange(512)[valid]] = 1.0
        onehot[32, var, ~valid] = 1.0
    return {"const": const, "mask1": mask1, "cmask": cmask, "onehot": onehot}


def kernel(**inputs):
    import concourse.bacc as bacc
    from concourse.bass_utils import run_bass_kernel_spmd

    a = {k: np.asarray(v) for k, v in inputs.items()}

    def units(w, subs=SUB):
        k, n = w.shape
        t = w.reshape(k // P, P, n // P, P).transpose(2, 0, 1, 3)
        t = t.reshape(n // P, k // P // subs, subs, P, P).transpose(0, 1, 3, 2, 4)
        return np.ascontiguousarray(t).reshape(-1, P, subs * P)

    def units_v(w):
        t = w.reshape(2, HALF, P, -1, S).transpose(3, 0, 2, 1, 4)
        return np.ascontiguousarray(t).reshape(-1, P, HALF * S)

    def feature(v):
        v = v.reshape(-1, v.shape[-1] // P, P)
        return np.ascontiguousarray(v.transpose(2, 1, 0)).reshape(P, -1)

    arrays = shape_constants()
    arrays["xt"] = np.ascontiguousarray(a["x"][0].T.reshape(NC_D, P, S).transpose(1, 0, 2))
    arrays["pos"] = a["positions"][0]

    order = np.array([[8 * (2 * gp + e) + j for e in range(2)] for gp in range(2) for j in range(8)]).reshape(-1)
    q_cols = (order[:, None] * HD + np.arange(HD)[None, :]).reshape(-1)
    arrays["sinks"] = a["attn_sinks"][0][order]
    w = a["w_in"][0]
    o = np.cumsum([0, 2048, 2048, 2048, 256, 256, 2048, 2048])
    arrays["w_X"] = units(w[:, o[0]:o[1]])
    arrays["w_Q"] = np.concatenate([units(w[:, o[2]:o[3]][:, q_cols]), units(w[:, o[3]:o[4]])])
    arrays["w_Y"] = units(w[:, o[1]:o[2]])
    arrays["w_V"] = units_v(w[:, o[4]:o[5]])
    arrays["w_G"] = units(w[:, o[5]:o[7]])
    rg = np.stack([a["w_rg_a"][0], a["w_rg_x"][0]])
    rg = rg.reshape(2, 2, 4, 2, P, 2, P).transpose(1, 0, 4, 2, 5, 3, 6)
    arrays["w_RG"] = np.ascontiguousarray(rg).reshape(4, P, SUB * P)
    arrays["w_MR"] = units(a["w_rnn_proj"][0])
    arrays["w_MA"] = units(a["w_attn_proj"][0][q_cols])
    arrays["w_O"] = units(a["w_out"][0])
    up, down = a["w_mlp_up"][0], a["w_mlp_down"][0]
    for hx in range(2):
        arrays[f"w_UP{hx}"] = units(up[:, hx * FF1 // 2:(hx + 1) * FF1 // 2])
        arrays[f"w_DN{hx}"] = units(down[hx * FF1 // 2:(hx + 1) * FF1 // 2])

    w = a["w_in_2"][0]
    b0, c0 = 2304, 3840
    kv0 = c0 + 768
    branch = lambda i, kv: w[:, kv0 + 192 * i + HD * kv:kv0 + 192 * i + HD * (kv + 1)]
    cols = [w[:, c0:kv0]]
    cols += [branch(i, kv) for kv in range(KV_C) for i in (0, 1)]
    cols += [branch(i, kv) for kv in range(KV_C) for i in (2, 4)]
    arrays["w_C2"] = units(np.concatenate(cols, 1))
    cols = [branch(i, kv) for i in (3, 5) for kv in range(KV_C)]
    cols += [w[:, kv0 + 1152:], np.zeros((D, P - 36), np.float32)]
    arrays["w_VC"] = units_v(np.concatenate(cols, 1))
    cols = [w[:, 768 * g + 256 * part:768 * g + 256 * (part + 1)] for g in range(3) for part in range(2)]
    arrays["w_A2"] = units(np.concatenate(cols, 1))
    arrays["w_B2"] = units(w[:, b0:b0 + 1024])
    cols = [w[:, 768 * g + 512:768 * g + 768] for g in range(3)] + [w[:, b0 + 1024:c0]]
    arrays["w_VAB"] = units_v(np.concatenate(cols, 1))
    arrays["w_O2"] = units(a["w_out_2"][0])
    up, down = a["w_up_2"][0], a["w_down_2"][0]
    both = units(up).reshape(2, 2, FF2_H, P, SUB * P)
    for hx in range(2):
        arrays[f"w_FU{hx}"] = np.ascontiguousarray(both[:, hx].transpose(1, 0, 2, 3)).reshape(-1, P, SUB * P)
        arrays[f"w_FD{hx}"] = units(down[hx * FF2 // 2:(hx + 1) * FF2 // 2], DN2_SUB)
    arrays["cw1"] = np.ascontiguousarray(a["cmp_w1_2"][0].reshape(2, CMP_LEN, HD, P).transpose(0, 2, 1, 3)).reshape(P, CMP_LEN, P)
    arrays["cw2"] = np.ascontiguousarray(a["cmp_w2_2"][0].transpose(1, 0, 2))
    arrays["cpe"] = np.ascontiguousarray(a["cmp_pe_2"][0].transpose(0, 2, 1)).reshape(P, CMP_LEN)
    arrays["table"] = np.ascontiguousarray(a["rel_table_2"].T)
    named = {k: a[k] for k in ("norm_mix_pre", "conv_w", "conv_b", "b_rg_a", "b_rg_x", "lru_lambda", "norm_mix_post",
                               "norm_mlp_pre", "norm_mlp_post")}
    named |= {k: a[k] for k in ("norm_attn_2", "norm_mlp_2", "norm_final_2", "conv_w_2", "conv_b_2")}
    arrays["par"] = np.concatenate([feature(named[k]) for k in PARAM_COLS], 1)

    nc = bacc.Bacc("TRN2", target_bir_lowering=False, num_devices=1)
    dram = {k: nc.dram_tensor(f"in_{k}", v.shape, mybir.dt.from_np(v.dtype), kind="ExternalInput").ap()
            for k, v in arrays.items()}
    dram["out"] = nc.dram_tensor("out", (P, NC_D, S), F32, kind="ExternalOutput").ap()
    program(nc, dram)
    r = run_bass_kernel_spmd(nc, [{f"in_{k}": v for k, v in arrays.items()}], core_ids=[0])
    out = np.asarray(r.results[0]["out"])
    return np.ascontiguousarray(out.transpose(2, 1, 0).reshape(1, S, D))
```

```python
from contextlib import ExitStack

import concourse.bass as bass
import numpy as np
from concourse import mybir

F32 = mybir.dt.float32
F32R = mybir.dt.float32r
I32 = mybir.dt.int32
ALU = mybir.AluOpType
ACT = mybir.ActivationFunctionType
AX = mybir.AxisListType

P = 128
S = 256
D = 2048
NC_D = D // P
EPS = 1e-6
HD = 64
QS = HD ** -0.5
NEG = -1e30
SUB = 16
HALF = SUB // 2
SUB_O = 6
FF1, FF2 = 8192, 5632
FF1_H = FF1 // P // 2
FF2_H = FF2 // P // 2
DN2_SUB = FF2_H // 2
SC = 384
JOB_C, JOB_A, JOB_B = 0, 12, 16
N_CMP = S // 16 - 1
CMP_LEN = 32
KV_C = 3

STREAM = [("X", 16, 16), ("RG", 4, 16), ("Q", 18, 16), ("Y", 16, 16), ("V", 2, 16), ("G", 32, 16),
          ("MR", 16, 16), ("MA", 16, 16), ("O", 16, 16),
          ("UP0", 32, 16), ("DN0", 32, 16), ("UP1", 32, 16), ("DN1", 32, 16),
          ("C2", 12, 16), ("VC", 4, 16), ("B2", 8, 16), ("A2", 12, 16), ("VAB", 10, 16),
          ("OC", 16, 6), ("OA", 16, 6), ("OB", 16, 4),
          ("FU0", 44, 16), ("FD0", 32, DN2_SUB), ("FU1", 44, 16), ("FD1", 32, DN2_SUB)]
U0, N_UNITS, T0 = {}, 0, {}
_t = 0
for _name, _n, _ in STREAM:
    U0[_name], T0[_name] = N_UNITS, _t
    N_UNITS += _n
    _t += {"RG": 0}.get(_name, _n // 2 if _name[:2] in ("DN", "FD") else _n)

PARAM_COLS = {}
N_PARAM = 0
for _name, _n in [("norm_mix_pre", 16), ("conv_w", 64), ("conv_b", 16), ("b_rg_a", 16), ("b_rg_x", 16),
                  ("lru_lambda", 16), ("norm_mix_post", 16), ("norm_mlp_pre", 16), ("norm_mlp_post", 16),
                  ("norm_attn_2", 16), ("norm_mlp_2", 16), ("norm_final_2", 16), ("conv_w_2", 264),
                  ("conv_b_2", 88)]:
    PARAM_COLS[_name] = N_PARAM
    N_PARAM += _n

C_ID, C_ROT, C_FREQ, N_CONST = 0, 128, 256, 257


class Link:

    def __init__(self, eng, sem):
        self.eng, self.sem, self.base, self.i, self.per, self.k = eng, sem, 0, 0, 0, 0

    def begin(self, i, per):
        self.i, self.per, self.k = i, per, 0

    def end(self, trips):
        assert self.k == self.per, f"{self.k} links in the loop"
        self.base, self.i, self.per, self.k = self.base + trips * self.per, 0, 0, 0

    def flush(self):
        self.base, self.k = self.base + self.k, 0

    def __call__(self, ins):
        self.k += 1
        ins.then_inc(self.sem, 1)
        self.eng.wait_ge(self.sem, self.base + self.i * self.per + self.k)


def split_sizes(n):
    return (n // 2 + n % 2, n // 2)


def windows(t, part, n_part, col, dims):
    a = t[part:part + n_part, col:col + 1]
    return bass.AP(a.tensor, a.offset, [list(a.ap[0])] + [list(d) for d in dims])


def program(nc, dram):
    with ExitStack() as ctx:
        top = [(nc.sbuf_base + 31) // 32 * 32]

        def place(name, shape, dtype=F32, at=None):
            size = int(np.prod(shape[1:])) * 4
            off = top[0] if at is None else at
            if at is None:
                top[0] += (size + 31) // 32 * 32
            return nc.alloc_sbuf_tensor_at(name, shape, dtype, offset=off)

        def region(size):
            off = top[0]
            top[0] += size
            assert top[0] <= nc.sbuf_usable_end, top[0]
            return off

        KB = 1024
        w_raw = place("w_raw", [P, 2, SUB * P])
        w_hi = place("w_hi", [P, 4, HALF * P], F32R)
        w_lo = place("w_lo", [P, 4, HALF * P], F32R)
        x = place("x", [P, NC_D, S])
        h_hi = place("h_hi", [P, NC_D, S], F32R)
        h_lo = place("h_lo", [P, NC_D, S], F32R)
        reg_c = region(16 * KB)
        qy = place("qy", [P, NC_D, S], at=reg_c)
        cw1 = place("cw1", [P, CMP_LEN, P], at=reg_c)
        oc_hi = place("oc_hi", [P, 6, S], F32R, at=reg_c)
        oc_lo = place("oc_lo", [P, 6, S], F32R, at=reg_c + 6 * KB)
        reg_d = region(64 * KB)
        d_hi = place("d_hi", [P, NC_D, S], F32R, at=reg_d)
        d_lo = place("d_lo", [P, NC_D, S], F32R, at=reg_d + 16 * KB)
        a_lru = place("a_lru", [P, NC_D, S], at=reg_d + 16 * KB)
        gates = place("gates", [P, 2 * NC_D, S], at=reg_d + 32 * KB)
        u_hi = place("u_hi", [P, FF1_H, S], F32R, at=reg_d)
        u_lo = place("u_lo", [P, FF1_H, S], F32R, at=reg_d + 32 * KB)
        qk2 = place("qk2", [P, 29, S], at=reg_d)
        ks2 = place("ks2", [P, 2, KV_C, S], at=reg_d + 29 * KB)
        v2 = place("v2", [P, 2, 14 * P], at=reg_d + 35 * KB)
        spare = [reg_d + 49 * KB]

        def in_spare(name, shape, dtype=F32):
            t = place(name, shape, dtype, at=spare[0])
            spare[0] += (int(np.prod(shape[1:])) * 4 + 31) // 32 * 32
            assert spare[0] <= reg_d + 64 * KB
            return t

        q2s = in_spare("q2s", [P, 3, S])
        v2s = in_spare("v2s", [P, 2, 3, 2, HD])
        pt2 = in_spare("pt2", [P, 3, SC])
        hid = in_spare("hid", [P, 2, KV_C * N_CMP])
        kc = in_spare("kc", [P, KV_C * N_CMP])
        vc = in_spare("vc", [N_CMP, KV_C, HD])
        vcs = in_spare("vcs", [N_CMP, HD])
        cw2 = in_spare("cw2", [P, 2, HD])
        gate2 = in_spare("gate2", [P, 2, 36])
        ptc = in_spare("ptc", [N_CMP, S])
        cpe = in_spare("cpe", [P, CMP_LEN])
        reg_e = region(16 * KB)
        xr = place("xr", [P, NC_D, S], at=reg_e)
        vv = place("vv", [P, 2, S], at=reg_e)
        mask1 = place("mask1", [P, SC], at=reg_e + 2 * KB)
        sb1 = place("sb1", [P, 2, SC], at=reg_e + 4 * KB)
        pt1 = place("pt1", [P, 2, SC], at=reg_e + 7 * KB)
        q1s = place("q1s", [P, S], at=reg_e + 10 * KB)
        kpe = place("kpe", [P, KV_C, N_CMP, CMP_LEN], at=reg_e)
        sb2 = place("sb2", [P, 2, 3, SC], at=reg_e)
        bias_a = place("bias_a", [P, 3, SC], at=reg_e + 9 * KB + 256)
        sbc = place("sbc", [P, 2, 2, N_CMP], at=reg_e + 14 * KB)
        cmask = place("cmask", [P, 2, 2, N_CMP], at=reg_e + 14 * KB + 256)
        f_hi = place("f_hi", [P, NC_D, S], F32R, at=reg_e)
        f_lo = place("f_lo", [P, NC_D, S], F32R, at=reg_c)
        reg_k = region(5 * KB)
        kt = place("kt", [P, 2, S], at=reg_k)
        sq_sum = place("sq_sum", [P, S], at=reg_k)
        rstd2 = place("rstd2", [P, S], at=reg_k + 2 * KB)
        cos = place("cos", [P, S], at=reg_k + 2 * KB)
        sin = place("sin", [P, S], at=reg_k + 3 * KB)
        is_reset = place("is_reset", [P, S], at=reg_k + 4 * KB)
        bias_b = place("bias_b", [P, 3, SC], at=reg_k)
        par = place("par", [P, N_PARAM])
        const = place("const", [P, N_CONST])
        ones = place("ones", [P, P])
        tmp = [place(f"tmp{j}", [P, 264]) for j in range(6)]
        k2s, kcs = tmp[0:3], tmp[3]
        sinks = place("sinks", [P, 32])
        sp8 = place("sp8", [P, 2, NC_D])
        eps = place("eps", [P, 1])
        small = place("small", [P, 64])
        assert top[0] <= nc.sbuf_usable_end, (top[0], nc.sbuf_usable_end)
        ident = const[:, C_ID:C_ID + P]
        rot_t = const[:, C_ROT:C_ROT + P]
        pos_i = place("pos_i", [P, S], I32, at=reg_e)
        pos = place("pos", [P, S], at=reg_e + KB)
        ang = place("ang", [P, 4, S], at=reg_e + 2 * KB)
        onehot = place("onehot", [33, 4, 512], at=reg_d + 32 * KB)
        table = place("table", [33, 32], at=reg_d + 40 * KB)
        rows = place("rows", [32, 4, 512], at=reg_d + 41 * KB)
        lam = place("lam", [P, 8, NC_D], at=reg_e + 8 * KB)

        bias_rows = nc.dram_tensor("bias_rows", (32, P, 512), F32, kind="Internal").ap()

        PS = ctx.enter_context(nc.psum_tensor("PS", [P, 8, 512], F32))

        def sem(name):
            return ctx.enter_context(nc.semaphore(name))

        def pcol(name, c, width=1):
            return par[:, bass.ds(PARAM_COLS[name] + c, width)]
        small_landed = sem("small_landed")
        x_landed = [sem(f"x_landed{k}") for k in range(4)]
        late_landed = sem("late_landed")
        w_landed = [sem(f"w_landed{s}") for s in range(2)]
        hi_ready = sem("hi_ready")
        lo_ready = sem("lo_ready")
        half_done = sem("half_done")
        acc_free = sem("acc_free")
        sq_ready = sem("sq_ready")
        ss_step = sem("ss_step")
        sums_ready = sem("sums_ready")
        std_ready = sem("std_ready")
        hv_ready = sem("hv_ready")
        h_hi_ready = sem("h_hi_ready")
        h_ready = sem("h_ready")
        branch_scaled = sem("branch_scaled")
        x_new = sem("x_new")
        rows_mm = sem("rows_mm")
        rows_ready = sem("rows_ready")
        bias_stored = sem("bias_stored")
        ang_ready = sem("ang_ready")
        rope_tab = sem("rope_tab")
        lam_exp_in = sem("lam_exp_in")
        lam_exp = sem("lam_exp")
        sp_ready = sem("sp_ready")
        setup_done = sem("setup_done")
        xr_ready = sem("xr_ready")
        xr_hi = sem("xr_hi")
        xr_lo = sem("xr_lo")
        rg_evac = sem("rg_evac")
        lru_act = sem("lru_act")
        lru_pre = sem("lru_pre")
        lru_mult = sem("lru_mult")
        gated_mult = sem("gated_mult")
        lru_in = sem("lru_in")
        rot_ready = sem("rot_ready")
        rope_done = sem("rope_done")
        yr_ready = sem("yr_ready")
        y_hi = sem("y_hi")
        y_lo = sem("y_lo")
        mask1_landed = sem("mask1_landed")
        q1_staged = sem("q1_staged")
        s1_ready = sem("s1_ready")
        s1_read = sem("s1_read")
        ng1_ready = sem("ng1_ready")
        e1_ready = sem("e1_ready")
        p1_ready = sem("p1_ready")
        t1_ready = sem("t1_ready")
        pt1_ready = sem("pt1_ready")
        o1_ready = sem("o1_ready")
        o1_free = sem("o1_free")
        sg_ready = sem("sg_ready")
        ya_hi = sem("ya_hi")
        ya_lo = sem("ya_lo")
        mix_ready = sem("mix_ready")
        mix_hi = sem("mix_hi")
        mix_lo = sem("mix_lo")
        relu_ready = sem("relu_ready")
        u_hi_ready = sem("u_hi_ready")
        u_ready = sem("u_ready")
        pad_ready = sem("pad_ready")
        av_ready = sem("av_ready")
        silu_ready = sem("silu_ready")
        uv_ready = sem("uv_ready")
        consts2_landed = sem("consts2_landed")
        gate2_ready = sem("gate2_ready")
        kpe_ready = sem("kpe_ready")
        hid_mm = sem("hid_mm")
        hid_ready = sem("hid_ready")
        kvc_mm = sem("kvc_mm")
        kvc_ready = sem("kvc_ready")
        qk2_staged = sem("qk2_staged")
        v2_staged = sem("v2_staged")
        bias_landed = [sem(f"bias_landed{e}") for e in range(2)]
        s2_ready = sem("s2_ready")
        s2_read = sem("s2_read")
        ng2_ready = sem("ng2_ready")
        e2_ready = sem("e2_ready")
        p2_ready = sem("p2_ready")
        t2_pair = sem("t2_pair")
        pt2_pair = sem("pt2_pair")
        t2_ready = sem("t2_ready")
        pt2_ready = sem("pt2_ready")
        o2_ready = sem("o2_ready")
        o2_hi = sem("o2_hi")
        o2_free = sem("o2_free")
        out_stored = sem("out_stored")
        dve_link, act_link = sem("dve_link"), sem("act_link")

        def units_done(u):
            return 4 + 2 * u + 2

        block = ctx.enter_context(nc.Block())

        @block.sync
        def _(sp):
            sp.dma_start(const[:], dram["const"]).then_inc(small_landed, 16)
            sp.dma_start(pos_i[:], dram["pos"].partition_broadcast(P)).then_inc(small_landed, 16)
            sp.dma_start(par[:], dram["par"]).then_inc(small_landed, 16)
            for k in range(4):
                sp.dma_start(x[:, 4 * k:4 * k + 4, :], dram["xt"][:, 4 * k:4 * k + 4, :]).then_inc(x_landed[k], 16)
            sp.dma_start(onehot[:], dram["onehot"]).then_inc(late_landed, 16)
            sp.dma_start(table[0:32, :], dram["table"]).then_inc(late_landed, 16)
            sp.dma_start(sinks[:], dram["sinks"].partition_broadcast(P)).then_inc(late_landed, 16)

            def load_unit(name, i, s, subs):
                sp.wait_ge(lo_ready, 2 * U0[name] + 2 + 4 * i + 2 * s)
                sp.dma_start(w_raw[:, s, 0:subs * P], dram["w_" + name][2 * i + s]).then_inc(w_landed[s], 16)

            def load(name, lo, hi, subs):
                with sp.Fori(lo, hi) as i:
                    for s in range(2):
                        load_unit(name, i, s, subs)

            def load_bias(buf, e, slot, head):
                base = bias_rows[head]
                for blk, (c0, n) in enumerate([(0, P), (P, S)]):
                    src = bass.AP(base.tensor, base.offset + (S - 1 - P * blk), [[511, P], [1, n]])
                    sp.dma_start(buf[:, slot, c0:c0 + n], src).then_inc(bias_landed[e], 16)

            bias_buf = [bias_a, bias_b]

            def load_biases(job0, head0, slots, t, e):
                sp.wait_ge(s2_read, job0 + 2 * t + e + 1)
                for g in range(slots):
                    load_bias(bias_buf[e], e, g, head0 + 4 * g + 2 * t + e)

            for name, n, subs in STREAM:
                if name == "A2":
                    sp.wait_ge(bias_stored, 128)
                    sp.wait_ge(std_ready, 5)
                    with sp.Fori(0, n // 2) as i:
                        for e in range(2):
                            load_unit(name, i, e, subs)
                            load_biases(JOB_C, 20, 1, i, e)
                elif name == "VAB":
                    load(name, 0, 2, subs)
                    for e in range(2):
                        load_biases(JOB_A, 0, 3, 0, e)
                    load(name, 2, n // 2, subs)
                elif name == "OC":
                    load(name, 0, 1, subs)
                    for e in range(2):
                        load_biases(JOB_A, 0, 3, 1, e)
                    load(name, 1, 5, subs)
                    for e in range(2):
                        load_biases(JOB_B, 12, 1, 0, e)
                    load(name, 5, n // 2, subs)
                elif name == "OA":
                    load(name, 0, 1, subs)
                    with sp.Fori(0, 3) as t:
                        for e in range(2):
                            for s in range(2):
                                load_unit(name, 2 * t + e + 1, s, subs)
                            load_biases(JOB_B, 12, 1, t + 1, e)
                    load(name, 7, 8, subs)
                else:
                    load(name, 0, n // 2, subs)
            sp.wait_ge(x_new, 48)
            sp.dma_start(dram["out"], qy[:]).then_inc(out_stored, 16)
            sp.wait_ge(out_stored, 16)

        @block.gpsimd
        def _(pool):
            pool.sem_inc(ss_step, 2)

            def add_squares(norm):
                n = NC_D * norm
                if norm:
                    pool.wait_ge(sums_ready, norm)
                pool.wait_ge(sq_ready, n + 1)
                pool.tensor_copy(sq_sum[:], tmp[0][:, 0:S]).then_inc(ss_step, 1)

                def add(c, s):
                    pool.wait_ge(sq_ready, n + c + 1)
                    pool.wait_ge(ss_step, 2 + n + c)
                    pool.tensor_tensor(sq_sum[:], sq_sum[:], tmp[s][:, 0:S], ALU.add).then_inc(ss_step, 1)

                add(1, 1)
                with pool.Fori(1, NC_D // 2) as i:
                    for s in range(2):
                        add(2 * i + s, s)

            add_squares(0)
            pool.wait_ge(rows_ready, 1)
            for h0 in range(0, 32, 4):
                pool.wait_ge(xr_ready, 2 + h0 // 2 + 1)
                src = rows[h0:h0 + 4, min(h0 // 4, 3), :]
                rep = bass.AP(src.tensor, src.offset, [list(src.ap[0]), [0, P], [1, 512]])
                pool.dma_start(bias_rows[h0:h0 + 4], rep).then_inc(bias_stored, 16)

            pool.wait_ge(lru_mult, 1)
            for g in range(4):
                own, gate = slice(4 * g, 4 * g + 4), slice(NC_D + 4 * g, NC_D + 4 * g + 4)
                pool.tensor_tensor(gates[:, gate, :], gates[:, own, :], gates[:, gate, :], ALU.mult).then_inc(gated_mult, 1)
                pool.wait_ge(gated_mult, g + 1)
                pool.tensor_tensor(gates[:, gate, :], gates[:, gate, :], xr[:, own, :], ALU.mult).then_inc(lru_in, 4)

            pool.wait_ge(yr_ready, 2 + NC_D)
            pool.dma_start(mask1[:], dram["mask1"]).then_inc(mask1_landed, 16)
            pool.wait_ge(rope_done, 2 + 18)
            pool.tensor_copy(q1s[:], qy[:, 0, :]).then_inc(q1_staged, 1)
            with pool.Fori(1, NC_D) as t:
                pool.wait_ge(s1_ready, 2 * t)
                pool.tensor_copy(q1s[:], qy[:, t, :]).then_inc(q1_staged, 1)

            for norm in range(1, 5):
                add_squares(norm)

            pool.wait_ge(std_ready, 4)
            pool.wait_ge(x_new, 32)
            pool.dma_start(cw1[:], dram["cw1"]).then_inc(consts2_landed, 16)
            pool.wait_ge(half_done, units_done(U0["C2"]))
            pool.dma_start(cw2[:], dram["cw2"]).then_inc(consts2_landed, 16)
            pool.dma_start(cpe[:], dram["cpe"]).then_inc(consts2_landed, 16)
            pool.dma_start(cmask[:], dram["cmask"]).then_inc(consts2_landed, 16)

            pool.wait_ge(consts2_landed, 64)
            for kv in range(KV_C):
                pool.wait_ge(acc_free, 2 + T0["C2"] + 7 + kv)
                pool.tensor_tensor(kpe[:, kv], windows(qk2[:, 26 + kv, :], 0, P, 0, [[16, N_CMP], [1, CMP_LEN]]),
                                   windows(cpe[:], 0, P, 0, [[0, N_CMP], [1, CMP_LEN]]), ALU.add).then_inc(kpe_ready, 1)

            with pool.Fori(0, KV_C) as kv:
                for uu in range(2):
                    job = JOB_C + 4 * kv + 2 * uu
                    pool.wait_ge(kvc_ready, 1)
                    pool.wait_ge(s2_ready, 2 + job)
                    last = pool.tensor_copy(q2s[:, 0, :], qk2[:, 20 + 2 * kv + uu, :])
                    if uu == 0:
                        pool.tensor_copy(kcs[:, 0:N_CMP], kc[:, bass.ds(kv * N_CMP, N_CMP)])
                        for br in range(2):
                            last = pool.tensor_copy(k2s[br][:, 0:S], ks2[:, br, kv, :])
                    last.then_inc(qk2_staged, 1)
                    if uu == 0:
                        pool.wait_ge(o2_ready, 2 + job)
                        pool.tensor_copy(vcs[:], vc[:, kv, :])
                        for br in range(2):
                            last = pool.tensor_copy(v2s[:, 0, br], v2[:, :, bass.ds(1280 + br * 192 + kv * HD, HD)])
                        last.then_inc(v2_staged, 4)
            with pool.Fori(0, 2) as t:
                pool.wait_ge(s2_ready, 2 + JOB_A + 2 * t)
                pool.wait_ge(acc_free, 2 + T0["VAB"])
                for g in range(3):
                    pool.tensor_copy(q2s[:, g, :], qk2[:, 4 * g + t, :])
                    last = pool.tensor_copy(k2s[g][:, 0:S], qk2[:, 4 * g + 2 + t, :])
                last.then_inc(qk2_staged, 1)
            with pool.Fori(0, 2) as t:
                for e in range(2):
                    pool.wait_ge(o2_ready, JOB_A + 2 * t + e + 1)
                    pool.wait_ge(acc_free, 2 + T0["OC"])
                    for g in range(3):
                        last = pool.tensor_copy(v2s[:, e, g], v2[:, :, bass.ds(g * 256 + (2 * t + e) * HD, HD)])
                    last.then_inc(v2_staged, 1)
            with pool.Fori(0, 4) as t:
                for e in range(2):
                    job = JOB_B + 2 * t + e
                    if e == 0:
                        pool.wait_ge(acc_free, 2 + T0["OC"])
                        pool.wait_ge(s2_ready, 2 + job)
                        pool.tensor_copy(q2s[:, 0, :], qk2[:, 12 + t, :])
                        pool.tensor_copy(k2s[0][:, 0:S], qk2[:, 16 + t, :]).then_inc(qk2_staged, 1)
                    pool.wait_ge(acc_free, 2 + T0["OC"])
                    pool.wait_ge(o2_ready, job + 1)
                    pool.tensor_copy(v2s[:, e, 0], v2[:, :, bass.ds(768 + (2 * t + e) * HD, HD)]).then_inc(v2_staged, 1)
            for norm in range(5, 7):
                add_squares(norm)

        @block.tensor
        def _(pe):
            pe.sem_inc(half_done, 4)
            pe.sem_inc(t1_ready, 2)
            pe.sem_inc(o1_ready, 2)
            pe.sem_inc(o2_ready, 2)
            pe.sem_inc(s2_ready, 2)
            pe.wait_ge(small_landed, 48)
            pe.wait_ge(setup_done, 1)

            def half_unit(u, s, hf, n, acc, rhs, k0, start, stop, ready=None):
                pe.wait_ge(lo_ready, 4 + 2 * u + hf + 1)
                for k in range(n):
                    if ready:
                        pe.wait_ge(ready[0], ready[1] + k0 + k + 1)
                    w0, w1 = (w[:, 2 * s + hf, k * P:(k + 1) * P] for w in (w_hi, w_lo))
                    r0, r1 = rhs(k0 + k) if callable(rhs) else (r[:, k0 + k, :] for r in rhs)
                    pe.matmul(acc, w0, r0, start=start and k == 0, stop=False)
                    pe.matmul(acc, w0, r1, start=False, stop=False)
                    mm = pe.matmul(acc, w1, r0, start=False, stop=stop and k == n - 1)
                mm.then_inc(half_done, 1)

            def product(name, n, rhs, mid=None, peel=False, subs=SUB, ready=None, norm=None, first=0):
                n0, n1 = split_sizes(subs)

                def pair(i):
                    for s in range(2):
                        u = U0[name] + 2 * i + s
                        pe.wait_ge(acc_free, T0[name] + 2 * i + s + 1)
                        acc = PS[:, s, 0:S]
                        follow = ready if isinstance(i, int) and s == 0 else None
                        half_unit(u, s, 0, n0, acc, rhs, 0, True, False, follow)
                        if mid is not None:
                            mid(i, s)
                        half_unit(u, s, 1, n1, acc, rhs, n0, False, True, follow)
                        if norm is not None and isinstance(i, int) and s == 0:
                            sum_features(norm)

                if peel or ready:
                    pair(0)
                with pe.Fori(1 if peel or ready else first, n // 2) as i:
                    pair(i)

            def product2(name, n, rhs, ready, subs=SUB):
                n0, n1 = split_sizes(subs)

                def pair(i):
                    for s in range(2):
                        pe.wait_ge(acc_free, T0[name] + 2 * i + s + 1)
                        for part in range(2):
                            u = U0[name] + 4 * i + 2 * s + part
                            acc = PS[:, s, 0:S]
                            follow = ready if isinstance(i, int) and s == 0 else None
                            half_unit(u, part, 0, n0, acc, rhs, part * subs, part == 0, False, follow)
                            half_unit(u, part, 1, n1, acc, rhs, part * subs + n0, False, part == 1, follow)

                pair(0)
                with pe.Fori(1, n // 2) as i:
                    pair(i)

            def pair_v(name, i, first, odd):
                if first:
                    pe.wait_ge(acc_free, T0[name] + 2)
                else:
                    pe.wait_ge(acc_free, T0[name] + 2 * i)
                for s in range(2):
                    for hf in range(2):
                        pe.wait_ge(lo_ready, 4 + 2 * (U0[name] + 2 * i + s) + hf + 1)
                        for k in range(HALF // 2):
                            w0, w1 = (w[:, 2 * s + hf, k * S:(k + 1) * S] for w in (w_hi, w_lo))
                            c = HALF * s + HALF // 2 * hf + k
                            for th in range(2):
                                acc = PS[:, 5 * odd + th, 0:S]
                                a0, a1 = (a[:, c, th * P:(th + 1) * P] for a in (h_hi, h_lo))
                                pe.matmul(acc, a0, w0, start=c == 0, stop=False)
                                pe.matmul(acc, a0, w1, start=False, stop=False)
                                mm = pe.matmul(acc, a1, w0, start=False, stop=c == NC_D - 1)
                        mm.then_inc(half_done, 1)

            def sum_features(norm):
                pe.wait_ge(ss_step, 2 + NC_D * (norm + 1))
                if norm:
                    pe.wait_ge(std_ready, norm)
                pe.matmul(PS[:, 7, 0:S], ones[:], sq_sum[:], start=True, stop=True).then_inc(sums_ready, 1)

            sum_features(0)
            pe.wait_ge(late_landed, 48)
            for var in range(4):
                mm = pe.matmul(PS[0:32, 2 + var, :], table[:], onehot[:, var, :], start=True, stop=True)
            mm.then_inc(rows_mm, 1)

            product("X", 16, (h_hi, h_lo), ready=(h_ready, 4))
            pe.wait_ge(rows_ready, 1)

            pe.wait_ge(acc_free, 2 + T0["Q"])
            with pe.Fori(0, 2) as bh:
                pe.wait_ge(xr_lo, 8 * bh + 8)
                for hx in range(4):
                    s, hf = hx // 2, hx % 2
                    u = U0["RG"] + 2 * bh + s
                    pe.wait_ge(lo_ready, 4 + 2 * u + hf + 1)
                    pe.wait_ge(rg_evac, 4 * bh + hx + 1)
                    for b in range(2):
                        for m in range(2):
                            acc = PS[:, 2 * hf + b, m * S:(m + 1) * S]
                            for kk in range(2):
                                sub = (b * 2 + m) * 2 + kk
                                w0, w1 = (w[:, 2 * s + hf, sub * P:(sub + 1) * P] for w in (w_hi, w_lo))
                                r0, r1 = (r[:, 8 * bh + 4 * hf + 2 * b + kk, :] for r in (d_hi, d_lo))
                                pe.matmul(acc, w0, r0, start=kk == 0, stop=False)
                                pe.matmul(acc, w0, r1, start=False, stop=False)
                                mm = pe.matmul(acc, w1, r0, start=False, stop=kk == 1)
                    mm.then_inc(half_done, 1)

            pe.wait_ge(rg_evac, 2 + 8)

            def rotate(c, s):
                pe.wait_ge(acc_free, 2 + T0["Q"] + c + 1)
                pe.wait_ge(rope_done, c + 1)
                pe.matmul(PS[:, 6 + s, 0:S], rot_t, tmp[s][:, 0:S], start=True, stop=True).then_inc(rot_ready, 1)

            def rotate_mid(i, s):
                if not (isinstance(i, int) and s == 0):
                    rotate(2 * i + s - 1, 1 - s)

            product("Q", 18, (h_hi, h_lo), mid=rotate_mid, peel=True)
            rotate(17, 1)
            product("Y", 16, (h_hi, h_lo))
            pair_v("V", 0, True, 0)

            pe.wait_ge(acc_free, 2 + T0["G"])
            pe.wait_ge(rope_done, 2 + 18)

            def scores1(hd, gp, e, tile):
                if e == 0:
                    pe.wait_ge(q1_staged, tile + 1)
                pe.wait_ge(s1_read, hd + 1)
                lo, up = HD * e, HD * e + HD
                pe.matmul(PS[:, 2 + e, 0:P], q1s[lo:up, 0:P], kt[lo:up, gp, 0:P], start=True, stop=True)
                pe.matmul(PS[:, 2 + e, P:SC], q1s[lo:up, P:S], kt[lo:up, gp, :], start=True, stop=True)\
                    .then_inc(s1_ready, 1)

            def turn1(hd, e):
                pe.wait_ge(p1_ready, hd + 1)
                pe.wait_ge(pt1_ready, hd + 1)
                for b in range(3):
                    mm = pe.transpose(PS[:, 4 + e, b * P:(b + 1) * P], sb1[:, e, b * P:(b + 1) * P], ident)
                mm.then_inc(t1_ready, 1)

            def pv1(hd, gp, e, tile):
                pe.wait_ge(pt1_ready, 2 + hd + 1)
                if e == 0:
                    pe.wait_ge(o1_free, tile + 1)
                o = PS[HD * e:HD * e + HD, 6, :]
                g = 2 * gp + e
                pe.matmul(o[:, 0:S], vv[:, 0, g * HD:(g + 1) * HD], pt1[:, e, 0:S], start=True, stop=False,
                          skip_group_check=True)
                pe.matmul(o[:, P:S], vv[:, 1, g * HD:(g + 1) * HD], pt1[:, e, S:SC], start=False, stop=True,
                          skip_group_check=True).then_inc(o1_ready, 1)

            pe.wait_ge(mask1_landed, 16)
            for gp in range(2):
                def tile_units(i):
                    first = isinstance(i, int)
                    tile = 8 * gp + i
                    for e in range(2):
                        u = U0["G"] + 2 * tile + e
                        hd = 2 * tile + e
                        pe.wait_ge(acc_free, T0["G"] + 2 * tile + e + 1)
                        acc = PS[:, e, 0:S]
                        half_unit(u, e, 0, HALF, acc, (h_hi, h_lo), 0, True, False)
                        if not (first and e == 0):
                            turn1(hd - 1, 1 - e)
                        scores1(hd, gp, e, tile)
                        half_unit(u, e, 1, HALF, acc, (h_hi, h_lo), HALF, False, True)
                        if not (first and e == 0):
                            pv1(hd - 1, gp, 1 - e, tile - (1 - e))

                tile_units(0)
                with pe.Fori(1, 8) as i:
                    tile_units(i)
                turn1(16 * gp + 15, 1)
                pv1(16 * gp + 15, gp, 1, 8 * gp + 7)

            pe.wait_ge(y_lo, NC_D)
            product("MR", 16, (d_hi, d_lo))
            pe.wait_ge(ya_lo, NC_D)
            product("MA", 16, (h_hi, h_lo))
            product("O", 16, (d_hi, d_lo), ready=(mix_lo, 0))
            sum_features(1)

            for hx in range(2):
                product(f"UP{hx}", 32, (h_hi, h_lo), ready=None if hx else (h_ready, 4 + NC_D),
                        norm=None if hx else 2)
                product2(f"DN{hx}", 16, (u_hi, u_lo), (u_ready, 2 + FF1_H * hx))
            sum_features(3)
            sum_features(4)

            product("C2", 12, (h_hi, h_lo), ready=(h_ready, 4 + 2 * NC_D))
            pair_v("VC", 0, True, 0)

            pe.wait_ge(consts2_landed, 64)
            pe.wait_ge(kpe_ready, KV_C)
            for br in range(2):
                lo, up = HD * br, HD * br + HD
                for j in range(CMP_LEN):
                    mm = pe.matmul(PS[:, 2 + br, 0:KV_C * N_CMP], cw1[lo:up, j, :],
                                   kpe[lo:up].rearrange("p v n j -> p (v n) j")[:, :, j],
                                   start=j == 0, stop=j == CMP_LEN - 1)
            mm.then_inc(hid_mm, 1)
            pair_v("VC", 1, False, 1)
            pe.wait_ge(hid_ready, 1)
            pe.matmul(PS[0:HD, 4, 0:KV_C * N_CMP], cw2[:, 0, :], hid[:, 0, :], start=True, stop=True)
            for kv in range(KV_C):
                mm = pe.matmul(PS[0:N_CMP, 7, kv * HD:(kv + 1) * HD], hid[:, 1, kv * N_CMP:(kv + 1) * N_CMP],
                               cw2[:, 1, :], start=True, stop=True)
            mm.then_inc(kvc_mm, 1)

            def scores2(bank, e, slot, k):
                lo, up = HD * e, HD * e + HD
                pe.matmul(PS[:, bank, 0:P], q2s[lo:up, slot, 0:P], k[:, 0:P], start=True, stop=True)
                return pe.matmul(PS[:, bank, P:SC], q2s[lo:up, slot, P:S], k, start=True, stop=True)

            def turn2(bank, e, slot):
                for b in range(3):
                    mm = pe.transpose(PS[:, bank, b * P:(b + 1) * P], sb2[:, e, slot, b * P:(b + 1) * P], ident)
                return mm

            def pv2(o, e, slot, start, stop):
                pe.matmul(o, v2s[:, e, slot, 0, :], pt2[:, slot, 0:S], start=start, stop=False, skip_group_check=True)
                return pe.matmul(o[:, P:S], v2s[:, e, slot, 1, :], pt2[:, slot, S:SC], start=False, stop=stop,
                                 skip_group_check=True)

            def scores_step(job0, t, e, scores):
                job = job0 + 2 * t + e
                if e == 0:
                    pe.wait_ge(qk2_staged, job0 // 2 + t + 1)
                pe.wait_ge(s2_read, 2 + job)
                scores(e).then_inc(s2_ready, 1)

            def turn_step(job0, t, e, turn):
                pe.wait_ge(p2_ready, job0 + 2 * t + e + 1)
                turn(e).then_inc(t2_ready, 1)

            def weigh_step(job0, t, e, weigh):
                job = job0 + 2 * t + e
                pe.wait_ge(v2_staged, job + 1)
                pe.wait_ge(pt2_ready, job + 1)
                if e == 0:
                    pe.wait_ge(o2_free, job0 // 2 + t + 1)
                weigh(e).then_inc(o2_ready, 1)

            def scores_c(e):
                lo, up = HD * e, HD * e + HD
                for qt in range(2):
                    pe.matmul(PS[:, 2, SC + qt * N_CMP:SC + (qt + 1) * N_CMP], q2s[lo:up, 0, qt * P:(qt + 1) * P],
                              kcs[lo:up, 0:N_CMP], start=True, stop=True)
                for br in range(2):
                    mm = scores2(2 + br, e, 0, k2s[br][lo:up, 0:S])
                return mm

            def turn_c(e):
                for qt in range(2):
                    pe.transpose(PS[0:N_CMP, 4, qt * P:(qt + 1) * P], sbc[:, e, qt, :], ident)
                for br in range(2):
                    mm = turn2(5 + br, e, br)
                return mm

            def weigh_c(e):
                o = PS[HD * e:HD * e + HD, 7, 0:S]
                pv2(o, 0, 0, True, False)
                pv2(o, 0, 1, False, False)
                return pe.matmul(o, vcs[:], ptc[:], start=False, stop=True, skip_group_check=True)

            product("B2", 6, (h_hi, h_lo))
            pe.wait_ge(kvc_ready, 1)
            scores_step(JOB_C, 0, 0, scores_c)
            product("B2", 8, (h_hi, h_lo), first=3)
            scores_step(JOB_C, 0, 1, scores_c)

            def tile_c(t, more):
                for e in range(2):
                    u = U0["A2"] + 2 * t + e
                    pe.wait_ge(acc_free, T0["A2"] + 2 * t + e + 1)
                    acc = PS[:, e, 0:S]
                    half_unit(u, e, 0, HALF, acc, (h_hi, h_lo), 0, True, False)
                    turn_step(JOB_C, t, e, turn_c)
                    if more:
                        scores_step(JOB_C, t + 1, e, scores_c)
                    half_unit(u, e, 1, HALF, acc, (h_hi, h_lo), HALF, False, True)
                    weigh_step(JOB_C, t, e, weigh_c)

            with pe.Fori(0, 2 * KV_C - 1) as t:
                tile_c(t, True)
            tile_c(2 * KV_C - 1, False)

            def scores_a(e):
                for g in range(3):
                    mm = scores2(2 + g, e, g, k2s[g][HD * e:HD * e + HD, 0:S])
                return mm

            def weigh_a(e):
                for g in range(3):
                    mm = pv2(PS[HD * e:HD * e + HD, 7 if g < 2 else 1, (g % 2) * S:(g % 2 + 1) * S], e, g, True, True)
                return mm

            pair_v("VAB", 0, True, 0)
            pair_v("VAB", 1, False, 1)
            pair_v("VAB", 2, False, 0)
            scores_step(JOB_A, 0, 0, scores_a)
            pair_v("VAB", 3, False, 1)
            scores_step(JOB_A, 0, 1, scores_a)
            pair_v("VAB", 4, False, 0)
            pe.wait_ge(acc_free, 2 + T0["OC"])

            def scores_b(e):
                return scores2(2, e, 0, k2s[0][HD * e:HD * e + HD, 0:S])

            for k in range(4):
                t, e = k // 2, k % 2

                def project_c(f):
                    c = 4 * k + f
                    pe.wait_ge(acc_free, 2 + T0["OC"] + c)
                    for hf, n in enumerate(split_sizes(SUB_O)):
                        half_unit(U0["OC"] + c, f % 2, hf, n, PS[:, 0, 0:S], (oc_hi, oc_lo), n * hf, hf == 0, hf == 1)

                project_c(0)
                pe.wait_ge(p2_ready, JOB_A + k + 1)
                for g in range(2):
                    mm = turn2(5 + g, e, g)
                mm.then_inc(t2_pair, 1)
                if t == 0:
                    scores_step(JOB_A, 1, e, scores_a)
                else:
                    scores_step(JOB_B, 0, e, scores_b)
                project_c(1)
                pe.wait_ge(pt2_pair, k + 1)
                turn2(5, e, 2).then_inc(t2_ready, 1)
                project_c(2)
                weigh_step(JOB_A, t, e, weigh_a)
                project_c(3)

            def project_a(t, e, s):
                u = U0["OA"] + 4 * t + 2 * e + s
                pe.wait_ge(acc_free, T0["OA"] + 4 * t + 2 * e + s + 1)
                for hf, n in enumerate(split_sizes(SUB_O)):
                    half_unit(u, s, hf, n, PS[:, s, 0:S], (h_hi, h_lo), n * hf, hf == 0, hf == 1)

            def tile_b(t, more):
                for e in range(2):
                    project_a(t, e, 0)
                    turn_step(JOB_B, t, e, lambda e: turn2(5, e, 0))
                    if more:
                        scores_step(JOB_B, t + 1, e, scores_b)
                    project_a(t, e, 1)
                    weigh_step(JOB_B, t, e, lambda e: pv2(PS[HD * e:HD * e + HD, 7, 0:S], e, 0, True, True))

            pe.wait_ge(o2_free, 1 + JOB_B // 2)
            pe.wait_ge(acc_free, 2 + T0["OA"])
            with pe.Fori(0, 3) as t:
                tile_b(t, True)
            tile_b(3, False)

            pe.wait_ge(o2_free, 1 + 12)
            product("OB", 16, [(h_hi[:, 6 + c, :], h_lo[:, 6 + c, :]) for c in range(4)].__getitem__, subs=4)

            for hx in range(2):
                product(f"FU{hx}", 44, (f_hi, f_lo), ready=None if hx else (h_ready, 4 + 3 * NC_D),
                        norm=None if hx else 5)
                product2(f"FD{hx}", 16, (u_hi, u_lo), (u_ready, 2 + 2 * FF1_H + FF2_H * hx), subs=DN2_SUB)
            sum_features(6)

        names = [n for n, _, _ in STREAM]
        subs_of = {n: k for n, _, k in STREAM}
        pairs_of = {n: k // 2 for n, k, _ in STREAM}

        def next_subs(name):
            at = names.index(name) + 1
            return subs_of[names[at]] if at < len(names) else 0

        def run_pairs(eng, name, trips, body, peel=False, link=None, per=0):
            lo = 0
            odd_end = next_subs(name) != subs_of[name]

            def one(i, n):
                if link:
                    link.begin(i, per)
                body(i, n)

            if peel:
                one(0, subs_of[name])
                lo = 1
            with eng.Fori(lo, trips - 1 if odd_end else trips) as i:
                one(i, subs_of[name])
            if odd_end:
                one(trips - 1, next_subs(name))
            if link:
                link.end(trips)

        @block.scalar
        def _(act):
            link = Link(act, act_link)
            act.sem_inc(acc_free, 2)
            act.sem_inc(rg_evac, 2)
            act.sem_inc(pt1_ready, 2)
            act.wait_ge(small_landed, 48)
            act.wait_ge(setup_done, 1)

            def half_hi(pair, s, hf, subs):
                n0, n1 = split_sizes(subs)
                n, off = (n0, 0) if hf == 0 else (n1, n0)
                if hf == 0:
                    act.wait_ge(w_landed[s], 16 * pair + 16)
                act.wait_ge(half_done, 4 * pair + 2 * s + hf + 1)
                act.activation(w_hi[:, 2 * s + hf, 0:n * P], w_raw[:, s, off * P:(off + n) * P], ACT.Copy)\
                    .then_inc(hi_ready, 1)

            def unit_hi(pair, s, subs):
                if subs:
                    half_hi(pair, s, 0, subs)
                    half_hi(pair, s, 1, subs)

            def next_hi(pair, s, subs, hf=None):
                at = (pair, 1) if s == 0 else (pair + 1, 0)
                for k in (0, 1) if hf is None else (hf,):
                    if subs:
                        half_hi(*at, k, subs)

            n_sq, n_norm, n_hv, n_x = [0], [0], [0], [0]

            def squares(first):
                for k in range(4 if first else 1):
                    with act.Fori(2 * k if first else 0, 2 * k + 2 if first else NC_D // 2) as i:
                        for s in range(2):
                            c = 2 * i + s
                            if not first:
                                act.wait_ge(x_new, n_x[0] + c + 1)
                            act.wait_ge(ss_step, n_sq[0] + c + 1)
                            if first:
                                act.wait_ge(x_landed[k], 16)
                            act.activation(tmp[s][:, 0:S], x[:, c, :], ACT.Square).then_inc(sq_ready, 1)
                n_sq[0] += NC_D
                n_x[0] += 0 if first else NC_D

            def squares_and_hi(gain):
                with act.Fori(0, NC_D // 2) as i:
                    for s in range(2):
                        c = 2 * i + s
                        act.wait_ge(ss_step, n_sq[0] + c + 1)
                        act.wait_ge(x_new, n_x[0] + c + 1)
                        act.activation(h_hi[:, c, :], x[:, c, :], ACT.Identity, scale=pcol(gain, c)).then_inc(h_hi_ready, 1)
                        act.activation(tmp[s][:, 0:S], x[:, c, :], ACT.Square).then_inc(sq_ready, 1)
                n_sq[0] += NC_D
                n_x[0] += NC_D

            def deviation():
                act.wait_ge(sums_ready, n_norm[0] + 1)
                act.activation(tmp[2][:, 0:S], PS[:, 7, 0:S], ACT.Sqrt, bias=eps[:, 0:1], scale=1.0 / D)\
                    .then_inc(std_ready, 1)
                n_norm[0] += 1

            def round_h():
                with act.Fori(0, NC_D // 4) as i:
                    for s in range(4):
                        c = 4 * i + s
                        act.wait_ge(hv_ready, n_hv[0] + c + 1)
                        act.activation(h_hi[:, c, :], tmp[(4, 5, 0, 1)[s]][:, 0:S], ACT.Copy).then_inc(h_hi_ready, 1)
                n_hv[0] += NC_D

            act.wait_ge(lam_exp_in, 1)
            act.activation(lam[:, 2, :], lam[:, 1, :], ACT.Exp).then_inc(lam_exp, 1)
            squares(True)
            act.wait_ge(ang_ready, 1)
            act.activation(sin[:], ang[:, 2, :], ACT.Sin)
            act.activation(cos[:], ang[:, 3, :], ACT.Sin).then_inc(rope_tab, 1)
            deviation()
            unit_hi(0, 0, SUB)
            round_h()
            act.wait_ge(rows_mm, 1)
            act.activation(rows[:], PS[0:32, 2:6, :], ACT.Copy).then_inc(rows_ready, 1)

            def conv_hi(c):
                act.wait_ge(xr_ready, 2 + c + 1)
                act.activation(d_hi[:, c, :], xr[:, c, :], ACT.Copy).then_inc(xr_hi, 1)

            def body(i, n):
                for s in range(2):
                    c, pair = 2 * i + s, U0["X"] // 2 + i
                    next_hi(pair, s, n)
                    if not isinstance(i, int) or i + s:
                        conv_hi(c - 1)
                    act.wait_ge(half_done, units_done(U0["X"] + c))
                    act.wait_ge(xr_ready, c + 1)
                    act.activation(tmp[2 + s][:, 0:S], PS[:, s, 0:S], ACT.Identity, scale=pcol("conv_w", 4 * c + 3),
                                   bias=pcol("conv_b", c))
                    act.activation(tmp[s][:, 3:3 + S], PS[:, s, 0:S], ACT.Copy).then_inc(acc_free, 1)
            run_pairs(act, "X", 8, body, peel=True)
            conv_hi(NC_D - 1)

            act.wait_ge(bias_stored, 128)
            act.preload_act_table(ACT.Sigmoid)
            with act.Fori(0, 2) as bh:
                for mat in range(2):
                    u, pair = U0["RG"] + 2 * bh + mat, U0["RG"] // 2 + bh
                    next_hi(pair, mat, SUB)
                    for hf in range(2):
                        act.wait_ge(half_done, 4 + 2 * u + hf + 1)
                        for t in range(4):
                            c = 8 * bh + 4 * hf + t
                            ins = act.activation(gates[:, 16 * mat + c, :], PS[:, 2 * hf + t // 2, t % 2 * S:(t % 2 + 1) * S],
                                                 ACT.Sigmoid, bias=pcol("b_rg_x" if mat else "b_rg_a", c))
                        ins.then_inc(rg_evac, 1)

            act.preload_act_table(ACT.Exp)
            act.wait_ge(sp_ready, 1)
            act.wait_ge(xr_lo, NC_D)

            def rope_in(c, s):
                act.wait_ge(half_done, units_done(U0["Q"] + c))
                act.wait_ge(rope_done, c + 1)
                act.activation(tmp[s][:, 0:S], PS[:, s, 0:S], ACT.Copy).then_inc(acc_free, 1)

            act.wait_ge(rg_evac, 2 + 8)
            with act.Fori(0, 8) as i:
                for s in range(2):
                    c = 2 * i + s
                    next_hi(U0["Q"] // 2 + i, s, SUB)
                    act.activation(a_lru[:, c, :], gates[:, c, :], ACT.Exp, scale=sp8[:, 1, bass.ds(c, 1)])
                    act.wait_ge(lru_pre, c + 1)
                    act.activation(tmp[4 + s][:, 0:S], gates[:, c, :], ACT.Tanh, scale=sp8[:, 0, bass.ds(c, 1)])\
                        .then_inc(lru_act, 1)
                    rope_in(c, s)
            for s in range(2):
                next_hi(U0["Q"] // 2 + 8, s, SUB)
                rope_in(16 + s, s)
            act.wait_ge(lru_pre, 2 + NC_D)
            act.activation(gates[:, 0:NC_D, :], gates[:, 0:NC_D, :], ACT.Sqrt).then_inc(lru_mult, 1)
            act.wait_ge(rope_done, 2 + 18)

            act.preload_act_table(ACT.Gelu_apprx_tanh)

            def body(i, n):
                for s in range(2):
                    c = 2 * i + s
                    next_hi(U0["Y"] // 2 + i, s, n)
                    act.wait_ge(half_done, units_done(U0["Y"] + c))
                    act.wait_ge(yr_ready, c + 1)
                    act.activation(tmp[s][:, 0:S], PS[:, s, 0:S], ACT.Gelu_apprx_tanh).then_inc(acc_free, 1)
                    act.wait_ge(yr_ready, 2 + c + 1)
                    act.activation(d_hi[:, c, :], tmp[4 + s][:, 0:S], ACT.Copy).then_inc(y_hi, 1)
            run_pairs(act, "Y", 8, body)

            next_hi(U0["V"] // 2, 0, SUB)
            next_hi(U0["V"] // 2, 1, SUB)
            act.wait_ge(half_done, units_done(U0["V"] + 1))
            for th in range(2):
                act.activation(vv[:, th, :], PS[:, th, 0:S], ACT.Copy).then_inc(acc_free, 1)

            act.preload_act_table(ACT.Exp)

            def copy_pt1(hd, e):
                act.wait_ge(t1_ready, 2 + hd + 1)
                act.wait_ge(o1_ready, hd + 1)
                act.activation(pt1[:, e, :], PS[:, 4 + e, 0:SC], ACT.Copy).then_inc(pt1_ready, 1)

            def exp1(hd, e):
                mx, ng, den, es, rd = (small[:, 10 * e + 2 * j:10 * e + 2 * j + 2] for j in range(5))
                act.wait_ge(ng1_ready, hd + 1)
                act.activation(sb1[:, e, 0:P], sb1[:, e, 0:P], ACT.Exp, bias=ng[:, 0:1], accum_out=den[:, 0:1])
                act.activation(sb1[:, e, P:SC], sb1[:, e, P:SC], ACT.Exp, bias=ng[:, 1:2], accum_out=den[:, 1:2])
                act.activation(es, ng, ACT.Exp, bias=sinks[:, bass.ds(hd, 1)]).then_inc(e1_ready, 1)

            for gp in range(2):
                def body(i):
                    first = isinstance(i, int)
                    for e in range(2):
                        hd = 16 * gp + 2 * i + e
                        pair = U0["G"] // 2 + 8 * gp + i
                        next_hi(pair, e, SUB, 0)
                        if not (first and e == 0):
                            copy_pt1(hd - 1, 1 - e)
                        next_hi(pair, e, SUB, 1)
                        exp1(hd, e)
                        act.wait_ge(half_done, units_done(U0["G"] + hd))
                        act.activation(gates[:, hd, :], PS[:, e, 0:S], ACT.Copy).then_inc(acc_free, 1)
                body(0)
                with act.Fori(1, 8) as i:
                    body(i)
                copy_pt1(16 * gp + 15, 1)

            act.preload_act_table(ACT.Sigmoid)
            act.wait_ge(o1_free, 1 + NC_D)

            def body(i, n):
                for s in range(2):
                    c = 2 * i + s
                    next_hi(U0["MR"] // 2 + i, s, n)
                    act.wait_ge(acc_free, T0["MR"] + c + 1)
                    act.activation(tmp[s][:, 0:S], gates[:, c, :], ACT.Sigmoid).then_inc(sg_ready, 1)
                    act.activation(h_hi[:, c, :], qy[:, c, :], ACT.Copy).then_inc(ya_hi, 1)
            run_pairs(act, "MR", 8, body)

            def body(i, n):
                for s in range(2):
                    c = 2 * i + s
                    next_hi(U0["MA"] // 2 + i, s, n)
                    act.wait_ge(acc_free, T0["MA"] + c + 1)
                    act.activation(tmp[s][:, 0:S], gates[:, NC_D + c, :], ACT.Sigmoid).then_inc(sg_ready, 1)
                    act.wait_ge(mix_ready, c + 1)
                    act.activation(d_hi[:, c, :], tmp[4 + s][:, 0:S], ACT.Copy).then_inc(mix_hi, 1)
            run_pairs(act, "MA", 8, body)

            act.preload_act_table(ACT.Sqrt)
            act.wait_ge(ya_lo, NC_D)

            def body(i, n):
                for s in range(2):
                    c = 2 * i + s
                    next_hi(U0["O"] // 2 + i, s, n)
                    act.wait_ge(half_done, units_done(U0["O"] + c))
                    act.wait_ge(ss_step, n_sq[0] + c + 1)
                    act.activation(tmp[s][:, 0:S], PS[:, s, 0:S], ACT.Square).then_inc(sq_ready, 1)
                    act.activation(qy[:, c, :], PS[:, s, 0:S], ACT.Copy).then_inc(acc_free, 1)
            run_pairs(act, "O", 8, body)
            n_sq[0] += NC_D
            deviation()
            squares_and_hi("norm_mlp_pre")

            n_u = 0
            for hx in range(2):
                def body(i, n):
                    for s in range(2):
                        c, name = 2 * i + s, f"UP{hx}"
                        next_hi(U0[name] // 2 + i, s, n)
                        if hx == 0 and s == 0 and isinstance(i, int) and i == 0:
                            deviation()
                        act.wait_ge(relu_ready, n_u + c + 1)
                        act.activation(u_hi[:, c, :], tmp[s][:, 0:S], ACT.Square).then_inc(u_hi_ready, 1)
                run_pairs(act, f"UP{hx}", FF1_H // 2, body, peel=hx == 0)
                n_u += FF1_H

                def body(i, n):
                    for s in range(2):
                        c, name = 2 * i + s, f"DN{hx}"
                        pair = U0[name] // 2 + 2 * i + s
                        next_hi(pair, 0, n)
                        next_hi(pair, 1, n)
                        if hx:
                            act.wait_ge(acc_free, 2 + T0[name] + c + 1)
                            act.wait_ge(ss_step, n_sq[0] + c + 1)
                            act.activation(tmp[s][:, 0:S], qy[:, c, :], ACT.Square).then_inc(sq_ready, 1)
                run_pairs(act, f"DN{hx}", 8, body)
            n_sq[0] += NC_D
            deviation()
            squares(False)
            deviation()
            round_h()

            def project(name, i, col):
                for s in range(2):
                    c = 2 * i + s
                    next_hi(U0[name] // 2 + i, s, SUB)
                    act.wait_ge(half_done, units_done(U0[name] + c))
                    act.activation(qk2[:, bass.ds(col + c, 1), :].rearrange("p a b -> p (a b)"), PS[:, s, 0:S], ACT.Copy)\
                        .then_inc(acc_free, 1)

            with act.Fori(0, 4) as i:
                project("C2", i, 20)
            for c in range(8, 12):
                s = c % 2
                next_hi(U0["C2"] // 2 + c // 2, s, SUB)
                act.wait_ge(half_done, units_done(U0["C2"] + c))
                if c == 8:
                    ins = act.activation(qk2[:, 28, :], PS[:, s, 0:S], ACT.Copy)
                else:
                    for br in range(2):
                        for half in range(2):
                            ins = act.activation(ks2[HD * half:HD * half + HD, br, c - 9, :],
                                                 PS[HD * br:HD * br + HD, s, 0:S], ACT.Copy)
                ins.then_inc(acc_free, 1)

            def values(name, i, odd, col, n=SUB):
                next_hi(U0[name] // 2 + i, 0, SUB)
                next_hi(U0[name] // 2 + i, 1, n)
                act.wait_ge(half_done, units_done(U0[name] + 2 * i + 1))
                for th in range(2):
                    act.activation(v2[:, th, bass.ds(col + i * S, S)], PS[:, 5 * odd + th, 0:S], ACT.Copy)\
                        .then_inc(acc_free, 1)
            values("VC", 0, 0, 1280)
            act.wait_ge(hid_mm, 1)
            act.activation(hid[:], PS[:, 2:4, 0:KV_C * N_CMP], ACT.Gelu_apprx_tanh).then_inc(hid_ready, 1)
            values("VC", 1, 1, 1280)
            act.wait_ge(acc_free, 2 + T0["B2"])
            act.activation(gate2[:], v2[:, :, 13 * P:13 * P + 36], ACT.Sigmoid).then_inc(gate2_ready, 1)
            act.wait_ge(kvc_mm, 1)
            act.activation(kc[0:HD], PS[0:HD, 4, 0:KV_C * N_CMP], ACT.Copy)
            act.activation(kc[HD:P], PS[0:HD, 4, 0:KV_C * N_CMP], ACT.Copy)
            act.activation(vc[:], PS[0:N_CMP, 7, 0:KV_C * HD].rearrange("p (v d) -> p v d", v=KV_C), ACT.Copy)\
                .then_inc(kvc_ready, 1)
            act.preload_act_table(ACT.Exp)


            def small2(e, j, n):
                return small[:, 32 * e + j:32 * e + j + n]

            def exp2(src, ng, den):
                return act.activation(src, src, ACT.Exp, bias=ng, accum_out=den)

            def exp_rows(e, cols, j):
                for blk in range(2):
                    ins = exp2(cols(slice(0, P) if blk == 0 else slice(P, SC)), small2(e, 6 + 2 * j + blk, 1),
                               small2(e, 12 + 2 * j + blk, 1))
                return ins

            def exp_a(e):
                return exp_rows(e, lambda c: sb2[:, e, :, c], 0)

            def exp_b(e):
                return exp_rows(e, lambda c: sb2[:, e, 0, c], 0)

            def exp_c(e):
                for br in range(2):
                    exp_rows(e, lambda c: sb2[:, e, br, c], br)
                for qt in range(2):
                    ins = act.activation(sbc[:, e, qt, :], sbc[:, e, qt, :], ACT.Exp, bias=small2(e, 10 + qt, 1))
                return ins

            def copy_slots(n):
                for g in range(n):
                    ins = act.activation(pt2[:, g, :], PS[:, 5 + g, 0:SC], ACT.Copy)
                return ins

            def copy_c():
                copy_slots(2)
                return act.activation(ptc[:], PS[0:N_CMP, 4, 0:S], ACT.Copy)

            def out_hi(hi, bank, col):
                act.activation(hi, PS[:, bank, col:col + S], ACT.Copy).then_inc(o2_hi, 1)

            def exp_step(job0, t, e, exps):
                act.wait_ge(ng2_ready, job0 + 2 * t + e + 1)
                exps(e).then_inc(e2_ready, 1)

            def copy_step(job0, t, e, copies):
                act.wait_ge(t2_ready, job0 + 2 * t + e + 1)
                copies().then_inc(pt2_ready, 1)

            def out_c(t):
                act.wait_ge(o2_ready, 2 + JOB_C + 2 * t + 2)
                out_hi(oc_hi[:, t, :], 7, 0)

            def tile_c(t, more):
                for e in range(2):
                    k, pair = 2 * t + e, U0["A2"] // 2 + t
                    next_hi(pair, e, SUB, 0)
                    if e == 0 and not isinstance(t, int) or e == 0 and t:
                        out_c(t - 1)
                    next_hi(pair, e, SUB, 1)
                    copy_step(JOB_C, t, e, copy_c)
                    act.wait_ge(half_done, units_done(U0["A2"] + k))
                    act.activation(qk2[:, k, :], PS[:, e, 0:S], ACT.Copy).then_inc(acc_free, 1)
                    if more:
                        exp_step(JOB_C, t + 1, e, exp_c)

            with act.Fori(0, 4) as i:
                project("B2", i, 12)
            exp_step(JOB_C, 0, 0, exp_c)
            exp_step(JOB_C, 0, 1, exp_c)
            tile_c(0, True)
            with act.Fori(1, 2 * KV_C - 1) as t:
                tile_c(t, True)
            tile_c(2 * KV_C - 1, False)
            out_c(2 * KV_C - 1)

            for i in range(5):
                values("VAB", i, i % 2, 0, SUB if i < 4 else SUB_O)
                if i >= 3:
                    exp_step(JOB_A, 0, i - 3, exp_a)

            for k in range(4):
                t, e, pair = k // 2, k % 2, U0["OC"] // 2 + 2 * k
                next_hi(pair, 0, SUB_O)
                act.wait_ge(t2_pair, k + 1)
                for g in range(2):
                    ins = act.activation(pt2[:, g, :], PS[:, 5 + g, 0:SC], ACT.Copy)
                ins.then_inc(pt2_pair, 1)
                next_hi(pair, 1, SUB_O)
                act.wait_ge(t2_ready, JOB_A + k + 1)
                act.activation(pt2[:, 2, :], PS[:, 5, 0:SC], ACT.Copy).then_inc(pt2_ready, 1)
                next_hi(pair + 1, 0, SUB_O)
                if t == 0:
                    exp_step(JOB_A, 1, e, exp_a)
                else:
                    exp_step(JOB_B, 0, e, exp_b)
                next_hi(pair + 1, 1, SUB_O)
                if e == 1:
                    act.wait_ge(o2_ready, 2 + JOB_A + k + 1)
                    for g in range(3):
                        out_hi(h_hi[:, 2 * g + t, :], 7 if g < 2 else 1, (g % 2) * S)

            def out_b(t):
                act.wait_ge(o2_ready, 2 + JOB_B + 2 * t + 2)
                out_hi(h_hi[:, 6 + t, :], 7, 0)

            def tile_b(t, more, n):
                for e in range(2):
                    pair = U0["OA"] // 2 + 2 * t + e
                    next_hi(pair, 0, SUB_O)
                    if e == 0 and not isinstance(t, int) or e == 0 and t:
                        out_b(t - 1)
                    copy_step(JOB_B, t, e, lambda: copy_slots(1))
                    next_hi(pair, 1, n if e else SUB_O)
                    if more:
                        exp_step(JOB_B, t + 1, e, exp_b)

            tile_b(0, True, SUB_O)
            with act.Fori(1, 3) as t:
                tile_b(t, True, SUB_O)
            tile_b(3, False, next_subs("OA"))
            out_b(3)

            act.preload_act_table(ACT.Sqrt)

            def square_x(name, c, s, gain=None):
                act.wait_ge(ss_step, n_sq[0] + c + 1)
                act.wait_ge(acc_free, 2 + T0[name] + c + 1)
                if gain:
                    act.activation(f_hi[:, c, :], x[:, c, :], ACT.Identity, scale=pcol(gain, c)).then_inc(h_hi_ready, 1)
                act.activation(tmp[s][:, 0:S], x[:, c, :], ACT.Square).then_inc(sq_ready, 1)

            def body(i, n):
                for s in range(2):
                    next_hi(U0["OB"] // 2 + i, s, n if s else subs_of["OB"])
                    if not isinstance(i, int) or i + s:
                        square_x("OB", 2 * i + s - 1, 1 - s, "norm_mlp_2")
            run_pairs(act, "OB", 8, body, peel=True)
            square_x("OB", NC_D - 1, 1, "norm_mlp_2")
            n_sq[0] += NC_D

            n_v = 0
            for hx in range(2):
                name = f"FU{hx}"

                def silu(i):
                    act.wait_ge(av_ready, n_v + i + 1)
                    act.activation(tmp[5][:, 0:S], tmp[4][:, 0:S], ACT.Silu).then_inc(silu_ready, 1)

                def hidden_hi(i):
                    act.wait_ge(uv_ready, n_v + i + 1)
                    act.activation(u_hi[:, i, :], tmp[2][:, 0:S], ACT.Copy).then_inc(u_hi_ready, 1)

                def body(i, n):
                    first = isinstance(i, int) and i == 0
                    next_hi(U0[name] // 2 + i, 0, SUB)
                    if first and hx == 0:
                        deviation()
                        act.preload_act_table(ACT.Silu)
                    if not first:
                        silu(i - 1)
                    next_hi(U0[name] // 2 + i, 1, n)
                    if not first:
                        hidden_hi(i - 1)
                run_pairs(act, name, FF2_H, body, peel=True)
                silu(FF2_H - 1)
                hidden_hi(FF2_H - 1)
                n_v += FF2_H
                if hx == 0:
                    def body(i, n):
                        for s in range(2):
                            pair = U0["FD0"] // 2 + 2 * i + s
                            next_hi(pair, 0, DN2_SUB)
                            next_hi(pair, 1, n if s else DN2_SUB)
                    run_pairs(act, "FD0", 8, body)
                else:
                    act.preload_act_table(ACT.Sqrt)

                    def body(i, n):
                        for s in range(2):
                            pair = U0["FD1"] // 2 + 2 * i + s
                            next_hi(pair, 0, DN2_SUB)
                            next_hi(pair, 1, n if s else DN2_SUB)
                            square_x("FD1", 2 * i + s, s)
                    run_pairs(act, "FD1", 8, body)
                    n_sq[0] += NC_D
            deviation()

        @block.vector
        def _(dve):
            link = Link(dve, dve_link)
            tt, ts, stt = dve.tensor_tensor, dve.tensor_scalar, dve.scalar_tensor_tensor

            dve.memset(ones[:], 1.0)
            dve.memset(eps[:], EPS)
            dve.memset(table[32:33, :], NEG)
            for credit, n in [(lo_ready, 4), (xr_ready, 2), (lru_pre, 2), (rope_done, 2), (yr_ready, 2), (s1_read, 2),
                              (o1_free, 1), (s2_read, 2), (o2_free, 1), (u_ready, 2), (h_ready, 4)]:
                dve.sem_inc(credit, n)
            link(dve.memset(tmp[0][:, 0:3], 0.0))
            dve.sem_inc(setup_done, 1)
            dve.wait_ge(small_landed, 48)

            lm = pcol("lru_lambda", 0, NC_D)
            link(ts(lam[:, 0, :], lm, -1.0, None, ALU.mult))
            tt(lam[:, 1, :], lam[:, 0, :], lm, ALU.min).then_inc(lam_exp_in, 1)

            TWO_PI = 2 * np.pi
            c1 = 6.28125
            c2 = float(np.float32(np.round((TWO_PI - c1) * 2 ** 21) / 2 ** 21))
            c3 = float(np.float32(TWO_PI - c1 - c2))
            magic = 1.5 * 2 ** 23
            edge = 3.1415925
            link(dve.tensor_copy(pos[:], pos_i[:]))
            link(ts(ang[:, 0, :], pos[:], const[:, C_FREQ:C_FREQ + 1], None, ALU.mult))
            for dst, turn in ((2, 0.0), (3, 0.25)):
                link(ts(ang[:, 1, :], ang[:, 0, :], 1 / TWO_PI, turn, ALU.mult, ALU.add))
                link(ts(ang[:, 1, :], ang[:, 1, :], magic, None, ALU.add))
                link(ts(ang[:, 1, :], ang[:, 1, :], magic, None, ALU.subtract))
                link(stt(ang[:, dst, :], ang[:, 1, :], -c1, ang[:, 0, :], ALU.mult, ALU.add))
                link(stt(ang[:, dst, :], ang[:, 1, :], -c2, ang[:, dst, :], ALU.mult, ALU.add))
                link(stt(ang[:, dst, :], ang[:, 1, :], -c3, ang[:, dst, :], ALU.mult, ALU.add))
                if turn:
                    link(ts(ang[:, dst, :], ang[:, dst, :], np.pi / 2, None, ALU.add))
                ins = ts(ang[:, dst, :], ang[:, dst, :], edge, -edge, ALU.min, ALU.max)
                if not turn:
                    link(ins)
            ins.then_inc(ang_ready, 1)
            link(ts(is_reset[:], pos[:], 0.0, None, ALU.is_equal))


            dve.wait_ge(lam_exp, 1)
            link(ts(lam[:, 3, :], lam[:, 2, :], 2.0, None, ALU.add))
            link(dve.reciprocal(lam[:, 3, :], lam[:, 3, :]))
            link(tt(lam[:, 4, :], lam[:, 2, :], lam[:, 3, :], ALU.mult))
            link(tt(lam[:, 5, :], lam[:, 4, :], lam[:, 4, :], ALU.mult))
            link(ts(lam[:, 6, :], lam[:, 5, :], 1.0 / 17, None, ALU.mult))
            for k in range(7, 0, -1):
                link(stt(lam[:, 6, :], lam[:, 6, :], 1.0 / (2 * k + 1), lam[:, 5, :], ALU.add, ALU.mult))
            link(stt(lam[:, 6, :], lam[:, 6, :], 1.0, lam[:, 4, :], ALU.add, ALU.mult))
            link(ts(lam[:, 7, :], lam[:, 0, :], 0.0, 0.5, ALU.max, ALU.mult))
            link(tt(lam[:, 6, :], lam[:, 6, :], lam[:, 7, :], ALU.add))
            ts(sp8[:, 0, :], lam[:, 6, :], 16.0, None, ALU.mult)
            ts(sp8[:, 1, :], lam[:, 6, :], -16.0, None, ALU.mult).then_inc(sp_ready, 1)
            link.flush()

            def half_lo(pair, s, hf, subs):
                n0, n1 = split_sizes(subs)
                n, off = (n0, 0) if hf == 0 else (n1, n0)
                slot = 2 * s + hf
                dve.wait_ge(hi_ready, 4 * pair + 2 * s + hf + 1)
                tt(w_lo[:, slot, 0:n * P], w_raw[:, s, off * P:(off + n) * P],
                   w_hi[:, slot, 0:n * P].bitcast(F32), ALU.subtract).then_inc(lo_ready, 1)

            def next_lo(pair, s, subs, hf=None):
                at = (pair, 1) if s == 0 else (pair + 1, 0)
                for k in (0, 1) if hf is None else (hf,):
                    if subs:
                        half_lo(*at, k, subs)

            n_norm, n_h, n_b = [0], [0], [0]
            rstd = tmp[3][:, 0:S]

            def inverse_deviation(out=rstd):
                n_norm[0] += 1
                dve.wait_ge(std_ready, n_norm[0])
                link(dve.reciprocal(out, tmp[2][:, 0:S]))
                link.flush()

            def normalise(gain):
                inverse_deviation()

                bufs = [tmp[k][:, 0:S] for k in (4, 5, 0, 1)]

                def scaled(c, s):
                    dve.wait_ge(h_ready, n_h[0] + c + 1)
                    stt(bufs[s], x[:, c, :], pcol(gain, c), rstd, ALU.mult, ALU.mult).then_inc(hv_ready, 1)

                def lo(c, s):
                    dve.wait_ge(h_hi_ready, n_h[0] + c + 1)
                    tt(h_lo[:, c, :], bufs[s], h_hi[:, c, :].bitcast(F32), ALU.subtract).then_inc(h_ready, 1)

                scaled(0, 0)
                scaled(1, 1)
                with dve.Fori(0, NC_D // 4 - 1) as i:
                    for s in range(4):
                        scaled(4 * i + s + 2, (s + 2) % 4)
                        lo(4 * i + s, s)
                for c in range(NC_D - 4, NC_D):
                    if c + 2 < NC_D:
                        scaled(c + 2, (c + 2) % 4)
                    lo(c, c % 4)
                n_h[0] += NC_D
                dve.wait_ge(h_ready, 4 + n_h[0])

            def gain_lo(c, lo, hi, gain):
                dve.wait_ge(h_hi_ready, n_h[0] + c + 1)
                stt(lo[:, c, :], x[:, c, :], pcol(gain, c), hi[:, c, :].bitcast(F32), ALU.mult, ALU.subtract)\
                    .then_inc(h_ready, 1)

            def add_branch(gain, next_gain=None):
                inverse_deviation()

                def scaled(c):
                    stt(qy[:, c, :], qy[:, c, :], pcol(gain, c), rstd, ALU.mult, ALU.mult).then_inc(branch_scaled, 1)

                def add(c):
                    dve.wait_ge(branch_scaled, n_b[0] + c + 1)
                    tt(x[:, c, :], x[:, c, :], qy[:, c, :], ALU.add).then_inc(x_new, 1)

                scaled(0)
                scaled(1)
                add(0)
                with dve.Fori(0, NC_D // 2 - 1) as i:
                    for s in range(2):
                        scaled(2 * i + s + 2)
                        add(2 * i + s + 1)
                        if next_gain:
                            gain_lo(2 * i + s, h_lo, h_hi, next_gain)
                add(NC_D - 1)
                if next_gain:
                    gain_lo(NC_D - 2, h_lo, h_hi, next_gain)
                    gain_lo(NC_D - 1, h_lo, h_hi, next_gain)
                    n_h[0] += NC_D
                n_b[0] += NC_D

            half_lo(0, 0, 0, SUB)
            half_lo(0, 0, 1, SUB)
            normalise("norm_mix_pre")

            link(dve.memset(tmp[0][:, 0:3], 0.0))
            link(dve.memset(tmp[1][:, 0:3], 0.0))
            link.flush()

            def conv_lo(c):
                dve.wait_ge(xr_hi, c + 1)
                tt(d_lo[:, c, :], xr[:, c, :], d_hi[:, c, :].bitcast(F32), ALU.subtract).then_inc(xr_lo, 1)

            def body(i, n):
                for s in range(2):
                    c = 2 * i + s
                    next_lo(U0["X"] // 2 + i, s, n)
                    if not isinstance(i, int) or i + s:
                        conv_lo(c - 1)
                    dve.wait_ge(acc_free, 2 + T0["X"] + c + 1)
                    pad, t2 = tmp[s], tmp[2 + s][:, 0:S]
                    w = [pcol("conv_w", 4 * c + k) for k in range(3)]
                    link(stt(t2, pad[:, 2:2 + S], w[2], t2, ALU.mult, ALU.add))
                    link(stt(t2, pad[:, 1:1 + S], w[1], t2, ALU.mult, ALU.add))
                    stt(xr[:, c, :], pad[:, 0:S], w[0], t2, ALU.mult, ALU.add).then_inc(xr_ready, 1)
            run_pairs(dve, "X", 8, body, peel=True, link=link, per=4)
            conv_lo(NC_D - 1)

            with dve.Fori(0, 2) as bh:
                for mat in range(2):
                    next_lo(U0["RG"] // 2 + bh, mat, SUB)

            def decay(c, s):
                a, r, th = a_lru[:, c, :], gates[:, c, :], tmp[4 + s][:, 0:S]
                dve.wait_ge(lru_act, c + 1)
                link(stt(a, is_reset[:], 1.0, a, ALU.subtract, ALU.mult, reverse0=True))
                link(tt(th, th, is_reset[:], ALU.max))
                link(tt(r, a, a, ALU.mult))
                stt(r, r, 1.0, th, ALU.add, ALU.mult).then_inc(lru_pre, 1)

            def rope(c, s, out):
                dve.wait_ge(rope_done, 2 + c)
                link(tt(tmp[2][:, 0:S], tmp[s][:, 0:S], cos[:], ALU.mult))
                dve.wait_ge(rot_ready, c + 1)
                link(tt(tmp[3][:, 0:S], PS[:, 6 + s, 0:S], sin[:], ALU.mult))
                tt(out, tmp[2][:, 0:S], tmp[3][:, 0:S], ALU.add).then_inc(rope_done, 1)

            dve.wait_ge(rope_tab, 1)

            def body(i):
                for s in range(2):
                    c = 2 * i + s
                    next_lo(U0["Q"] // 2 + i, s, SUB)
                    decay(c, s)
                    if not (isinstance(i, int) and s == 0):
                        dve.wait_ge(acc_free, 2 + T0["Q"] + c)
                        rope(c - 1, 1 - s, qy[:, c - 1, :])

            link.begin(0, 5 + 3 + 2)
            body(0)
            link.k = 0
            link.flush()
            link.base += 8
            with dve.Fori(1, 8) as i:
                link.begin(i - 1, 10)
                body(i)
            link.end(7)
            next_lo(U0["Q"] // 2 + 8, 0, SUB)
            dve.wait_ge(acc_free, 2 + T0["Q"] + 16)
            rope(15, 1, qy[:, 15, :])
            next_lo(U0["Q"] // 2 + 8, 1, SUB)
            for t in range(2):
                dve.wait_ge(acc_free, 2 + T0["Q"] + 17 + t)
                rope(16 + t, t, kt[:, t, :])
            link.flush()

            def body(i, n):
                for s in range(2):
                    c = 2 * i + s
                    next_lo(U0["Y"] // 2 + i, s, n)
                    t2, y = tmp[2 + s][:, 0:S], tmp[4 + s][:, 0:S]
                    dve.wait_ge(lru_in, c + 1)
                    link(dve.tensor_tensor_scan(t2, a_lru[:, c, :], gates[:, NC_D + c, :], 0.0, ALU.mult, ALU.add))
                    dve.wait_ge(acc_free, 2 + T0["Y"] + c + 1)
                    tt(y, t2, tmp[s][:, 0:S], ALU.mult).then_inc(yr_ready, 1)
                    dve.wait_ge(y_hi, c + 1)
                    tt(d_lo[:, c, :], y, d_hi[:, c, :].bitcast(F32), ALU.subtract).then_inc(y_lo, 1)
            run_pairs(dve, "Y", 8, body, link=link, per=2)

            for s in range(2):
                next_lo(U0["V"] // 2, s, SUB)

            dve.wait_ge(mask1_landed, 16)

            def soft1(hd, e):
                mx, ng = (small[:, 10 * e + 2 * j:10 * e + 2 * j + 2] for j in range(2))
                dve.wait_ge(s1_ready, hd + 1)
                dve.wait_ge(t1_ready, hd + 1)
                stt(sb1[:, e, :], PS[:, 2 + e, 0:SC], QS, mask1[:], ALU.mult, ALU.add).then_inc(s1_read, 1)
                dve.wait_ge(s1_read, 2 + hd + 1)
                dve.tensor_reduce(mx[:, 0:1], sb1[:, e, 0:P], AX.X, ALU.max)
                link(dve.tensor_reduce(mx[:, 1:2], sb1[:, e, P:SC], AX.X, ALU.max))
                ts(ng, mx, sinks[:, bass.ds(hd, 1)], -1.0, ALU.max, ALU.mult).then_inc(ng1_ready, 1)

            def norm1(hd, e):
                den, es, rd = (small[:, 10 * e + 2 * j:10 * e + 2 * j + 2] for j in range(2, 5))
                dve.wait_ge(e1_ready, hd + 1)
                link(tt(den, den, es, ALU.add))
                link(dve.reciprocal(rd, den))
                ts(sb1[:, e, 0:P], sb1[:, e, 0:P], rd[:, 0:1], None, ALU.mult)
                ts(sb1[:, e, P:SC], sb1[:, e, P:SC], rd[:, 1:2], None, ALU.mult).then_inc(p1_ready, 1)

            def out1(tile):
                dve.wait_ge(o1_ready, 2 + 2 * tile + 2)
                dve.tensor_copy(qy[:, tile, :], PS[:, 6, 0:S]).then_inc(o1_free, 1)

            for gp in range(2):
                def body(i):
                    first = isinstance(i, int)
                    for e in range(2):
                        hd = 16 * gp + 2 * i + e
                        pair = U0["G"] // 2 + 8 * gp + i
                        next_lo(pair, e, SUB, 0)
                        if e == 1 and not first:
                            out1(8 * gp + i - 1)
                        soft1(hd, e)
                        next_lo(pair, e, SUB, 1)
                        norm1(hd, e)
                link.begin(0, 6)
                body(0)
                with dve.Fori(1, 8) as i:
                    link.begin(i, 6)
                    body(i)
                link.end(8)
                out1(8 * gp + 7)

            def body(i, n):
                for s in range(2):
                    c = 2 * i + s
                    next_lo(U0["MR"] // 2 + i, s, n)
                    dve.wait_ge(ya_hi, c + 1)
                    tt(h_lo[:, c, :], qy[:, c, :], h_hi[:, c, :].bitcast(F32), ALU.subtract).then_inc(ya_lo, 1)
                    dve.wait_ge(sg_ready, c + 1)
                    dve.wait_ge(half_done, units_done(U0["MR"] + c))
                    tt(gates[:, c, :], PS[:, s, 0:S], tmp[s][:, 0:S], ALU.mult).then_inc(acc_free, 1)
            run_pairs(dve, "MR", 8, body)

            def body(i, n):
                for s in range(2):
                    c = 2 * i + s
                    next_lo(U0["MA"] // 2 + i, s, n)
                    dve.wait_ge(sg_ready, NC_D + c + 1)
                    dve.wait_ge(half_done, units_done(U0["MA"] + c))
                    tt(tmp[2][:, 0:S], PS[:, s, 0:S], tmp[s][:, 0:S], ALU.mult).then_inc(acc_free, 1)
                    dve.wait_ge(acc_free, 2 + T0["MA"] + c + 1)
                    tt(tmp[4 + s][:, 0:S], tmp[2][:, 0:S], gates[:, c, :], ALU.add).then_inc(mix_ready, 1)
                    dve.wait_ge(mix_hi, c + 1)
                    tt(d_lo[:, c, :], tmp[4 + s][:, 0:S], d_hi[:, c, :].bitcast(F32), ALU.subtract).then_inc(mix_lo, 1)
            run_pairs(dve, "MA", 8, body)

            def body(i, n):
                for s in range(2):
                    next_lo(U0["O"] // 2 + i, s, n)
            run_pairs(dve, "O", 8, body)
            add_branch("norm_mix_post", "norm_mlp_pre")

            n_u = 0
            for hx in range(2):
                def body(i, n):
                    for s in range(2):
                        c, name = 2 * i + s, f"UP{hx}"
                        next_lo(U0[name] // 2 + i, s, n)
                        if hx == 0 and s == 0 and isinstance(i, int) and i == 0:
                            inverse_deviation()
                        dve.wait_ge(half_done, units_done(U0[name] + c))
                        stt(tmp[s][:, 0:S], PS[:, s, 0:S], 0.0, rstd, ALU.max, ALU.mult).then_inc(acc_free, 1)
                        dve.wait_ge(acc_free, 2 + T0[name] + c + 1)
                        tt(tmp[4 + s][:, 0:S], tmp[s][:, 0:S], tmp[s][:, 0:S], ALU.mult).then_inc(relu_ready, 1)
                        dve.wait_ge(u_hi_ready, n_u + c + 1)
                        tt(u_lo[:, c, :], tmp[4 + s][:, 0:S], u_hi[:, c, :].bitcast(F32), ALU.subtract)\
                            .then_inc(u_ready, 1)
                run_pairs(dve, f"UP{hx}", FF1_H // 2, body, peel=hx == 0)
                n_u += FF1_H

                def body(i, n):
                    for s in range(2):
                        c, name = 2 * i + s, f"DN{hx}"
                        pair = U0[name] // 2 + 2 * i + s
                        next_lo(pair, 0, n)
                        next_lo(pair, 1, n)
                        dve.wait_ge(half_done, units_done(2 * pair + 1))
                        if hx:
                            tt(qy[:, c, :], PS[:, s, 0:S], qy[:, c, :], ALU.add).then_inc(acc_free, 1)
                        else:
                            dve.tensor_copy(qy[:, c, :], PS[:, s, 0:S]).then_inc(acc_free, 1)
                run_pairs(dve, f"DN{hx}", 8, body)
            add_branch("norm_mlp_post")
            normalise("norm_attn_2")

            def splits(name):
                def body(i, n):
                    for s in range(2):
                        next_lo(U0[name] // 2 + i, s, n if s else subs_of[name])
                run_pairs(dve, name, pairs_of[name], body)

            splits("C2")
            splits("VC")
            dve.wait_ge(gate2_ready, 1)
            dve.wait_ge(hid_ready, 1)

            bias_buf = [bias_a, bias_b]

            def small2(e, j, n):
                return small[:, 32 * e + j:32 * e + j + n]

            def biased(bank, e, slot, bias):
                return stt(sb2[:, e, slot, :], PS[:, bank, 0:SC], QS, bias, ALU.mult, ALU.add)

            def maxima(e, cols, j, axis):
                for blk in range(2):
                    ins = dve.tensor_reduce(small2(e, 2 * j + blk, 1), cols(slice(0, P) if blk == 0 else slice(P, SC)),
                                            axis, ALU.max)
                return ins

            def times(e, cols, j):
                for blk in range(2):
                    src = cols(slice(0, P) if blk == 0 else slice(P, SC))
                    ins = ts(src, src, small2(e, 18 + 2 * j + blk, 1), None, ALU.mult)
                return ins

            def out_lo(lo, hi, bank, col):
                return tt(lo, PS[:, bank, col:col + S], hi.bitcast(F32), ALU.subtract)

            def soft(job0, t, e, landed, read, top):
                job = job0 + 2 * t + e
                dve.wait_ge(bias_landed[e], landed)
                dve.wait_ge(s2_ready, 2 + job + 1)
                read(e).then_inc(s2_read, 1)
                dve.wait_ge(s2_read, 2 + job + 1)
                n, ins = top(e)
                link(ins)
                ts(small2(e, 6, n), small2(e, 0, n), -1.0, None, ALU.mult).then_inc(ng2_ready, 1)

            def normal_step(job0, t, e, normal):
                dve.wait_ge(e2_ready, job0 + 2 * t + e + 1)
                normal(t, e).then_inc(p2_ready, 1)

            def read_c(e):
                for br in range(2):
                    biased(2 + br, e, br, bias_buf[e][:, 0, :])
                return stt(sbc[:, e], PS[:, 2, SC:SC + 2 * N_CMP].rearrange("p (q n) -> p q n", q=2), QS, cmask[:, 0],
                           ALU.mult, ALU.add)

            def top_c(e):
                for br in range(2):
                    maxima(e, lambda c: sb2[:, e, br, c], br, AX.X)
                return 6, dve.tensor_reduce(small2(e, 4, 2), sbc[:, e], AX.X, ALU.max)

            def normal_c(t, e):
                link(tt(sbc[:, e], sbc[:, e], cmask[:, 1], ALU.mult))
                link(dve.tensor_reduce(small2(e, 16, 2), sbc[:, e], AX.X, ALU.add))
                link(ts(small2(e, 16, 2), small2(e, 16, 2), 1e-30, None, ALU.max))
                link(dve.reciprocal(small2(e, 18, 6), small2(e, 12, 6)))
                for br, col in ((0, 1), (1, 2), (2, 0)):
                    coef = small2(e, 18 + 2 * br, 2)
                    ins = tt(coef, coef, gate2[:, :, bass.ds(3 * (2 * t + e) + col, 1)].rearrange("p a b -> p (a b)"), ALU.mult)
                link(ins)
                for br in range(2):
                    times(e, lambda c: sb2[:, e, br, c], br)
                for qt in range(2):
                    ins = ts(sbc[:, e, qt, :], sbc[:, e, qt, :], small2(e, 22 + qt, 1), None, ALU.mult)
                return ins

            def soft_c(t, e):
                soft(JOB_C, t, e, 32 * (t + 1), read_c, top_c)

            def out_c(t):
                dve.wait_ge(o2_hi, t + 1)
                out_lo(oc_lo[:, t, :], oc_hi[:, t, :], 7, 0).then_inc(o2_free, 1)

            def tile_c(t, more):
                for e in range(2):
                    normal_step(JOB_C, t, e, normal_c)
                    next_lo(U0["A2"] // 2 + t, e, SUB)
                    if e == 0 and not isinstance(t, int) or e == 0 and t:
                        out_c(t - 1)
                    if more:
                        soft_c(t + 1, e)

            with dve.Fori(0, 3) as i:
                for s in range(2):
                    next_lo(U0["B2"] // 2 + i, s, SUB)
            for e in range(2):
                next_lo(U0["B2"] // 2 + 3, e, SUB)
                soft_c(0, e)
            link.flush()
            tile_c(0, True)
            link.flush()
            with dve.Fori(1, 2 * KV_C - 1) as t:
                link.begin(t - 1, 2 + 2 * 5)
                tile_c(t, True)
            link.end(2 * KV_C - 2)
            tile_c(2 * KV_C - 1, False)
            out_c(2 * KV_C - 1)
            link.flush()
            def read_a(e):
                for g in range(3):
                    ins = biased(2 + g, e, g, bias_buf[e][:, g, :])
                return ins

            def normal_a(t, e):
                link(dve.reciprocal(small2(e, 18, 2), small2(e, 12, 2)))
                return times(e, lambda c: sb2[:, e, :, c], 0)

            def soft_a(t, e):
                soft(JOB_A, t, e, 192 + 96 * (t + 1), read_a, lambda e: (2, maxima(e, lambda c: sb2[:, e, :, c], 0, AX.XY)))

            def normal_b(t, e):
                link(dve.reciprocal(small2(e, 18, 2), small2(e, 12, 2)))
                return times(e, lambda c: sb2[:, e, 0, c], 0)

            def soft_b(t, e):
                soft(JOB_B, t, e, 384 + 32 * (t + 1), lambda e: biased(2, e, 0, bias_buf[e][:, 0, :]),
                     lambda e: (2, maxima(e, lambda c: sb2[:, e, 0, c], 0, AX.X)))

            with dve.Fori(0, 3) as i:
                for s in range(2):
                    next_lo(U0["VAB"] // 2 + i, s, SUB)
            for e in range(2):
                soft_a(0, e)
                next_lo(U0["VAB"] // 2 + 3 + e, 0, SUB)
                next_lo(U0["VAB"] // 2 + 3 + e, 1, SUB_O if e else SUB)

            def join(name, c, bank):
                dve.wait_ge(half_done, units_done(U0[name] + c))
                tt(x[:, c, :], PS[:, bank, 0:S], x[:, c, :], ALU.add).then_inc(acc_free, 1)

            for k in range(4):
                t, e, pair = k // 2, k % 2, U0["OC"] // 2 + 2 * k
                normal_step(JOB_A, t, e, normal_a)
                for f in range(4):
                    next_lo(pair + f // 2, f % 2, SUB_O)
                    join("OC", 4 * k + f, 0)
                    if f == 1:
                        dve.wait_ge(t2_ready, JOB_A + k + 1)
                        (soft_b if t else soft_a)(0 if t else 1, e)
                if e == 1:
                    dve.wait_ge(o2_hi, 6 + 3 * (t + 1))
                    for g in range(3):
                        ins = out_lo(h_lo[:, 2 * g + t, :], h_hi[:, 2 * g + t, :], 7 if g < 2 else 1, (g % 2) * S)
                    ins.then_inc(o2_free, 1)
            link.flush()

            def out_b(t):
                dve.wait_ge(o2_hi, 12 + t + 1)
                out_lo(h_lo[:, 6 + t, :], h_hi[:, 6 + t, :], 7, 0).then_inc(o2_free, 1)

            def tile_b(t, more, n):
                for e in range(2):
                    pair = U0["OA"] // 2 + 2 * t + e
                    normal_step(JOB_B, t, e, normal_b)
                    next_lo(pair, 0, SUB_O)
                    join("OA", 4 * t + 2 * e, 0)
                    if e == 0 and not isinstance(t, int) or e == 0 and t:
                        out_b(t - 1)
                    if more:
                        soft_b(t + 1, e)
                    next_lo(pair, 1, n if e else SUB_O)
                    join("OA", 4 * t + 2 * e + 1, 1)

            tile_b(0, True, SUB_O)
            link.flush()
            with dve.Fori(1, 3) as t:
                link.begin(t - 1, 4)
                tile_b(t, True, SUB_O)
            link.end(2)
            tile_b(3, False, next_subs("OA"))
            out_b(3)
            link.flush()

            def join_x(name, units, gain=None):
                def body(i, n):
                    for s in range(2):
                        c = 2 * i + s
                        first = isinstance(i, int) and i + s == 0
                        if units == 1:
                            unit = U0[name] + 2 * i + s
                            next_lo(U0[name] // 2 + i, s, n if s else subs_of[name])
                        else:
                            pair = U0[name] // 2 + 2 * i + s
                            unit = 2 * pair + 1
                            next_lo(pair, 0, subs_of[name])
                            next_lo(pair, 1, n if s else subs_of[name])
                        if gain and not first:
                            gain_lo(c - 1, f_lo, f_hi, gain)
                        dve.wait_ge(half_done, units_done(unit))
                        tt(x[:, c, :], PS[:, s, 0:S], x[:, c, :], ALU.add).then_inc(acc_free, 1)
                run_pairs(dve, name, 8, body, peel=gain is not None)
                if gain:
                    gain_lo(NC_D - 1, f_lo, f_hi, gain)
                    n_h[0] += NC_D

            join_x("OB", 1, "norm_mlp_2")

            n_v = 0
            for hx in range(2):
                name = f"FU{hx}"

                def gated(i):
                    dve.wait_ge(silu_ready, n_v + i + 1)
                    tt(tmp[2][:, 0:S], tmp[5][:, 0:S], tmp[3][:, 0:S], ALU.mult).then_inc(uv_ready, 1)

                def hidden_lo(i):
                    dve.wait_ge(u_hi_ready, 2 * FF1_H + n_v + i + 1)
                    tt(u_lo[:, i, :], tmp[2][:, 0:S], u_hi[:, i, :].bitcast(F32), ALU.subtract).then_inc(u_ready, 1)

                def conv(i, s):
                    c = 44 * s + FF2_H * hx + i
                    v = tmp[3 + s][:, 0:S]
                    dve.wait_ge(half_done, units_done(U0[name] + 2 * i + s))
                    tt(tmp[s][:, 2:2 + S], PS[:, s, 0:S], rstd2[:], ALU.mult).then_inc(acc_free, 1)
                    dve.wait_ge(acc_free, 2 + T0[name] + 2 * i + s + 1)
                    link(ts(v, tmp[s][:, 2:2 + S], pcol("conv_w_2", 3 * c), pcol("conv_b_2", c), ALU.mult, ALU.add))
                    link(stt(v, tmp[s][:, 1:1 + S], pcol("conv_w_2", 3 * c + 1), v, ALU.mult, ALU.add))
                    return stt(v, tmp[s][:, 0:S], pcol("conv_w_2", 3 * c + 2), v, ALU.mult, ALU.add)

                def body(i, n):
                    first = isinstance(i, int) and i == 0
                    next_lo(U0[name] // 2 + i, 0, SUB)
                    if first and hx == 0:
                        inverse_deviation(rstd2[:])
                        link(dve.memset(tmp[0][:, 0:2], 0.0))
                        link(dve.memset(tmp[1][:, 0:2], 0.0))
                        link.flush()
                        link.begin(0, 4)
                    if not first:
                        gated(i - 1)
                        dve.wait_ge(uv_ready, n_v + i)
                    conv(i, 0)
                    next_lo(U0[name] // 2 + i, 1, n)
                    if not first:
                        hidden_lo(i - 1)
                    conv(i, 1).then_inc(av_ready, 1)
                run_pairs(dve, name, FF2_H, body, peel=True, link=link, per=4)
                gated(FF2_H - 1)
                hidden_lo(FF2_H - 1)
                n_v += FF2_H
                join_x(f"FD{hx}", 2)

            inverse_deviation()
            with dve.Fori(0, NC_D // 2) as i:
                for s in range(2):
                    c = 2 * i + s
                    stt(qy[:, c, :], x[:, c, :], pcol("norm_final_2", c), rstd, ALU.mult, ALU.mult).then_inc(x_new, 1)


def shape_constants():
    const = np.zeros((P, N_CONST), np.float32)
    const[:, C_ID:C_ID + P] = np.eye(P)
    for m in range(P):
        first = m % HD < HD // 2
        const[m + 32 if first else m - 32, C_ROT + m] = -1.0 if first else 1.0
    const[:, C_FREQ] = np.float32(10000.0) ** (-(2 * (np.arange(P) % (HD // 2))).astype(np.float32) / np.float32(HD))
    p, k = np.arange(P)[:, None], np.arange(S)[None, :]
    dist = np.concatenate([(p - k)[:, :P], p + P - k], 1)
    mask1 = np.where((dist >= 0) & (dist < 128), 0.0, NEG).astype(np.float32)
    ok = np.stack([16 * np.arange(N_CMP)[None, :] + CMP_LEN - 1 <= p + P * q for q in range(2)], 1)
    cmask = np.stack([np.where(ok, 0.0, NEG), ok], 1).astype(np.float32)
    dist = S - 1 - np.arange(512)
    n = np.maximum(dist, 1)
    large = 16 + (np.log(n / 16) / np.log(2048 / 16) * 16).astype(np.int64)
    bucket = np.where(dist < 16, np.maximum(dist, 0), np.minimum(large, 31))
    onehot = np.zeros((33, 4, 512), np.float32)
    for var, valid in enumerate([(dist >= 0) & (dist <= 128), (dist >= 0) & (dist % 4 == 0),
                                 (dist >= 0) & (dist % 16 == 0), dist >= 0]):
        onehot[bucket[valid], var, np.arange(512)[valid]] = 1.0
        onehot[32, var, ~valid] = 1.0
    return {"const": const, "mask1": mask1, "cmask": cmask, "onehot": onehot}


def kernel(**inputs):
    import concourse.bacc as bacc
    from concourse.bass_utils import run_bass_kernel_spmd

    a = {k: np.asarray(v) for k, v in inputs.items()}

    def units(w, subs=SUB):
        k, n = w.shape
        t = w.reshape(k // P, P, n // P, P).transpose(2, 0, 1, 3)
        t = t.reshape(n // P, k // P // subs, subs, P, P).transpose(0, 1, 3, 2, 4)
        return np.ascontiguousarray(t).reshape(-1, P, subs * P)

    def units_v(w):
        t = w.reshape(2, HALF, P, -1, S).transpose(3, 0, 2, 1, 4)
        return np.ascontiguousarray(t).reshape(-1, P, HALF * S)

    def feature(v):
        v = v.reshape(-1, v.shape[-1] // P, P)
        return np.ascontiguousarray(v.transpose(2, 1, 0)).reshape(P, -1)

    arrays = shape_constants()
    arrays["xt"] = np.ascontiguousarray(a["x"][0].T.reshape(NC_D, P, S).transpose(1, 0, 2))
    arrays["pos"] = a["positions"][0]

    order = np.array([[8 * (2 * gp + e) + j for e in range(2)] for gp in range(2) for j in range(8)]).reshape(-1)
    q_cols = (order[:, None] * HD + np.arange(HD)[None, :]).reshape(-1)
    arrays["sinks"] = a["attn_sinks"][0][order]
    w = a["w_in"][0]
    o = np.cumsum([0, 2048, 2048, 2048, 256, 256, 2048, 2048])
    arrays["w_X"] = units(w[:, o[0]:o[1]])
    arrays["w_Q"] = np.concatenate([units(w[:, o[2]:o[3]][:, q_cols]), units(w[:, o[3]:o[4]])])
    arrays["w_Y"] = units(w[:, o[1]:o[2]])
    arrays["w_V"] = units_v(w[:, o[4]:o[5]])
    arrays["w_G"] = units(w[:, o[5]:o[7]])
    rg = np.stack([a["w_rg_a"][0], a["w_rg_x"][0]])
    rg = rg.reshape(2, 2, 4, 2, P, 2, P).transpose(1, 0, 4, 2, 5, 3, 6)
    arrays["w_RG"] = np.ascontiguousarray(rg).reshape(4, P, SUB * P)
    arrays["w_MR"] = units(a["w_rnn_proj"][0])
    arrays["w_MA"] = units(a["w_attn_proj"][0][q_cols])
    arrays["w_O"] = units(a["w_out"][0])
    up, down = a["w_mlp_up"][0], a["w_mlp_down"][0]
    for hx in range(2):
        arrays[f"w_UP{hx}"] = units(up[:, hx * FF1 // 2:(hx + 1) * FF1 // 2])
        arrays[f"w_DN{hx}"] = units(down[hx * FF1 // 2:(hx + 1) * FF1 // 2])

    w = a["w_in_2"][0]
    b0, c0 = 2304, 3840
    kv0 = c0 + 768
    branch = lambda i, kv: w[:, kv0 + 192 * i + HD * kv:kv0 + 192 * i + HD * (kv + 1)]
    cols = [w[:, c0:kv0]]
    cols += [branch(i, kv) for kv in range(KV_C) for i in (0, 1)]
    cols += [branch(i, kv) for kv in range(KV_C) for i in (2, 4)]
    arrays["w_C2"] = units(np.concatenate(cols, 1))
    cols = [branch(i, kv) for i in (3, 5) for kv in range(KV_C)]
    cols += [w[:, kv0 + 1152:], np.zeros((D, P - 36), np.float32)]
    arrays["w_VC"] = units_v(np.concatenate(cols, 1))
    cols = [w[:, 768 * g + 256 * part:768 * g + 256 * (part + 1)] for g in range(3) for part in range(2)]
    arrays["w_A2"] = units(np.concatenate(cols, 1))
    arrays["w_B2"] = units(w[:, b0:b0 + 1024])
    cols = [w[:, 768 * g + 512:768 * g + 768] for g in range(3)] + [w[:, b0 + 1024:c0]]
    arrays["w_VAB"] = units_v(np.concatenate(cols, 1))
    w = a["w_out_2"][0]
    arrays["w_OC"] = units(w[20 * HD:], SUB_O)
    arrays["w_OA"] = units(w[:12 * HD], SUB_O)
    arrays["w_OB"] = units(w[12 * HD:20 * HD], 4)
    up, down = a["w_up_2"][0], a["w_down_2"][0]
    both = units(up).reshape(2, 2, FF2_H, P, SUB * P)
    for hx in range(2):
        arrays[f"w_FU{hx}"] = np.ascontiguousarray(both[:, hx].transpose(1, 0, 2, 3)).reshape(-1, P, SUB * P)
        arrays[f"w_FD{hx}"] = units(down[hx * FF2 // 2:(hx + 1) * FF2 // 2], DN2_SUB)
    arrays["cw1"] = np.ascontiguousarray(a["cmp_w1_2"][0].reshape(2, CMP_LEN, HD, P).transpose(0, 2, 1, 3)).reshape(P, CMP_LEN, P)
    arrays["cw2"] = np.ascontiguousarray(a["cmp_w2_2"][0].transpose(1, 0, 2))
    arrays["cpe"] = np.ascontiguousarray(a["cmp_pe_2"][0].transpose(0, 2, 1)).reshape(P, CMP_LEN)
    arrays["table"] = np.ascontiguousarray(a["rel_table_2"].T)
    named = {k: a[k] for k in ("norm_mix_pre", "conv_w", "conv_b", "b_rg_a", "b_rg_x", "lru_lambda", "norm_mix_post",
                               "norm_mlp_pre", "norm_mlp_post")}
    named |= {k: a[k] for k in ("norm_attn_2", "norm_mlp_2", "norm_final_2", "conv_w_2", "conv_b_2")}
    arrays["par"] = np.concatenate([feature(named[k]) for k in PARAM_COLS], 1)

    nc = bacc.Bacc("TRN2", target_bir_lowering=False, num_devices=1)
    dram = {k: nc.dram_tensor(f"in_{k}", v.shape, mybir.dt.from_np(v.dtype), kind="ExternalInput").ap()
            for k, v in arrays.items()}
    dram["out"] = nc.dram_tensor("out", (P, NC_D, S), F32, kind="ExternalOutput").ap()
    program(nc, dram)
    r = run_bass_kernel_spmd(nc, [{f"in_{k}": v for k, v in arrays.items()}], core_ids=[0])
    out = np.asarray(r.results[0]["out"])
    return np.ascontiguousarray(out.transpose(2, 1, 0).reshape(1, S, D))
```
